# Optimizing a Trainium2 kernel written in Bass

```python
import math
import jax
import jax.numpy as jnp
from jax import lax
import numpy as np
import jax, jax.numpy as jnp

D_MODEL = 1024
BATCH = 1
SEQ = 256
DEPTH = 2

N_EVEN = (DEPTH + 1) // 2
N_ODD = DEPTH // 2
HEAD_DIM = 64
CONV_W = 3
A_W = D_MODEL // 2
B_W = D_MODEL - A_W
POOL_WINDOWS = (2, 4, 8, 16)
N_POOL = len(POOL_WINDOWS)
POOL_G = B_W // N_POOL
EV_IN_W = 3 * A_W + B_W
MIX_W = A_W + B_W
H_FOX = D_MODEL // (2 * HEAD_DIM)
H_MOBA = D_MODEL // (2 * HEAD_DIM)
H_ATT = H_FOX + H_MOBA
ATT_W = H_ATT * HEAD_DIM
OD_IN_W = 3 * ATT_W + H_FOX
ATTN_SCALE = HEAD_DIM ** -0.5
FOX_Q_BLOCK = 128
MOBA_BLOCK = 256
MOBA_TOPK = 3
MOBA_Q_CHUNK = 32
T5_BUCKETS = 32
T5_MAX_DIST = 128
FORGET_BIAS_INIT = 2.0
D_FF = 2816
RMS_EPS = 1e-6


def rmsnorm(x, g):
    xf = x.astype(jnp.float32)
    y = xf * lax.rsqrt(jnp.mean(xf * xf, axis=-1, keepdims=True) + RMS_EPS)
    return (y * g.astype(jnp.float32)).astype(x.dtype)

def causal_dwconv(u, w):
    s = u.shape[1]
    up = jnp.pad(u, ((0, 0), (CONV_W - 1, 0), (0, 0)))
    return sum(w[i] * up[:, i:i + s] for i in range(CONV_W))

def multiscale_pool(u, pool_w, pool_scale):
    bsz, s, _ = u.shape
    cs = jnp.cumsum(jnp.pad(u.astype(jnp.float32), ((0, 0), (1, 0), (0, 0))), axis=1)
    pos = jnp.arange(s)
    groups = []
    for g, w in enumerate(POOL_WINDOWS):
        csg = cs[..., g * POOL_G:(g + 1) * POOL_G]
        hi = csg[:, 1:]
        lo = jnp.pad(csg[:, :s + 1 - w], ((0, 0), (w - 1, 0), (0, 0)))
        cnt = jnp.minimum(pos + 1, w).astype(jnp.float32)[None, :, None]
        groups.append((hi - lo) / cnt - u[..., g * POOL_G:(g + 1) * POOL_G].astype(jnp.float32))
    p = jnp.stack(groups, axis=2).astype(u.dtype)
    y = jnp.einsum('bsgc,gcd->bsgd', p, pool_w).reshape(bsz, s, B_W)
    return y * pool_scale

def even_mixer(h, w_in, conv_w, pool_w, pool_scale, w_out):
    z = h @ w_in
    gate_b = z[..., :A_W]
    gate_c = z[..., A_W:2 * A_W]
    val = z[..., 2 * A_W:3 * A_W]
    pool_in = z[..., 3 * A_W:]
    y_a = gate_b * causal_dwconv(gate_c * val, conv_w)
    y_b = multiscale_pool(pool_in, pool_w, pool_scale)
    return jnp.concatenate([y_a, y_b], axis=-1) @ w_out

def t5_bucket(dist):
    dist = jnp.maximum(dist, 0)
    exact = T5_BUCKETS // 2
    d_f = jnp.maximum(dist, 1).astype(jnp.float32)
    log_b = exact + (jnp.log(d_f / exact) / math.log(T5_MAX_DIST / exact)
                     * (T5_BUCKETS - exact)).astype(jnp.int32)
    log_b = jnp.minimum(log_b, T5_BUCKETS - 1)
    return jnp.where(dist < exact, dist, log_b)

def forgetting_attention(q, k, v, log_f):
    bsz, nh, s, dh = q.shape
    fcum = jnp.cumsum(log_f, axis=-1)
    nq = s // FOX_Q_BLOCK
    q_blocks = q.reshape(bsz, nh, nq, FOX_Q_BLOCK, dh).transpose(2, 0, 1, 3, 4)
    f_blocks = fcum.reshape(bsz, nh, nq, FOX_Q_BLOCK).transpose(2, 0, 1, 3)
    kpos = jnp.arange(s)

    def one_block(args):
        i, q_i, f_i = args
        qpos = i * FOX_Q_BLOCK + jnp.arange(FOX_Q_BLOCK)
        logits = jnp.einsum('bhqd,bhkd->bhqk', q_i, k).astype(jnp.float32) * ATTN_SCALE
        logits = logits + f_i[..., :, None] - fcum[..., None, :]
        logits = jnp.where(kpos[None, :] <= qpos[:, None], logits, -jnp.inf)
        p = jax.nn.softmax(logits, axis=-1)
        return jnp.einsum('bhqk,bhkd->bhqd', p.astype(v.dtype), v)

    out = lax.map(one_block, (jnp.arange(nq), q_blocks, f_blocks))
    return out.transpose(1, 2, 0, 3, 4).reshape(bsz, nh, s, dh)

def moba_attention(q, k, v, rel_bias):
    bsz, nh, s, dh = q.shape
    n_blk = -(-s // MOBA_BLOCK)
    pad = n_blk * MOBA_BLOCK - s
    k_p = jnp.pad(k, ((0, 0), (0, 0), (0, pad), (0, 0)))
    v_p = jnp.pad(v, ((0, 0), (0, 0), (0, pad), (0, 0)))
    k_blk = k_p.reshape(bsz, nh, n_blk, MOBA_BLOCK, dh)
    v_blk = v_p.reshape(bsz, nh, n_blk, MOBA_BLOCK, dh)
    k_mean = jnp.mean(k_blk.astype(jnp.float32), axis=3)
    topk = min(MOBA_TOPK, n_blk)
    nq = s // MOBA_Q_CHUNK
    q_chunks = q.reshape(bsz, nh, nq, MOBA_Q_CHUNK, dh).transpose(2, 0, 1, 3, 4)
    blk_ids = jnp.arange(n_blk)
    kpos_in_blk = jnp.arange(MOBA_BLOCK)
    head_ids = jnp.arange(nh)[:, None, None, None]
    bias_t = rel_bias.T
    gather_blocks = jax.vmap(jax.vmap(lambda kb, ix: kb[ix]))

    def one_chunk(args):
        c, q_i = args
        start = c * MOBA_Q_CHUNK
        cur = start // MOBA_BLOCK
        qpos = start + jnp.arange(MOBA_Q_CHUNK)
        gate = jnp.einsum('bhqd,bhnd->bhqn', q_i.astype(jnp.float32), k_mean)
        gate = jnp.where(blk_ids < cur, gate, -jnp.inf)
        _, idx = lax.top_k(gate, topk)
        valid = idx < cur
        k_sel = gather_blocks(k_blk, idx)
        v_sel = gather_blocks(v_blk, idx)
        kpos_sel = idx[..., None] * MOBA_BLOCK + kpos_in_blk
        bias_sel = bias_t[head_ids, t5_bucket(qpos[:, None, None] - kpos_sel)]
        l_sel = jnp.einsum('bhqd,bhqtld->bhqtl', q_i, k_sel).astype(jnp.float32) * ATTN_SCALE
        l_sel = jnp.where(valid[..., None], l_sel + bias_sel, -jnp.inf)
        k_own = lax.dynamic_slice_in_dim(k_p, cur * MOBA_BLOCK, MOBA_BLOCK, axis=2)
        v_own = lax.dynamic_slice_in_dim(v_p, cur * MOBA_BLOCK, MOBA_BLOCK, axis=2)
        kpos_own = cur * MOBA_BLOCK + kpos_in_blk
        dist_own = qpos[:, None] - kpos_own[None, :]
        bias_own = rel_bias[t5_bucket(dist_own)].transpose(2, 0, 1)
        l_own = jnp.einsum('bhqd,bhld->bhql', q_i, k_own).astype(jnp.float32) * ATTN_SCALE
        l_own = jnp.where(dist_own >= 0, l_own + bias_own, -jnp.inf)
        logits = jnp.concatenate(
            [l_sel.reshape(bsz, nh, MOBA_Q_CHUNK, topk * MOBA_BLOCK), l_own], axis=-1)
        p = jax.nn.softmax(logits, axis=-1).astype(v.dtype)
        p_sel = p[..., :topk * MOBA_BLOCK].reshape(bsz, nh, MOBA_Q_CHUNK, topk, MOBA_BLOCK)
        p_own = p[..., topk * MOBA_BLOCK:]
        return (jnp.einsum('bhqtl,bhqtld->bhqd', p_sel, v_sel)
                + jnp.einsum('bhql,bhld->bhqd', p_own, v_own))

    out = lax.map(one_chunk, (jnp.arange(nq), q_chunks))
    return out.transpose(1, 2, 0, 3, 4).reshape(bsz, nh, s, dh)

def odd_mixer(h, w_in, b_f, w_out, rel_bias):
    bsz, s, _ = h.shape
    z = h @ w_in
    qkv = z[..., :3 * ATT_W].reshape(bsz, s, 3, H_ATT, HEAD_DIM).transpose(2, 0, 3, 1, 4)
    q, k, v = qkv[0], qkv[1], qkv[2]
    log_f = jax.nn.log_sigmoid((z[..., 3 * ATT_W:] + b_f).astype(jnp.float32)).transpose(0, 2, 1)
    y_c = forgetting_attention(q[:, :H_FOX], k[:, :H_FOX], v[:, :H_FOX], log_f)
    y_d = moba_attention(q[:, H_FOX:], k[:, H_FOX:], v[:, H_FOX:], rel_bias)
    y = jnp.concatenate([y_c, y_d], axis=1).transpose(0, 2, 1, 3).reshape(bsz, s, ATT_W)
    return y @ w_out

def conv_ffn(h, w_in, conv_w, conv_b, w_out):
    z = h @ w_in
    u, g = z[..., :D_FF], z[..., D_FF:]
    a = causal_dwconv(u, conv_w) + conv_b
    return (jax.nn.silu(a) * g) @ w_out

def first_inputs(seed: int = 0) -> dict:
    key = jax.random.key(seed)
    ks = jax.random.split(key, 17)
    f32 = jnp.float32

    def nrm(k, shape, scale):
        return jax.random.normal(k, shape, f32) * scale

    out_scale = (2 * DEPTH) ** -0.5
    return {
        "x": nrm(ks[0], (BATCH, SEQ, D_MODEL), 1.0),
        "mix_norm_g": 1.0 + nrm(ks[1], (DEPTH, D_MODEL), 0.05),
        "ffn_norm_g": 1.0 + nrm(ks[2], (DEPTH, D_MODEL), 0.05),
        "final_norm_g": 1.0 + nrm(ks[3], (D_MODEL,), 0.05),
        "ev_w_in": nrm(ks[4], (N_EVEN, D_MODEL, EV_IN_W), D_MODEL ** -0.5),
        "ev_conv_w": nrm(ks[5], (N_EVEN, CONV_W, A_W), CONV_W ** -0.5),
        "ev_pool_w": nrm(ks[6], (N_EVEN, N_POOL, POOL_G, POOL_G), POOL_G ** -0.5),
        "ev_pool_scale": 1.0 + nrm(ks[7], (N_EVEN, B_W), 0.1),
        "ev_w_out": nrm(ks[8], (N_EVEN, MIX_W, D_MODEL), MIX_W ** -0.5 * out_scale),
        "od_w_in": nrm(ks[9], (N_ODD, D_MODEL, OD_IN_W), D_MODEL ** -0.5),
        "od_b_f": FORGET_BIAS_INIT + nrm(ks[10], (N_ODD, H_FOX), 0.5),
        "od_w_out": nrm(ks[11], (N_ODD, ATT_W, D_MODEL), ATT_W ** -0.5 * out_scale),
        "rel_bias": nrm(ks[12], (T5_BUCKETS, H_MOBA), 0.5),
        "ffn_w_in": nrm(ks[13], (DEPTH, D_MODEL, 2 * D_FF), D_MODEL ** -0.5),
        "ffn_conv_w": nrm(ks[14], (DEPTH, CONV_W, D_FF), CONV_W ** -0.5),
        "ffn_conv_b": nrm(ks[15], (DEPTH, D_FF), 0.02),
        "ffn_w_out": nrm(ks[16], (DEPTH, D_FF, D_MODEL), D_FF ** -0.5 * out_scale),
    }

def first_block(x, mix_norm_g, ffn_norm_g, final_norm_g, ev_w_in, ev_conv_w, ev_pool_w,
              ev_pool_scale, ev_w_out, od_w_in, od_b_f, od_w_out, rel_bias,
              ffn_w_in, ffn_conv_w, ffn_conv_b, ffn_w_out):
    h = x
    for layer in range(DEPTH):
        hn = rmsnorm(h, mix_norm_g[layer])
        if layer % 2 == 0:
            e = layer // 2
            h = h + even_mixer(hn, ev_w_in[e], ev_conv_w[e], ev_pool_w[e],
                               ev_pool_scale[e], ev_w_out[e])
        else:
            o = layer // 2
            h = h + odd_mixer(hn, od_w_in[o], od_b_f[o], od_w_out[o], rel_bias)
        h = h + conv_ffn(rmsnorm(h, ffn_norm_g[layer]), ffn_w_in[layer],
                         ffn_conv_w[layer], ffn_conv_b[layer], ffn_w_out[layer])
    return rmsnorm(h, final_norm_g)


GRID_W = 64
CTX_LEN = 256
N_MIXERS = 2
N_A = (DEPTH + 1) // 2
N_B = DEPTH // 2
MLA_HEADS = 8
QK_NOPE = 128
QK_ROPE = 64
V_DIM = 128
QK_DIM = QK_NOPE + QK_ROPE
Q_LORA = 384
KV_LORA = 256
ROPE_THETA = 10000.0
Q_BLOCK = 128
GM_CHUNK = 128
GM_GROUPS = 8
GM_HALF = 2 * D_MODEL
GM_GROUP_DIM = GM_HALF // GM_GROUPS
FFN_HIDDEN = 4 * D_MODEL
N_MOD = 6
EPS = 1e-6


def rmsnorm_2(x, g):
    xf = x.astype(jnp.float32)
    y = xf * lax.rsqrt(jnp.mean(xf * xf, axis=-1, keepdims=True) + EPS)
    return (y * g.astype(jnp.float32)).astype(x.dtype)

def layernorm(x, g, b):
    xf = x.astype(jnp.float32)
    mu = jnp.mean(xf, axis=-1, keepdims=True)
    var = jnp.mean(jnp.square(xf - mu), axis=-1, keepdims=True)
    y = (xf - mu) * lax.rsqrt(var + EPS)
    return (y * g.astype(jnp.float32) + b.astype(jnp.float32)).astype(x.dtype)

def modulate(x, g, shift, scale):
    return rmsnorm_2(x, g) * (1.0 + scale) + shift

def axial_rope_tables(n_tokens, dtype):
    rows = n_tokens // GRID_W
    row = jnp.repeat(jnp.arange(rows, dtype=jnp.float32), GRID_W)
    col = jnp.tile(jnp.arange(GRID_W, dtype=jnp.float32), rows)
    half = QK_ROPE // 2
    inv = ROPE_THETA ** (-jnp.arange(0, half, 2, dtype=jnp.float32) / half)
    ang_r = row[:, None] * inv[None, :]
    ang_c = col[:, None] * inv[None, :]
    ang = jnp.concatenate([ang_r, ang_r, ang_c, ang_c], axis=-1)
    return jnp.cos(ang).astype(dtype), jnp.sin(ang).astype(dtype)

def rotate_axial(x):
    a1, a2, b1, b2 = jnp.split(x, 4, axis=-1)
    return jnp.concatenate([-a2, a1, -b2, b1], axis=-1)

def rope_part(t, cos, sin):
    nope, pe = t[..., :QK_NOPE], t[..., QK_NOPE:]
    c = cos[None, :, None, :]
    s = sin[None, :, None, :]
    return jnp.concatenate([nope, pe * c + rotate_axial(pe) * s], axis=-1)

def block_attention(q, k, v, scale):
    B, Sq, H, Dk = q.shape
    nb = Sq // Q_BLOCK
    qb = q.reshape(B, nb, Q_BLOCK, H, Dk).transpose(1, 0, 2, 3, 4)

    def one(qi):
        s = jnp.einsum('bqhd,bkhd->bhqk', qi, k, preferred_element_type=jnp.float32) * scale
        p = jax.nn.softmax(s, axis=-1)
        return jnp.einsum('bhqk,bkhd->bqhd', p.astype(v.dtype), v)

    o = lax.map(one, qb)
    return o.transpose(1, 0, 2, 3, 4).reshape(B, Sq, H, v.shape[-1])

def mla_queries(h, wq_a, q_a_norm, wq_b, q_norm):
    B, S, _ = h.shape
    cq = rmsnorm_2(h @ wq_a, q_a_norm)
    q = (cq @ wq_b).reshape(B, S, MLA_HEADS, QK_DIM)
    return rmsnorm_2(q, q_norm)

def mla_keys_values(h, wkv_a, kv_a_norm, wkv_b, k_norm):
    B, S, _ = h.shape
    kv_a = h @ wkv_a
    ckv, k_pe = kv_a[..., :KV_LORA], kv_a[..., KV_LORA:]
    kv = (rmsnorm_2(ckv, kv_a_norm) @ wkv_b).reshape(B, S, MLA_HEADS, QK_NOPE + V_DIM)
    k_nope, v = kv[..., :QK_NOPE], kv[..., QK_NOPE:]
    k_pe = jnp.broadcast_to(k_pe[:, :, None, :], (B, S, MLA_HEADS, QK_ROPE))
    k = rmsnorm_2(jnp.concatenate([k_nope, k_pe], axis=-1), k_norm)
    return k, v

def mla_mixer(h_lat, h_ctx, cos, sin, wq_a, q_a_norm, wq_b, wkv_a, kv_a_norm, wkv_b,
              q_norm, k_norm, wo, with_ctx):
    B, S, _ = h_lat.shape
    scale = QK_DIM ** -0.5
    k_lat, v_lat = mla_keys_values(h_lat, wkv_a, kv_a_norm, wkv_b, k_norm)
    k_ctx, v_ctx = mla_keys_values(h_ctx, wkv_a, kv_a_norm, wkv_b, k_norm)
    k_lat = rope_part(k_lat, cos, sin)
    q_lat = rope_part(mla_queries(h_lat, wq_a, q_a_norm, wq_b, q_norm), cos, sin)
    k_all = jnp.concatenate([k_ctx, k_lat], axis=1)
    v_all = jnp.concatenate([v_ctx, v_lat], axis=1)
    o_lat = block_attention(q_lat, k_all, v_all, scale).reshape(B, S, MLA_HEADS * V_DIM) @ wo
    o_ctx = None
    if with_ctx:
        q_ctx = mla_queries(h_ctx, wq_a, q_a_norm, wq_b, q_norm)
        o_ctx = block_attention(q_ctx, k_ctx, v_ctx, scale).reshape(
            B, h_ctx.shape[1], MLA_HEADS * V_DIM) @ wo
    return o_lat, o_ctx

def gmlp_mixer(h, w_in, ln_g, ln_b, ws, bs, w_out):
    B, S, _ = h.shape
    z = jax.nn.gelu(h @ w_in, approximate=False)
    u, v = z[..., :GM_HALF], z[..., GM_HALF:]
    v = layernorm(v, ln_g, ln_b)
    vc = v.reshape(B, S // GM_CHUNK, GM_CHUNK, GM_GROUPS, GM_GROUP_DIM)
    mixed = jnp.einsum('gpq,bnqgc->bnpgc', ws, vc) + bs.T[None, None, :, :, None]
    return (u * mixed.reshape(B, S, GM_HALF)) @ w_out

def squared_relu_mlp(h, w1, w2):
    return jnp.square(jax.nn.relu(h @ w1)) @ w2

def second_inputs(seed: int = 0) -> dict:
    key = jax.random.key(seed)
    ks = jax.random.split(key, 32)
    D = D_MODEL

    def nrm(k, shape, scale):
        return jax.random.normal(k, shape, jnp.float32) * scale

    def gain(k, shape):
        return 1.0 + 0.05 * jax.random.normal(k, shape, jnp.float32)

    return {
        "x": nrm(ks[0], (BATCH, SEQ, D), 1.0),
        "c": nrm(ks[1], (BATCH, D), 1.0),
        "ctx": nrm(ks[2], (BATCH, CTX_LEN, D), 1.0),
        "c_ctx": nrm(ks[3], (D,), 1.0),
        "ada_w": nrm(ks[4], (DEPTH, D, N_MOD * D), 0.5 * D ** -0.5),
        "ada_b": nrm(ks[5], (DEPTH, N_MOD * D), 0.01),
        "norm_mix_g": gain(ks[6], (DEPTH, D)),
        "norm_ffn_g": gain(ks[7], (DEPTH, D)),
        "mla_wq_a": nrm(ks[8], (N_A, D, Q_LORA), D ** -0.5),
        "mla_q_a_norm": gain(ks[9], (N_A, Q_LORA)),
        "mla_wq_b": nrm(ks[10], (N_A, Q_LORA, MLA_HEADS * QK_DIM), Q_LORA ** -0.5),
        "mla_wkv_a": nrm(ks[11], (N_A, D, KV_LORA + QK_ROPE), D ** -0.5),
        "mla_kv_a_norm": gain(ks[12], (N_A, KV_LORA)),
        "mla_wkv_b": nrm(ks[13], (N_A, KV_LORA, MLA_HEADS * (QK_NOPE + V_DIM)), KV_LORA ** -0.5),
        "mla_q_norm": gain(ks[14], (N_A, QK_DIM)),
        "mla_k_norm": gain(ks[15], (N_A, QK_DIM)),
        "mla_wo": nrm(ks[16], (N_A, MLA_HEADS * V_DIM, D), (MLA_HEADS * V_DIM) ** -0.5),
        "gm_w_in": nrm(ks[17], (N_B, D, 2 * GM_HALF), D ** -0.5),
        "gm_ln_g": gain(ks[18], (N_B, GM_HALF)),
        "gm_ln_b": nrm(ks[19], (N_B, GM_HALF), 0.02),
        "gm_ws": nrm(ks[20], (N_B, GM_GROUPS, GM_CHUNK, GM_CHUNK), GM_CHUNK ** -0.5),
        "gm_bs": gain(ks[21], (N_B, GM_GROUPS, GM_CHUNK)),
        "gm_w_out": nrm(ks[22], (N_B, GM_HALF, D), GM_HALF ** -0.5),
        "ffn_w1": nrm(ks[23], (DEPTH, D, FFN_HIDDEN), D ** -0.5),
        "ffn_w2": nrm(ks[24], (DEPTH, FFN_HIDDEN, D), FFN_HIDDEN ** -0.5),
    }

def second_block(x, c, ctx, c_ctx, ada_w, ada_b, norm_mix_g, norm_ffn_g,
              mla_wq_a, mla_q_a_norm, mla_wq_b, mla_wkv_a, mla_kv_a_norm, mla_wkv_b,
              mla_q_norm, mla_k_norm, mla_wo,
              gm_w_in, gm_ln_g, gm_ln_b, gm_ws, gm_bs, gm_w_out,
              ffn_w1, ffn_w2):
    S = x.shape[1]
    cos, sin = axial_rope_tables(S, x.dtype)
    silu_c = jax.nn.silu(c)
    silu_cc = jax.nn.silu(c_ctx)
    y = ctx
    for i in range(DEPTH):
        with_ctx = i < DEPTH - 1
        use_mla = (i % N_MIXERS) == 0
        j = i // N_MIXERS
        m_lat = (silu_c @ ada_w[i] + ada_b[i])[:, None, :]
        m_ctx = silu_cc @ ada_w[i] + ada_b[i]
        sh_m, sc_m, g_m, sh_f, sc_f, g_f = jnp.split(m_lat, N_MOD, axis=-1)
        csh_m, csc_m, cg_m, csh_f, csc_f, cg_f = jnp.split(m_ctx, N_MOD, axis=-1)

        h_lat = modulate(x, norm_mix_g[i], sh_m, sc_m)
        if use_mla:
            h_ctx = modulate(y, norm_mix_g[i], csh_m, csc_m)
            o_lat, o_ctx = mla_mixer(h_lat, h_ctx, cos, sin, mla_wq_a[j], mla_q_a_norm[j],
                                     mla_wq_b[j], mla_wkv_a[j], mla_kv_a_norm[j], mla_wkv_b[j],
                                     mla_q_norm[j], mla_k_norm[j], mla_wo[j], with_ctx)
        else:
            o_lat = gmlp_mixer(h_lat, gm_w_in[j], gm_ln_g[j], gm_ln_b[j], gm_ws[j], gm_bs[j],
                               gm_w_out[j])
            o_ctx = None
            if with_ctx:
                h_ctx = modulate(y, norm_mix_g[i], csh_m, csc_m)
                o_ctx = gmlp_mixer(h_ctx, gm_w_in[j], gm_ln_g[j], gm_ln_b[j], gm_ws[j], gm_bs[j],
                                   gm_w_out[j])
        x = x + g_m * o_lat
        x = x + g_f * squared_relu_mlp(modulate(x, norm_ffn_g[i], sh_f, sc_f), ffn_w1[i], ffn_w2[i])
        if with_ctx:
            y = y + cg_m * o_ctx
            y = y + cg_f * squared_relu_mlp(modulate(y, norm_ffn_g[i], csh_f, csc_f),
                                            ffn_w1[i], ffn_w2[i])
    return x


def setup_inputs(seed=0):
    out = dict(first_inputs(seed))
    for name, value in second_inputs(seed + 1).items():
        if name != "x":
            out[name + "_2"] = value
    return out


def reference(
    x, mix_norm_g, ffn_norm_g, final_norm_g, ev_w_in, ev_conv_w, ev_pool_w, ev_pool_scale,
    ev_w_out, od_w_in, od_b_f, od_w_out, rel_bias, ffn_w_in, ffn_conv_w, ffn_conv_b, ffn_w_out,
    c_2, ctx_2, c_ctx_2, ada_w_2, ada_b_2, norm_mix_g_2, norm_ffn_g_2, mla_wq_a_2,
    mla_q_a_norm_2, mla_wq_b_2, mla_wkv_a_2, mla_kv_a_norm_2, mla_wkv_b_2, mla_q_norm_2,
    mla_k_norm_2, mla_wo_2, gm_w_in_2, gm_ln_g_2, gm_ln_b_2, gm_ws_2, gm_bs_2, gm_w_out_2,
    ffn_w1_2, ffn_w2_2,
):
    x = first_block(
        x, mix_norm_g, ffn_norm_g, final_norm_g, ev_w_in, ev_conv_w, ev_pool_w, ev_pool_scale,
        ev_w_out, od_w_in, od_b_f, od_w_out, rel_bias, ffn_w_in, ffn_conv_w, ffn_conv_b,
        ffn_w_out,
    )
    return second_block(
        x, c_2, ctx_2, c_ctx_2, ada_w_2, ada_b_2, norm_mix_g_2, norm_ffn_g_2, mla_wq_a_2,
        mla_q_a_norm_2, mla_wq_b_2, mla_wkv_a_2, mla_kv_a_norm_2, mla_wkv_b_2, mla_q_norm_2,
        mla_k_norm_2, mla_wo_2, gm_w_in_2, gm_ln_g_2, gm_ln_b_2, gm_ws_2, gm_bs_2, gm_w_out_2,
        ffn_w1_2, ffn_w2_2,
    )


_drawn_inputs = setup_inputs


def setup_inputs(seed=0):
    import zlib

    import numpy as np

    out = dict(_drawn_inputs(seed))
    spreads = {}
    factors = {'ffn_conv_b': 7.127,
     'ctx_2': 3.587,
     'norm_mix_g_2': 3.264,
     'mla_q_a_norm_2': 8.0,
     'mla_kv_a_norm_2': 8.0,
     'mla_q_norm_2': 8.0,
     'mla_k_norm_2': 8.0,
     'gm_ln_g_2': 5.544,
     'gm_ln_b_2': 24.295,
     'gm_bs_2': 5.722,
     'norm_ffn_g_2': 4.521}
    for name, (base, spread) in spreads.items():
        noise = np.random.default_rng([zlib.crc32(name.encode()), seed]).standard_normal(out[name].shape)
        drawn = base * np.exp(spread * noise) if base else spread * noise
        out[name] = jnp.asarray(drawn.astype(out[name].dtype))
    for name, factor in factors.items():
        out[name] = (out[name] * factor).astype(out[name].dtype)
    return out
```

```python
from contextlib import ExitStack

import concourse.bass as bass
from concourse import mybir

F32 = mybir.dt.float32
F32R = mybir.dt.float32r
ALU = mybir.AluOpType
ACT = mybir.ActivationFunctionType
AX = mybir.AxisListType

P = 128
S = 256
TT = S // P
D = 1024
KB = D // P
FF = 2816
FFB = FF // P
HID = 4096
GMH = 2048
EPS = 1e-6
SLOTS = 4
SLOT_W = 2048
HD = 64
HEADS = 16
FOX = 8
MH = 8
NOPE, ROPE, VD = 128, 64, 128
QKD = NOPE + ROPE
QL, KVL = 384, 256
CTX = 256
KT = (CTX + S) // P
NEG = -1e30

C_ID, C_U, C_MASK, C_TAB, C_COS, C_SIN = 0, 128, 384, 512, 576, 704
C_ALL = 832
ROWS = [("mix_norm_g", 16), ("ffn_norm_g", 16), ("ev_conv_w", 12), ("ev_pool_scale", 4), ("ffn_conv_w", 132),
        ("ffn_conv_b", 44), ("norm_mix_g_2", 16), ("norm_ffn_g_2", 16), ("c_2", 8), ("c_ctx_2", 8),
        ("mla_q_a_norm_2", 3), ("mla_kv_a_norm_2", 2), ("mla_q_norm_2", 1), ("mla_k_norm_2", 1),
        ("ada_b_2", 96)]
ROW = {}
_n = 0
for _name, _k in ROWS:
    ROW[_name] = _n
    _n += _k
N_ROWS = _n
ROW_TILES = -(-N_ROWS // P)
N_ROW_DMAS = sum((ROW[_name] + _k - 1) // P - ROW[_name] // P + 1 for _name, _k in ROWS)


class Aff:

    def __init__(self, c, reg=None, k=0):
        self.c, self.reg, self.k = c, reg, k

    def __add__(self, n):
        return Aff(self.c + n, self.reg, self.k)

    def __sub__(self, n):
        return self + (-n)

    def __mul__(self, n):
        return Aff(self.c * n, self.reg, self.k * n)


def val(x):
    if not isinstance(x, Aff):
        return x
    return x.c if x.reg is None else x.reg * x.k + x.c


def build(nc, I, out):
    ctx = ExitStack()
    with ctx:
        def sb(name, shape, dt=F32):
            return ctx.enter_context(nc.sbuf_tensor(name, shape, dt))

        def sem(name):
            return ctx.enter_context(nc.semaphore(name))

        raw = [sb(f"raw{i}", [P, SLOT_W]) for i in range(SLOTS)]
        w_hi = [sb(f"w_hi{i}", [P, SLOT_W], F32R) for i in range(SLOTS)]
        w_lo = [sb(f"w_lo{i}", [P, SLOT_W], F32R) for i in range(SLOTS)]
        xn_hi, xn_lo = sb("xn_hi", [P, KB * S], F32R), sb("xn_lo", [P, KB * S], F32R)
        a_hi, a_lo = sb("a_hi", [P, KB * S], F32R), sb("a_lo", [P, KB * S], F32R)
        h = sb("h", [P, TT, D])
        side = sb("side", [P, SLOTS, 1024])
        acc = sb("acc", [P, 5, 1024])
        work = sb("work", [P, 7424])
        cst = sb("cst", [P, C_ALL])
        vec = sb("vec", [P, ROW_TILES * P])
        st = sb("st", [P, 88])
        mod = sb("mod", [P, 48])
        cs = sb("cs", [P, 16])
        pe_g = sb("pe_g", [P, 2, ROPE])
        bf = sb("bf", [P, 8])
        wf = sb("wf", [P, KB, 8])
        zf = sb("zf", [P, 5, 16])
        rs = sb("rs", [P, 40])
        rstd = sb("rstd", [P, 40])
        half = sb("half", [P, 8])
        rel = sb("rel", [33, 8])
        ps = [ctx.enter_context(nc.psum_tensor(f"ps{i}", [P, 512], F32)) for i in range(8)]

        ident = cst[:, C_ID:C_ID + P]
        tri_ones = cst[:, C_U:C_U + 2 * P]
        ones = cst[:, C_U + P:C_U + 2 * P]
        causal = cst[:, C_MASK:C_MASK + P]
        pool_tab = cst[:, C_TAB:C_TAB + 64].rearrange("p (g t) -> p g t", g=4)
        cos = cst[:, C_COS:C_COS + P].rearrange("p (t d) -> p t d", t=TT)
        sin = cst[:, C_SIN:C_SIN + P].rearrange("p (t d) -> p t d", t=TT)

        def wk(a, n):
            return work[:, a:a + n]

        hs = wk(0, 2048).rearrange("p (t d) -> p t d", t=TT)
        xf = wk(4096, 2048).rearrange("p (k t) -> p k t", k=KB)
        xn_hi3 = xn_hi[:, :].rearrange("p (k t) -> p k t", k=KB)
        xn_lo3 = xn_lo[:, :].rearrange("p (k t) -> p k t", k=KB)
        a_hi3 = a_hi[:, :].rearrange("p (k t) -> p k t", k=KB)
        a_lo3 = a_lo[:, :].rearrange("p (k t) -> p k t", k=KB)

        def col(name, n=0):
            c = ROW[name] + n
            return vec[:, c:c + 1]

        def vcol(name, n):
            return vec[:, bass.ds(val(n + ROW[name]), 1)]

        scratch = nc.dram_tensor("bias_rows", (8, 512), F32, kind="Internal").ap()

        def kview(w):
            return w.rearrange("(k p) n -> p k n", p=P)

        def f_src(w, c0=0, stride=256, n=256):
            v = kview(w)
            return lambda j: v[:, :, bass.ds(val(j * stride + c0), n)]

        def t_src(w, n):
            v = kview(w)
            return lambda j: v[:, bass.ds(val(j * n), n), :]

        width, straight = [], {}

        def add(src, kb, n, at=0):
            width.append(sum(k * m for _, k, m, _ in (src if isinstance(src, list) else [(0, kb, n, 0)])))
            straight[len(width) - 1] = src if isinstance(src, list) else [(src, kb, n, at)]

        ev_w = I["ev_w_in"][0]
        T_EV = len(width)
        EV_COLS = [512, 1024, 0, 768, 1280, 256, 1536, 1792]
        for c0 in EV_COLS:
            add(f_src(ev_w, c0), KB, 256)
        T_EVO = len(width)
        for j in range(2):
            add(t_src(I["ev_w_out"][0], 2), 2, D, j)
        T_POOL = len(width)
        pool_v = I["ev_pool_w"][0].rearrange("g c d -> c g d")
        add(lambda j: pool_v, 4, P)
        for j in range(2, 4):
            add(t_src(I["ev_w_out"][0], 2), 2, D, j)

        G_STEPS = FFB // 2

        def gated_sources(layer):
            w, wo = I["ffn_w_in"][layer], I["ffn_w_out"][layer]
            return f_src(w), f_src(w, FF), t_src(wo, 1)

        def add_gated(layer):
            u, g, t = gated_sources(layer)
            base = len(width)
            for j in range(G_STEPS + 1):
                if j < G_STEPS:
                    add(u, KB, 256, j)
                    add(g, KB, 256, j)
                if j:
                    add(t, 1, D, 2 * j - 2)
                    add(t, 1, D, 2 * j - 1)
            return base

        R_STEPS = HID // 256

        def relu_sources(layer):
            return f_src(I["ffn_w1_2"][layer]), t_src(I["ffn_w2_2"][layer], 2)

        def add_paired(f, t, steps):
            base = len(width)
            for j in range(steps + 1):
                if j < steps:
                    add(f, KB, 256, j)
                if j:
                    add(t, 2, D, j - 1)
            return base

        T_FFN0 = add_gated(0)
        od_w = I["od_w_in"][0]
        T_QK = len(width)
        for j in range(8):
            add(f_src(od_w), KB, 256, j)
        T_V = len(width)
        for j in range(4):
            add(t_src(od_w[:, 2 * D:3 * D], 2), 2, D, j)
        T_ODO = len(width)
        for j in range(4):
            add(t_src(I["od_w_out"][0], 2), 2, D, j)
        T_FFN1 = add_gated(1)
        T_LA = len(width)
        kva_v = kview(I["mla_wkv_a_2"][0])
        qa_v = kview(I["mla_wq_a_2"][0])
        for j in range(2):
            add(lambda j: kva_v[:, 4 * j:4 * j + 4, :], 4, KVL + ROPE, j)
        for j in range(2):
            add(lambda j: qa_v[:, 4 * j:4 * j + 4, :], 4, QL, j)
        T_HEAD = len(width)
        kvb_v = kview(I["mla_wkv_b_2"][0])
        qb_v = kview(I["mla_wq_b_2"][0])
        for j in range(MH):
            add([(lambda j: kvb_v[:, :, 256 * j:256 * j + 256], 2, 256, j),
                 (lambda j: qb_v[:, :, QKD * j:QKD * j + QKD], 3, QKD, j)], 0, 0)
        T_WO = len(width)
        for j in range(4):
            add(t_src(I["mla_wo_2"][0], 2), 2, D, j)
        T_RELU0 = add_paired(*relu_sources(0), R_STEPS)
        T_GMV = len(width)
        gm_w = I["gm_w_in_2"][0]
        gmv_v = kview(gm_w)
        for j in range(8):
            add(lambda j: gmv_v[:, 4 * (j % 2):4 * (j % 2) + 4, GMH + 512 * (j // 2):GMH + 512 * (j // 2) + 512],
                4, 512, j)
        GM_STEPS = GMH // 256
        T_GM = add_paired(f_src(gm_w), t_src(I["gm_w_out_2"][0], 2), GM_STEPS)
        T_RELU1 = add_paired(*relu_sources(1), R_STEPS)
        N_TILES = len(width)

        LOOP0, LOOP1 = 2, 10
        TRIPS = (LOOP1 - LOOP0) // 2

        U_FFN0 = 0
        U_FFN1 = U_FFN0 + 16
        U_BC1 = U_FFN1 + 32
        U_RELU0 = U_BC1 + 3
        U_BC2 = U_RELU0 + 32
        U_GM = U_BC2 + 5
        U_BC3 = U_GM + 16

        raw_full = [sem(f"raw_full{i}") for i in range(SLOTS)]
        hi_done, lo_done, w_used = sem("hi_done"), sem("lo_done"), sem("w_used")
        side_full = [sem(f"side_full{i}") for i in range(SLOTS)]
        side_used = sem("side_used")
        in_h, in_cst, in_rows, in_small = sem("in_h"), sem("in_cst"), sem("in_rows"), sem("in_small")
        vec_ps, vec_ready, cs_ready = sem("vec_ps"), sem("vec_ready"), sem("cs_ready")
        rb_ready, half_ready, rows_ps, rows_sb, rows_out = sem("rb_ready"), sem("half_ready"), sem("rows_ps"), sem("rows_sb"), sem("rows_out")
        bias_in, ctx_in = sem("bias_in"), sem("ctx_in")
        h_ready, sq_done, ms_step, rstd_ready = sem("h_ready"), sem("sq_done"), sem("ms_step"), sem("rstd_ready")
        hs_ready, xt_ps, xf_ready = sem("hs_ready"), sem("xt_ps"), sem("xf_ready")
        xhi_done, xn_ready = sem("xhi_done"), sem("xn_ready")
        acc_zero, ada_done, ada_ps, mod_step, mod_ready = (
            sem("acc_zero"), sem("ada_done"), sem("ada_ps"), sem("mod_step"), sem("mod_ready"))
        all_out = sem("all_out")
        act_step, dve_step, pool_step = sem("act_step"), sem("dve_step"), sem("pool_step")

        def group(prefix, *names):
            return {n: sem(f"{prefix}_{n}") for n in names}

        EV = group("ev", "gate", "prod", "tap2", "tap1", "conv", "y", "yhi", "a_ready", "pin", "pool", "phi",
                   "pool_ready", "pool_mm", "ybf", "ybhi")
        FFN = [group(f"ffn{n}", "a0", "tap", "conv", "silu", "prod", "ahi", "a_ready") for n in range(2)]
        RELU = [group(f"relu{n}", "relu", "sq", "ahi", "a_ready") for n in range(2)]
        AT = group("at", "qk", "v_sb", "z_ps", "z", "nabs", "ez", "ln", "neg", "f_ps", "f", "lbc", "s_ps", "s_sb",
                   "max", "exp", "rec", "p", "t_ps", "pt", "o_ps", "ohi", "a_ready")
        LA = group("la", "kv_sb", "q_sb", "lsq", "lrstd", "lscaled", "lt_ps", "lxf", "lhi", "l_ready", "kpe", "a_ps", "a_sq",
                   "a_ms", "a_rstd", "kn", "qpe", "kq_ps", "kq", "s_ps", "max", "exp", "rec", "p", "t_ps", "pt_a", "pt_d",
                   "o_ps", "ohi", "a_ready")
        GM = group("gm", "v", "mu", "sq", "rstd", "norm", "gain", "vn", "ws_in", "ws_ps", "ws", "bs_in", "u", "vs", "m_ps",
                   "t", "prod", "ahi", "a_ready")

        block = ctx.enter_context(nc.Block())

        NORM = {n: k for k, n in enumerate(
            ["ev", "ffn0", "od", "ffn1", "ctx", "lat", "relu0", "gm", "relu1"])}
        H_READY = {"ffn0": 0, "od": 2, "ffn1": 4, "final": 6, "lat": 8, "relu0": 10, "gm": 12, "relu1": 14, "out": 16}
        RSTD = {n: k for k, n in enumerate(
            ["ev", "ffn0", "od", "ffn1", "final", "ctx", "lat", "relu0", "gm", "relu1"])}
        RCOL = dict({n: 2 * k for n, k in NORM.items()}, final=18)
        MOD_COUNT = {"ctx": 1, "lat": 1, "relu0": 2, "gm": 3, "relu1": 4}

        @block.sync
        def _(sp):
            sp.dma_start(h[:, :, :], I["x"][0].rearrange("(t p) d -> p t d", p=P)).then_inc(in_h, 16)

            def load(t):
                if t >= SLOTS:
                    sp.wait_ge(lo_done, t - SLOTS + 1)
                at, parts = 0, straight[t]
                for src, k, n, j in parts:
                    dst = raw[t % SLOTS][:, at:at + k * n].rearrange("p (k n) -> p k n", k=k)
                    sp.dma_start(dst, src(j)).then_inc(raw_full[t % SLOTS], 16)
                    at += k * n

            def load_gated(layer, base):
                u, g, w = gated_sources(layer)
                first = base + 4 * LOOP0 - 2
                for t in range(base, first):
                    load(t)
                with sp.Fori(0, LOOP1 - LOOP0) as i:
                    j = Aff(LOOP0, i, 1)
                    views = [(u(j), KB, 256), (g(j), KB, 256), (w(j * 2 - 2), 1, D), (w(j * 2 - 1), 1, D)]
                    free = [sp.snap(val(j * 4 + (base - 2 + m - SLOTS + 1))) for m in range(4)]
                    for m, (src, k, n) in enumerate(views):
                        s = (first + m) % SLOTS
                        sp.wait_ge(lo_done, free[m])
                        sp.dma_start(raw[s][:, 0:k * n].rearrange("p (k n) -> p k n", k=k), src)\
                            .then_inc(raw_full[s], 16)
                for t in range(base + 4 * LOOP1 - 2, base + 4 * G_STEPS):
                    load(t)

            def load_paired(f, w, base, steps, loop0, loop1):
                first = base + 2 * loop0 - 1
                for t in range(base, first):
                    load(t)
                with sp.Fori(0, (loop1 - loop0) // 2) as i:
                    js = [Aff(loop0 + m, i, 2) for m in range(2)]
                    views = []
                    for j in js:
                        views += [(f(j), KB, 256), (w(j - 1), 2, D)]
                    free = [sp.snap(val(js[0] * 2 + (base - 1 + m - SLOTS + 1))) for m in range(4)]
                    for m, (src, k, n) in enumerate(views):
                        s = (first + m) % SLOTS
                        sp.wait_ge(lo_done, free[m])
                        sp.dma_start(raw[s][:, 0:k * n].rearrange("p (k n) -> p k n", k=k), src)\
                            .then_inc(raw_full[s], 16)
                for t in range(base + 2 * loop1 - 1, base + 2 * steps):
                    load(t)

            for t in range(T_EV, T_FFN0):
                load(t)
            load_gated(0, T_FFN0)
            for t in range(T_QK, T_FFN1):
                load(t)
            load_gated(1, T_FFN1)
            for t in range(T_LA, T_RELU0):
                load(t)
            load_paired(*relu_sources(0), T_RELU0, R_STEPS, 2, 14)
            for t in range(T_GMV, T_GM):
                load(t)
            load_paired(f_src(gm_w), t_src(I["gm_w_out_2"][0], 2), T_GM, GM_STEPS, 2, 6)
            load_paired(*relu_sources(1), T_RELU1, R_STEPS, 2, 14)
            sp.wait_ge(h_ready, H_READY["out"] + 2)
            sp.dma_start(out[0].rearrange("(t p) d -> p t d", p=P), h[:, :, :]).then_inc(all_out, 16)
            sp.wait_ge(all_out, 16)
            sp.wait_ge(rows_out, 16)

        landed = []
        per_slot = [0] * SLOTS
        for t in range(N_TILES):
            per_slot[t % SLOTS] += 16 * len(straight[t])
            landed.append(per_slot[t % SLOTS])

        @block.scalar
        def _(act):
            def split(t):
                t = t if isinstance(t, Aff) else Aff(t)
                if t.c >= N_TILES:
                    return
                s, w = t.c % SLOTS, width[t.c]
                act.wait_ge(raw_full[s], val(Aff(landed[t.c], t.reg, t.k * 16 // SLOTS)))
                if t.c >= SLOTS:
                    act.wait_ge(w_used, val(t - (SLOTS - 1)))
                nc.scalar.activation(w_hi[s][:, 0:w], raw[s][:, 0:w], ACT.Copy).then_inc(hi_done, 1)

            act.dma_start(cst[:, :], I["consts"][:, 0:C_ALL]).then_inc(in_cst, 16)
            at = 0
            stage = wk(6144, ROW_TILES * P).rearrange("p (r c) -> p r c", r=ROW_TILES)
            for name, n in ROWS:
                src = I[name]
                if name.endswith(("q_norm_2", "k_norm_2")):
                    src = src[0:1, 0:P]
                else:
                    while len(src.shape) > 1:
                        src = src.rearrange("a b -> (a b)") if len(src.shape) == 2 else src.rearrange("a b c -> (a b c)")
                    src = src.rearrange("(r c) -> r c", c=P)
                r = 0
                while r < n:
                    m = min(n - r, P - (at % P))
                    act.dma_start(stage[at % P:at % P + m, at // P, :], src[r:r + m, :]).then_inc(in_rows, 16)
                    r, at = r + m, at + m
            split(0)
            split(1)
            split(2)
            split(3)

            def norm(name, src, gain, shift=None):
                k = NORM[name]
                for t in range(TT):
                    if name == "ctx":
                        act.wait_ge(ctx_in, 16)
                    elif name == "ev":
                        act.wait_ge(in_h, 16)
                    else:
                        act.wait_ge(h_ready, H_READY[name] + t + 1)
                    nc.scalar.activation(hs[:, t, :], src[:, t, :], ACT.Square, accum_out=st[:, 2 * k + t:2 * k + t + 1])\
                        .then_inc(sq_done, 1)
                if name in ("ctx", "lat", "relu0", "gm", "relu1"):
                    act.wait_ge(mod_ready, MOD_COUNT[name])
                if name == "ev":
                    act.wait_ge(vec_ready, 1)
                for i in range(4):
                    act.wait_ge(xt_ps, 4 * k + i + 1)
                    for m in range(2):
                        b = 2 * i + m
                        if shift is None:
                            last = nc.scalar.activation(xf[:, b, :], ps[i][:, m * S:m * S + S], ACT.Copy, scale=gain(b))
                        else:
                            last = nc.scalar.activation(xf[:, b, :], ps[i][:, m * S:m * S + S], ACT.Identity,
                                                        scale=gain(b), bias=shift(b))
                    last.then_inc(xf_ready, 1)

            act.wait_ge(vec_ready, 1)
            nc.scalar.activation(cs[:, :], vec[:, ROW["c_2"]:ROW["c_2"] + 16], ACT.Silu).then_inc(cs_ready, 1)

            norm("ev", h, lambda b: col("mix_norm_g", b))

            ev_c = wk(6144, 512)
            ev_cv = wk(2048, 2 * 258).rearrange("p (b t) -> p b t", b=2)
            ev_a = wk(6656, 512).rearrange("p (b t) -> p b t", b=2)
            ev_y = wk(0, 512)
            for m in range(2):
                t = T_EV + 3 * m
                bank = 3 * m
                act.wait_ge(w_used, t + 1)
                nc.scalar.activation(ev_c, ps[bank % 4][:, :], ACT.Copy).then_inc(EV["gate"], 1)
                split(t + 4)
                act.wait_ge(EV["prod"], m + 1)
                for b in range(2):
                    nc.scalar.activation(ev_a[:, b, :], ev_cv[:, b, 2:258], ACT.Copy,
                                         scale=col("ev_conv_w", 8 + 2 * m + b)).then_inc(EV["tap2"], 1)
                split(t + 5)
                split(t + 6)
                act.wait_ge(EV["y"], m + 1)
                nc.scalar.activation(a_hi[:, 512 * m:512 * m + 512], ev_y, ACT.Copy).then_inc(EV["yhi"], 1)
            ev_u = wk(2564, 4 * 272).rearrange("p (g t) -> p g t", g=4)
            for m in range(2):
                t = T_EV + 6 + m
                act.wait_ge(w_used, t + 1)
                if m == 0:
                    act.wait_ge(EV["pin"], 1)
                nc.scalar.activation(ev_u[:, 2 * m:2 * m + 2, 16:272],
                                     ps[(6 + m) % 4][:, :].rearrange("p (g t) -> p g t", g=2), ACT.Copy)\
                    .then_inc(EV["pool"], 1)
                split(t + 4)
            split(T_EVO + 4)
            act.wait_ge(EV["pool_ready"], 1)
            nc.scalar.activation(a_hi[:, 1024:2048], wk(6144, 1024), ACT.Copy).then_inc(EV["phi"], 1)
            split(T_EVO + 5)
            for m in range(2):
                act.wait_ge(w_used, T_POOL + 1)
                for g in range(2):
                    nc.scalar.activation(wk(0, 1024)[:, (2 * m + g) * S:(2 * m + g + 1) * S], ps[m][:, g * S:g * S + S],
                                         ACT.Copy, scale=col("ev_pool_scale", 2 * m + g)).then_inc(EV["ybf"], 1)
            split(T_POOL + 4)
            act.wait_ge(EV["ybf"], 4)
            nc.scalar.activation(a_hi[:, 1024:2048], wk(0, 1024), ACT.Copy).then_inc(EV["ybhi"], 1)
            split(T_POOL + 5)
            split(T_POOL + 6)

            f_a0 = wk(6144, 512).rearrange("p (b t) -> p b t", b=2)
            f_s, f_p = wk(6656, 512), wk(2048, 512)

            def gated(n, base):
                g = FFN[n]

                def step(j, par):
                    u = j * 4 + (base - 2) if j.c else Aff(base)
                    act.wait_ge(w_used, val(u + 1))
                    for b in range(2):
                        nc.scalar.activation(f_a0[:, b, :], ps[0][:, b * S:b * S + S], ACT.Identity,
                                             scale=vcol("ffn_conv_w", j * 2 + (n * 3 * FFB + 2 * FFB + b)),
                                             bias=vcol("ffn_conv_b", j * 2 + (n * FFB + b))).then_inc(g["a0"], 1)
                    split(u + 4)
                    act.wait_ge(g["conv"], val(j * 2 + 2))
                    nc.scalar.activation(f_s, wk(6144, 512), ACT.Silu).then_inc(g["silu"], 1)
                    split(u + 5)
                    act.wait_ge(g["prod"], val(j + 1))
                    nc.scalar.activation(a_hi[:, par * 512:par * 512 + 512], f_p, ACT.Copy).then_inc(g["ahi"], 1)
                    if j.c:
                        split(u + 6)
                        split(u + 7)

                for j in range(LOOP0):
                    step(Aff(j), j % 2)
                with act.Fori(0, TRIPS) as i:
                    for m in range(2):
                        step(Aff(LOOP0 + m, i, 2), m)
                for j in range(LOOP1, G_STEPS):
                    step(Aff(j), j % 2)
                split(base + 4 * G_STEPS + 2)
                split(base + 4 * G_STEPS + 3)

            norm("ffn0", h, lambda b: col("ffn_norm_g", b))
            gated(0, T_FFN0)

            norm("od", h, lambda b: col("mix_norm_g", 8 + b))
            act.wait_ge(AT["nabs"], 1)
            nc.scalar.activation(zf[:, 1, :], zf[:, 1, :], ACT.Exp).then_inc(AT["ez"], 1)
            act.wait_ge(AT["ez"], 1)
            nc.scalar.activation(zf[:, 1, :], zf[:, 1, :], ACT.Ln, bias=1.0).then_inc(AT["ln"], 1)
            for j in range(8):
                act.wait_ge(w_used, T_QK + j + 1)
                nc.scalar.activation(wk(512 * j, 512), ps[j % 4][:, :], ACT.Copy, scale=HD ** -0.5 if j < 4 else 1.0)\
                    .then_inc(AT["qk"], 1)
                split(T_QK + j + 4)
            for j in range(4):
                split(T_V + j + 4)
            at_s = wk(6144, 768).rearrange("p (b k) -> p b k", b=2)
            at_pt = wk(6912, 384)
            SEG = [(0, P), (P, 3 * P)]

            def at_exp(i):
                act.wait_ge(AT["max"], 2 * i + 2)
                src = at_s[:, i % 2, :] if i < FOX else ps[i % 2]
                for t, (c0, c1) in enumerate(SEG):
                    nc.scalar.activation(at_s[:, i % 2, c0:c1], src[:, c0:c1], ACT.Exp,
                                         bias=st[:, 32 + 4 * (i % 2) + t:33 + 4 * (i % 2) + t],
                                         accum_out=st[:, 34 + 4 * (i % 2) + t:35 + 4 * (i % 2) + t]).then_inc(AT["exp"], 1)

            at_exp(0)
            for i in range(HEADS):
                act.wait_ge(AT["t_ps"], i + 1)
                nc.scalar.activation(at_pt, ps[2 + i % 2][:, 0:384], ACT.Copy).then_inc(AT["pt"], 1)
                if i + 1 < HEADS:
                    at_exp(i + 1)
                act.wait_ge(AT["o_ps"], i + 1)
                r = HD * (i % 2)
                nc.scalar.activation(a_hi3[r:r + HD, i // 2, :], ps[4 + i % 2][r:r + HD, 0:S], ACT.Copy).then_inc(AT["ohi"], 1)
            for j in range(4):
                split(T_ODO + j + 4)

            norm("ffn1", h, lambda b: col("ffn_norm_g", 8 + b))
            gated(1, T_FFN1)

            for t in range(TT):
                act.wait_ge(h_ready, H_READY["final"] + t + 1)
                nc.scalar.activation(wk(4096 + D * t, D), h[:, t, :], ACT.Square, accum_out=st[:, 18 + t:19 + t]).then_inc(sq_done, 1)

            ctxt = wk(2048, 2048).rearrange("p (t d) -> p t d", t=TT)
            kva = wk(6144, KT * (KVL + ROPE)).rearrange("p (t d) -> p t d", t=KT)
            cq = wk(2048, TT * QL).rearrange("p (t d) -> p t d", t=TT)
            norm("ctx", ctxt, lambda b: mod[:, 8 + b:9 + b], lambda b: mod[:, b:b + 1])

            act.wait_ge(LA["a_ps"], 1)
            for t in range(TT):
                nc.scalar.activation(kva[:, t, :], ps[4 + t][:, 0:KVL + ROPE], ACT.Copy).then_inc(LA["kv_sb"], 1)
            norm("lat", h, lambda b: mod[:, 24 + b:25 + b], lambda b: mod[:, 16 + b:17 + b])
            act.wait_ge(w_used, T_LA + 2)
            for t in range(TT):
                nc.scalar.activation(kva[:, TT + t, :], ps[6 + t][:, 0:KVL + ROPE], ACT.Copy).then_inc(LA["kv_sb"], 1)
            split(T_LA + 4)
            split(T_LA + 5)
            act.wait_ge(w_used, T_LA + 4)
            for t in range(TT):
                nc.scalar.activation(cq[:, t, :], ps[4 + t][:, 0:QL], ACT.Copy).then_inc(LA["q_sb"], 1)
            split(T_LA + 6)
            split(T_LA + 7)
            act.wait_ge(LA["kv_sb"], 4)
            act.wait_ge(LA["q_sb"], 2)
            for t in range(KT):
                nc.scalar.activation(wk(KVL * t, KVL), kva[:, t, 0:KVL], ACT.Square, accum_out=st[:, 48 + t:49 + t]).then_inc(LA["lsq"], 1)
            for t in range(TT):
                nc.scalar.activation(wk(KT * KVL + QL * t, QL), cq[:, t, :], ACT.Square, accum_out=st[:, 52 + t:53 + t]).then_inc(LA["lsq"], 1)
            for t in range(KT):
                nc.scalar.activation(wk(KT * KVL + TT * QL + ROPE * t, ROPE), kva[:, t, KVL:], ACT.Square, accum_out=st[:, 64 + t:65 + t])\
                    .then_inc(LA["lsq"], 1)
            lf_kv, lf_q = wk(4096, 1024), wk(5120, 768)
            act.wait_ge(LA["lt_ps"], 1)
            for b in range(2):
                nc.scalar.activation(lf_kv[:, 512 * b:512 * b + 512], ps[b][:, :], ACT.Copy, scale=col("mla_kv_a_norm_2", b))\
                    .then_inc(LA["lxf"], 1)
            for b in range(3):
                nc.scalar.activation(lf_q[:, S * b:S * b + S], ps[2 + b // 2][:, S * (b % 2):S * (b % 2) + S], ACT.Copy,
                                     scale=col("mla_q_a_norm_2", b)).then_inc(LA["lxf"], 1)

            la_kta = [wk(512 * p, 512) for p in range(2)]
            la_ktb = [wk(1024 + 512 * p, 512) for p in range(2)]
            la_qt = [wk(2048 + 512 * p, 512) for p in range(2)]
            la_v = [wk(3072 + 512 * p, 512).rearrange("p (t d) -> p t d", t=KT) for p in range(2)]
            la_p = wk(4096, 1024).rearrange("p (t k) -> p t k", t=TT)
            la_pt = wk(5120, 1024)
            la_junk = acc[:, 1, :]

            def la_values(i):
                act.wait_ge(w_used, T_HEAD + i + 1)
                for m in range(2):
                    kv2 = ps[m][:, :].rearrange("p (t d) -> p t d", t=2)
                    nc.scalar.activation(la_v[i % 2][:, 2 * m:2 * m + 2, :], kv2[:, :, NOPE:], ACT.Copy)
                for t in range(KT):
                    nc.scalar.activation(la_junk[:, NOPE * t:NOPE * t + NOPE], ps[t // 2][:, 256 * (t % 2):256 * (t % 2) + NOPE], ACT.Square,
                                         accum_out=st[:, 72 + t:73 + t]).then_inc(LA["a_sq"], 1)
                for t in range(TT):
                    nc.scalar.activation(la_junk[:, KT * NOPE + QKD * t:KT * NOPE + QKD * t + QKD], ps[2][:, QKD * t:QKD * t + QKD], ACT.Square,
                                         accum_out=st[:, 76 + t:77 + t]).then_inc(LA["a_sq"], 1)
                split(T_HEAD + i + 4)

            def la_transposed(i):
                act.wait_ge(LA["kq_ps"], i + 1)
                p = i % 2
                nc.scalar.activation(la_kta[p], ps[3][:, :], ACT.Copy, scale=col("mla_k_norm_2"))
                nc.scalar.activation(la_ktb[p][0:ROPE, :], ps[0][0:ROPE, :], ACT.Copy)
                nc.scalar.activation(la_qt[p][:, 0:S], ps[1][:, 0:S], ACT.Copy, scale=col("mla_q_norm_2"))
                nc.scalar.activation(la_qt[p][0:ROPE, S:2 * S], ps[1][0:ROPE, S:2 * S], ACT.Copy).then_inc(LA["kq"], 1)

            la_values(0)
            la_transposed(0)
            for i in range(MH):
                if i + 1 < MH:
                    la_values(i + 1)
                act.wait_ge(LA["max"], i + 1)
                for t in range(TT):
                    nc.scalar.activation(la_p[:, t, :], ps[4 + t][:, :], ACT.Exp, scale=QKD ** -0.5,
                                         bias=st[:, 82 + t:83 + t], accum_out=st[:, 84 + t:85 + t]).then_inc(LA["exp"], 1)
                if i + 1 < MH:
                    la_transposed(i + 1)
                act.wait_ge(LA["t_ps"], i + 1)
                nc.scalar.activation(la_pt[:, 0:512], ps[6][:, :], ACT.Copy).then_inc(LA["pt_a"], 1)
                act.wait_ge(LA["o_ps"], i + 1)
                nc.scalar.activation(a_hi3[:, i, :], ps[4][:, 0:S], ACT.Copy).then_inc(LA["ohi"], 1)
            for j in range(4):
                split(T_WO + j + 4)

            r_r, r_s = wk(6144, 512), [wk(2048 + 512 * m, 512) for m in range(2)]

            def relu(n, base):
                g = RELU[n]

                def step(j, par):
                    f = j * 2 + (base - 1) if j.c else Aff(base)
                    act.wait_ge(w_used, val(f + 1))
                    nc.scalar.activation(r_r, ps[par][:, :], ACT.Relu).then_inc(g["relu"], 1)
                    split(f + 4)
                    act.wait_ge(g["sq"], val(j + 1))
                    nc.scalar.activation(a_hi[:, par * 512:par * 512 + 512], r_s[par], ACT.Copy).then_inc(g["ahi"], 1)
                    if j.c:
                        split(f + 5)

                for j in range(2):
                    step(Aff(j), j % 2)
                with act.Fori(0, 6) as i:
                    for m in range(2):
                        step(Aff(2 + m, i, 2), m)
                for j in range(14, R_STEPS):
                    step(Aff(j), j % 2)
                split(base + 2 * R_STEPS + 3)

            norm("relu0", h, lambda b: mod[:, 40 + b:41 + b], lambda b: mod[:, 32 + b:33 + b])
            relu(0, T_RELU0)

            norm("gm", h, lambda b: mod[:, 24 + b:25 + b], lambda b: mod[:, 16 + b:17 + b])
            gm_v = wk(0, 4096).rearrange("p (t d) -> p t d", t=TT)
            for c in range(4):
                act.wait_ge(w_used, T_GMV + 2 * c + 2)
                for t in range(TT):
                    nc.scalar.activation(gm_v[:, t, 512 * c:512 * c + 512], ps[2 * c + t][:, :], ACT.Gelu,
                                         accum_out=st[:, 48 + 4 * t + c:49 + 4 * t + c]).then_inc(GM["v"], 1)
                split(T_GMV + 2 * c + 4)
                split(T_GMV + 2 * c + 5)
            for t in range(TT):
                act.wait_ge(GM["mu"], 1)
                for c in range(4):
                    junk = ps[4 + c][:, :] if t else acc[:, 3 + c // 2, 512 * (c % 2):512 * (c % 2) + 512]
                    nc.scalar.activation(junk, gm_v[:, t, 512 * c:512 * c + 512], ACT.Square,
                                         bias=st[:, 58 + t:59 + t], accum_out=st[:, 64 + 4 * t + c:65 + 4 * t + c])\
                        .then_inc(GM["sq"], 1)
            gm_u = wk(6144, 512)
            gm_t = [acc[:, 4, 512 * m:512 * m + 512] for m in range(2)]

            def gm_step(j, par):
                f = j * 2 + (T_GM - 1) if j.c else Aff(T_GM)
                act.wait_ge(w_used, val(f + 1))
                nc.scalar.activation(gm_u, ps[par][:, :], ACT.Gelu).then_inc(GM["u"], 1)
                split(f + 4)
                act.wait_ge(GM["prod"], val(j + 1))
                nc.scalar.activation(a_hi[:, par * 512:par * 512 + 512], gm_t[par], ACT.Copy).then_inc(GM["ahi"], 1)
                if j.c:
                    split(f + 5)

            act.wait_ge(GM["ws"], 2)
            for j in range(2):
                gm_step(Aff(j), j % 2)
            with act.Fori(0, 2) as i:
                for m in range(2):
                    gm_step(Aff(2 + m, i, 2), m)
            for j in range(6, GM_STEPS):
                gm_step(Aff(j), j % 2)
            split(T_GM + 2 * GM_STEPS + 3)

            norm("relu1", h, lambda b: mod[:, 40 + b:41 + b], lambda b: mod[:, 32 + b:33 + b])
            relu(1, T_RELU1)

        ev_c = wk(6144, 512).rearrange("p (b t) -> p b t", b=2)
        ev_cv = wk(2048, 2 * 258).rearrange("p (b t) -> p b t", b=2)
        ev_a = wk(6656, 512)
        ev_y = wk(0, 512)
        ev_u = wk(2564, 4 * 272).rearrange("p (g t) -> p g t", g=4)
        ev_s0 = wk(4096, 4 * 272).rearrange("p (g t) -> p g t", g=4)
        ev_s1 = wk(5184, 3 * 272).rearrange("p (g t) -> p g t", g=3)
        ev_p = wk(6144, 1024).rearrange("p (g t) -> p g t", g=4)
        onehot = acc[0:33, 4, 0:511]
        bias_rows = acc[0:8, 4, 512:1023]
        t5_bias = acc[:, 0:3, :].rearrange("p a b -> p (a b)").rearrange("p (h k) -> p h k", h=8)
        flip = acc[:, 3, 512:640]
        f_a0 = wk(6144, 512).rearrange("p (b t) -> p b t", b=2)
        f_s, f_p = wk(6656, 512), wk(2048, 512)
        at_qk = wk(0, 4096).rearrange("p (b t) -> p b t", b=16)
        at_v = wk(4096, 2048).rearrange("p (t d) -> p t d", t=TT)
        at_s = wk(6144, 768).rearrange("p (b k) -> p b k", b=2)
        at_pt = wk(6912, 384)
        at_l = acc[:, 3, 0:512].rearrange("p (b t q) -> p b t q", b=2, t=TT)
        ctxt = wk(2048, 2048).rearrange("p (t d) -> p t d", t=TT)
        kva = wk(6144, KT * (KVL + ROPE)).rearrange("p (t d) -> p t d", t=KT)
        cq = wk(2048, TT * QL).rearrange("p (t d) -> p t d", t=TT)
        lf_kv, lf_q = wk(4096, 1024), wk(5120, 768)
        la_kta = [wk(512 * p, 512) for p in range(2)]
        la_ktb = [wk(1024 + 512 * p, 512) for p in range(2)]
        la_qt = [wk(2048 + 512 * p, 512) for p in range(2)]
        la_v = [wk(3072 + 512 * p, 512).rearrange("p (t d) -> p t d", t=KT) for p in range(2)]
        la_p = wk(4096, 1024).rearrange("p (t k) -> p t k", t=TT)
        la_pt = wk(5120, 1024)
        la_kn = wk(6144, KT * QKD).rearrange("p (t d) -> p t d", t=KT)
        la_qn = wk(6912, TT * QKD).rearrange("p (t d) -> p t d", t=TT)
        la_kpe = acc[:, 2, 0:KT * ROPE].rearrange("p (t d) -> p t d", t=KT)
        la_rot = acc[:, 2, 256:256 + TT * ROPE].rearrange("p (t d) -> p t d", t=TT)
        r_r, r_s = wk(6144, 512), [wk(2048 + 512 * m, 512) for m in range(2)]
        gm_v = wk(0, 4096).rearrange("p (t d) -> p t d", t=TT)
        gm_bs, gm_wst, gm_ws = wk(4096, 1024), wk(5120, 1024), wk(6144, 1024)
        gm_u = wk(6144, 512)
        gm_t = [acc[:, 4, 512 * m:512 * m + 512] for m in range(2)]
        gm_vs = acc[:, 3, 0:512].rearrange("p (t c) -> p t c", t=TT)
        SEG = [(0, P), (P, 3 * P)]

        @block.vector
        def _(dve):
            steps = [0]

            def chain(ins):
                steps[0] += 1
                ins.then_inc(dve_step, 1)
                dve.wait_ge(dve_step, steps[0])

            def split(t):
                t = t if isinstance(t, Aff) else Aff(t)
                if t.c >= N_TILES:
                    return
                s, w = t.c % SLOTS, width[t.c]
                dve.wait_ge(hi_done, val(t + 1))
                nc.vector.tensor_tensor(w_lo[s][:, 0:w], raw[s][:, 0:w], w_hi[s][:, 0:w].bitcast(F32), ALU.subtract)\
                    .then_inc(lo_done, 1)

            def norm(name, src):
                k = NORM[name]
                dve.wait_ge(rstd_ready, RSTD[name] + 1)
                for t in range(TT):
                    nc.vector.tensor_scalar(hs[:, t, :], src[:, t, :], rstd[:, 2 * k + t:2 * k + t + 1], None, ALU.mult)\
                        .then_inc(hs_ready, 1)
                for i in range(4):
                    dve.wait_ge(xf_ready, 4 * k + i + 1)
                    nc.vector.tensor_copy(xn_hi3[:, 2 * i:2 * i + 2, :], xf[:, 2 * i:2 * i + 2, :]).then_inc(xhi_done, 1)
                    dve.wait_ge(xhi_done, 4 * k + i + 1)
                    nc.vector.tensor_tensor(xn_lo3[:, 2 * i:2 * i + 2, :], xf[:, 2 * i:2 * i + 2, :],
                                            xn_hi3[:, 2 * i:2 * i + 2, :].bitcast(F32), ALU.subtract).then_inc(xn_ready, 1)

            def residual(last, gate=None):
                dve.wait_ge(w_used, last + 1)
                for t in range(TT):
                    for c in range(2):
                        hv = h[:, t, 512 * c:512 * c + 512]
                        part = ps[4 + 2 * t + c][:, :]
                        if gate is not None:
                            tmp = wk(6144 + 512 * c, 512)
                            chain(nc.vector.tensor_tensor(tmp, part, gate[:, 512 * c:512 * c + 512], ALU.mult))
                            part = tmp
                        add = nc.vector.tensor_tensor(hv, part, hv, ALU.add)
                    add.then_inc(h_ready, 1)

            def ada(s, slot, kb, also=None):
                s = s if isinstance(s, Aff) else Aff(s)
                tile = side[:, s.c % SLOTS, :]
                dve.wait_ge(side_full[s.c % SLOTS], val(Aff(16 * (s.c // SLOTS + 1), s.reg, s.k * 4)))
                if also is not None:
                    nc.vector.scalar_tensor_tensor(acc[:, also, :], tile, cs[:, bass.ds(val(kb + 8), 1)], acc[:, also, :],
                                                   ALU.mult, ALU.add)
                nc.vector.scalar_tensor_tensor(acc[:, slot, :], tile, cs[:, bass.ds(val(kb), 1)], acc[:, slot, :],
                                               ALU.mult, ALU.add).then_inc(side_used, 1)

            def bias_cols(layer, comp):
                c = ROW["ada_b_2"] + 48 * layer + 8 * comp
                return vec[:, c:c + 8]

            def shift_cols(dst, bank_col, layer, comp):
                return nc.vector.tensor_tensor(mod[:, dst:dst + 8], ps[3][:, bank_col:bank_col + 8], bias_cols(layer, comp), ALU.add)

            def gain_cols(dst, bank_col, layer, comp, g):
                chain(shift_cols(dst, bank_col, layer, comp))
                return nc.vector.scalar_tensor_tensor(mod[:, dst:dst + 8], mod[:, dst:dst + 8], 1.0, g, ALU.add, ALU.mult)

            def gate_rows(slot, banks, unit):
                dve.wait_ge(side_full[unit % SLOTS], 16 * (unit // SLOTS + 1))
                for c in range(2):
                    last = nc.vector.tensor_tensor(acc[:, slot, 512 * c:512 * c + 512], ps[banks[c]][:, :],
                                                   side[:, unit % SLOTS, 512 * c:512 * c + 512], ALU.add)
                last.then_inc(side_used, 1)

            dve.wait_ge(vec_ps, 1)
            nc.vector.tensor_copy(vec[:, 0:N_ROWS], ps[0][:, 0:N_ROWS]).then_inc(vec_ready, 1)
            dve.wait_ge(rows_ps, 1)
            nc.vector.tensor_copy(bias_rows, ps[1][0:8, 0:511]).then_inc(rows_sb, 1)
            for t in range(SLOTS):
                split(t)
            nc.vector.memset(ev_cv[:, :, 0:2], 0.0)
            nc.vector.memset(ev_u[:, :, 0:16], 0.0).then_inc(EV["pin"], 1)
            dve.wait_ge(EV["pin"], 1)
            dve.wait_ge(in_h, 16)
            norm("ev", h)

            for m in range(2):
                t = T_EV + 3 * m
                dve.wait_ge(EV["gate"], m + 1)
                dve.wait_ge(w_used, t + 2)
                nc.vector.tensor_tensor(ev_cv[:, :, 2:258], ps[(3 * m + 1) % 4][:, :].rearrange("p (b t) -> p b t", b=2),
                                        ev_c, ALU.mult).then_inc(EV["prod"], 1)
                split(t + 4)
                dve.wait_ge(EV["tap2"], 2 * m + 2)
                for tap, done in ((1, EV["tap1"]), (0, EV["conv"])):
                    for b in range(2):
                        av = ev_a[:, b * S:b * S + S]
                        nc.vector.scalar_tensor_tensor(av, ev_cv[:, b, tap:tap + S], col("ev_conv_w", 4 * tap + 2 * m + b),
                                                       av, ALU.mult, ALU.add).then_inc(done, 1)
                    dve.wait_ge(done, 2 * m + 2)
                split(t + 5)
                dve.wait_ge(w_used, t + 3)
                nc.vector.tensor_tensor(ev_y, ps[(3 * m + 2) % 4][:, :], ev_a, ALU.mult).then_inc(EV["y"], 1)
                split(t + 6)
                dve.wait_ge(EV["yhi"], m + 1)
                c = slice(512 * m, 512 * m + 512)
                nc.vector.tensor_tensor(a_lo[:, c], ev_y, a_hi[:, c].bitcast(F32), ALU.subtract).then_inc(EV["a_ready"], 1)
            dve.wait_ge(EV["pool"], 2)
            split(T_EV + 10)
            split(T_EV + 11)
            chain(nc.vector.tensor_tensor(ev_s0[:, :, 1:272], ev_u[:, :, 1:272], ev_u[:, :, 0:271], ALU.add))
            chain(nc.vector.tensor_tensor(ev_s1[:, :, 3:272], ev_s0[:, 1:4, 3:272], ev_s0[:, 1:4, 1:270], ALU.add))
            chain(nc.vector.tensor_tensor(ev_s0[:, 2:4, 7:272], ev_s1[:, 1:3, 7:272], ev_s1[:, 1:3, 3:268], ALU.add))
            chain(nc.vector.tensor_tensor(ev_s1[:, 2, 15:272], ev_s0[:, 3, 15:272], ev_s0[:, 3, 7:264], ALU.add))
            sums = [ev_s0[:, 0, :], ev_s1[:, 0, :], ev_s0[:, 2, :], ev_s1[:, 2, :]]
            for g in range(4):
                nc.vector.tensor_tensor(ev_p[:, g, 0:16], sums[g][:, 16:32], pool_tab[:, g, :], ALU.mult)
                chain(nc.vector.scalar_tensor_tensor(ev_p[:, g, 16:S], sums[g][:, 32:272], 1.0 / (2 << g),
                                                     ev_u[:, g, 32:272], ALU.mult, ALU.subtract))
            nc.vector.tensor_tensor(ev_p[:, :, 0:16], ev_p[:, :, 0:16], ev_u[:, :, 16:32], ALU.subtract).then_inc(EV["pool_ready"], 1)
            split(T_EVO + 4)
            dve.wait_ge(EV["phi"], 1)
            nc.vector.tensor_tensor(a_lo[:, 1024:2048], wk(6144, 1024), a_hi[:, 1024:2048].bitcast(F32), ALU.subtract)\
                .then_inc(EV["a_ready"], 1)
            split(T_EVO + 5)
            split(T_POOL + 4)
            dve.wait_ge(EV["ybhi"], 1)
            nc.vector.tensor_tensor(a_lo[:, 1024:2048], wk(0, 1024), a_hi[:, 1024:2048].bitcast(F32), ALU.subtract)\
                .then_inc(EV["a_ready"], 1)
            split(T_POOL + 5)
            split(T_POOL + 6)
            residual(T_FFN0 - 1)

            def gated(n, base):
                g = FFN[n]

                def step(j, par, units):
                    u = j * 4 + (base - 2) if j.c else Aff(base)
                    dve.wait_ge(g["a0"], val(j * 2 + 2))
                    for shift, done in ((1, g["tap"]), (2, g["conv"])):
                        for b in range(2):
                            av = f_a0[:, b, shift:S]
                            tap = 2 - shift
                            nc.vector.scalar_tensor_tensor(av, ps[0][:, b * S:b * S + S - shift],
                                                           vcol("ffn_conv_w", j * 2 + (n * 3 * FFB + tap * FFB + b)),
                                                           av, ALU.mult, ALU.add).then_inc(done, 1)
                        if shift == 1:
                            dve.wait_ge(done, val(j * 2 + 2))
                    split(u + 4)
                    dve.wait_ge(g["silu"], val(j + 1))
                    dve.wait_ge(w_used, val(u + 2))
                    nc.vector.tensor_tensor(f_p, ps[1][:, :], f_s, ALU.mult).then_inc(g["prod"], 1)
                    split(u + 5)
                    dve.wait_ge(g["ahi"], val(j + 1))
                    c = slice(par * 512, par * 512 + 512)
                    nc.vector.tensor_tensor(a_lo[:, c], f_p, a_hi[:, c].bitcast(F32), ALU.subtract).then_inc(g["a_ready"], 1)
                    if units:
                        kb = j - LOOP0
                        if n == 0:
                            ada(kb * 2 + U_FFN0, 0, kb, 2)
                            ada(kb * 2 + (U_FFN0 + 1), 1, kb, 3)
                        else:
                            for c in range(4):
                                ada(kb * 4 + (U_FFN1 + c), c, kb)
                    if j.c:
                        split(u + 6)
                        split(u + 7)

                for j in range(LOOP0):
                    step(Aff(j), j % 2, False)
                dve.wait_ge(acc_zero, n + 1)
                dve.wait_ge(cs_ready, 1)
                with dve.Fori(0, TRIPS) as i:
                    for m in range(2):
                        step(Aff(LOOP0 + m, i, 2), m, True)
                for j in range(LOOP1, G_STEPS):
                    step(Aff(j), j % 2, False)
                split(base + 4 * G_STEPS + 2)
                split(base + 4 * G_STEPS + 3)
                residual(base + 4 * G_STEPS - 1)

            norm("ffn0", h)
            gated(0, T_FFN0)
            dve.wait_ge(ada_ps, 1)
            g_mix = vec[:, ROW["norm_mix_g_2"]:ROW["norm_mix_g_2"] + 8]
            shift_cols(0, 16, 0, 0)
            gain_cols(8, 24, 0, 1, g_mix)
            shift_cols(16, 0, 0, 0)
            gain_cols(24, 8, 0, 1, g_mix).then_inc(mod_ready, 1)

            norm("od", h)
            dve.wait_ge(in_small, 16 * 5)
            dve.wait_ge(AT["z_ps"], 1)
            for t in range(TT):
                nc.vector.tensor_tensor(zf[:, 0, 8 * t:8 * t + 8], ps[7][:, 8 * t:8 * t + 8], bf[:, :], ALU.add).then_inc(AT["z"], 1)
            dve.wait_ge(AT["z"], 2)
            chain(nc.vector.tensor_scalar(zf[:, 2, :], zf[:, 0, :], 0.0, None, ALU.min))
            nc.vector.scalar_tensor_tensor(zf[:, 1, :], zf[:, 2, :], 2.0, zf[:, 0, :], ALU.mult, ALU.subtract).then_inc(AT["nabs"], 1)
            dve.wait_ge(AT["ln"], 1)
            nc.vector.tensor_tensor(zf[:, 3, :], zf[:, 1, :], zf[:, 2, :], ALU.subtract).then_inc(AT["neg"], 1)
            for j in range(8):
                split(T_QK + j + 4)
            dve.wait_ge(AT["f_ps"], 1)
            nc.vector.tensor_scalar(zf[:, 4, :], ps[6][:, 0:16], -1.0, None, ALU.mult).then_inc(AT["f"], 1)
            for j in range(4):
                split(T_V + j + 4)
            for t in range(TT):
                for c in range(2):
                    dve.wait_ge(w_used, T_V + 4)
                    nc.vector.tensor_copy(at_v[:, t, 512 * c:512 * c + 512], ps[4 + 2 * t + c][:, :]).then_inc(AT["v_sb"], 1)

            def at_decay(i):
                dve.wait_ge(AT["neg"], 1)
                for t in range(TT):
                    nc.vector.tensor_scalar(at_l[:, i % 2, t, :], ones, zf[:, 3, 8 * t + i:8 * t + i + 1], None, ALU.mult)\
                        .then_inc(AT["lbc"], 1)

            def at_scores(i):
                dve.wait_ge(AT["s_ps"], i + 1)
                s, bank = at_s[:, i % 2, :], ps[i % 2]
                if i < FOX:
                    if i == 0:
                        dve.wait_ge(AT["f"], 1)
                    f = [zf[:, 4, 8 * t + i:8 * t + i + 1] for t in range(TT)]
                    nc.vector.scalar_tensor_tensor(s[:, 0:P], bank[:, 0:P], f[0], causal, ALU.add, ALU.add).then_inc(AT["s_sb"], 1)
                    nc.vector.tensor_scalar(s[:, P:2 * P], bank[:, P:2 * P], f[1], None, ALU.add).then_inc(AT["s_sb"], 1)
                    nc.vector.scalar_tensor_tensor(s[:, 2 * P:3 * P], bank[:, 2 * P:3 * P], f[1], causal, ALU.add, ALU.add)\
                        .then_inc(AT["s_sb"], 1)
                    dve.wait_ge(AT["s_sb"], 3 * i + 3)
                else:
                    s = bank
                for t, (c0, c1) in enumerate(SEG):
                    c = 32 + 4 * (i % 2) + t
                    nc.vector.tensor_reduce(st[:, c:c + 1], s[:, c0:c1], AX.X, ALU.max, negate=True).then_inc(AT["max"], 1)

            at_decay(0)
            at_decay(1)
            at_scores(0)
            for i in range(HEADS):
                dve.wait_ge(AT["exp"], 2 * i + 2)
                c = 34 + 4 * (i % 2)
                nc.vector.reciprocal(st[:, 40:42], st[:, c:c + 2]).then_inc(AT["rec"], 1)
                dve.wait_ge(AT["rec"], i + 1)
                for t, (c0, c1) in enumerate(SEG):
                    nc.vector.tensor_scalar(at_s[:, i % 2, c0:c1], at_s[:, i % 2, c0:c1], st[:, 40 + t:41 + t], None, ALU.mult)\
                        .then_inc(AT["p"], 1)
                if i + 2 < FOX:
                    at_decay(i + 2)
                if i + 1 < HEADS:
                    at_scores(i + 1)
                dve.wait_ge(AT["ohi"], i + 1)
                r = HD * (i % 2)
                nc.vector.tensor_tensor(a_lo3[r:r + HD, i // 2, :], ps[4 + i % 2][r:r + HD, 0:S],
                                        a_hi3[r:r + HD, i // 2, :].bitcast(F32), ALU.subtract).then_inc(AT["a_ready"], 1)
            for j in range(4):
                split(T_ODO + j + 4)
            residual(T_FFN1 - 1)

            norm("ffn1", h)
            gated(1, T_FFN1)

            dve.wait_ge(rstd_ready, RSTD["final"] + 1)
            dve.wait_ge(side_full[U_BC1 % SLOTS], 16 * (U_BC1 // SLOTS + 1))
            for t in range(TT):
                nc.vector.scalar_tensor_tensor(h[:, t, :], h[:, t, :], rstd[:, 18 + t:19 + t], side[:, U_BC1 % SLOTS, :],
                                               ALU.mult, ALU.mult).then_inc(h_ready, 1)
            dve.wait_ge(ada_ps, 2)
            g_ffn = vec[:, ROW["norm_ffn_g_2"]:ROW["norm_ffn_g_2"] + 8]
            shift_cols(32, 0, 0, 3).then_inc(side_used, 1)
            gain_cols(40, 8, 0, 4, g_ffn).then_inc(mod_ready, 1)
            gate_rows(0, (0, 1), U_BC1 + 1)
            gate_rows(4, (4, 5), U_BC1 + 2)

            norm("ctx", ctxt)
            norm("lat", h)
            split(T_LA + 4)
            split(T_LA + 5)
            split(T_LA + 6)
            split(T_LA + 7)
            dve.wait_ge(LA["kv_sb"], 4)
            chain(nc.vector.tensor_tensor(la_kpe, kva[:, :, KVL:], pe_g[:, 1:2, :].to_broadcast([P, KT, ROPE]), ALU.mult))

            def turn(x):
                v = [y.rearrange("p t (a s c) -> p t a s c", a=2, s=2) for y in (x, la_rot, sin)]
                for s in range(2):
                    last = nc.vector.tensor_tensor(v[1][:, :, :, s, :], v[0][:, :, :, 1 - s, :], v[2][:, :, :, s, :], ALU.mult)
                chain(last)
                chain(nc.vector.tensor_tensor(x, x, cos, ALU.mult))
                return nc.vector.tensor_tensor(x, x, la_rot, ALU.add)

            chain(turn(la_kpe[:, TT:KT, :]))
            dve.wait_ge(LA["lrstd"], 1)
            for t in range(KT):
                nc.vector.tensor_scalar(kva[:, t, 0:KVL], kva[:, t, 0:KVL], rstd[:, 20 + t:21 + t], None, ALU.mult)\
                    .then_inc(LA["lscaled"], 1)
            for t in range(TT):
                nc.vector.tensor_scalar(cq[:, t, :], cq[:, t, :], rstd[:, 24 + t:25 + t], None, ALU.mult).then_inc(LA["lscaled"], 1)
            dve.wait_ge(LA["lxf"], 5)
            nc.vector.tensor_copy(xn_hi[:, 0:1024], lf_kv).then_inc(LA["lhi"], 1)
            nc.vector.tensor_copy(xn_hi[:, 1024:1792], lf_q).then_inc(LA["lhi"], 1)
            dve.wait_ge(LA["lhi"], 2)
            nc.vector.tensor_tensor(xn_lo[:, 0:1024], lf_kv, xn_hi[:, 0:1024].bitcast(F32), ALU.subtract).then_inc(LA["l_ready"], 1)
            nc.vector.tensor_tensor(xn_lo[:, 1024:1792], lf_q, xn_hi[:, 1024:1792].bitcast(F32), ALU.subtract)\
                .then_inc(LA["l_ready"], 1)

            def la_normed(i):
                dve.wait_ge(LA["a_rstd"], i + 1)
                for m in range(2):
                    kv2 = ps[m][:, :].rearrange("p (t d) -> p t d", t=2)
                    r = rstd[:, 28 + 2 * m:30 + 2 * m].unsqueeze(2).to_broadcast([P, 2, NOPE])
                    nc.vector.tensor_tensor(la_kn[:, 2 * m:2 * m + 2, 0:NOPE], kv2[:, :, 0:NOPE], r, ALU.mult)
                nc.vector.tensor_tensor(la_kn[:, :, NOPE:], la_kpe, rstd[:, 28:32].unsqueeze(2).to_broadcast([P, KT, ROPE]),
                                        ALU.mult).then_inc(LA["kn"], 1)
                for t in range(TT):
                    last = nc.vector.tensor_scalar(la_qn[:, t, :], ps[2][:, QKD * t:QKD * t + QKD], rstd[:, 32 + t:33 + t],
                                                   None, ALU.mult)
                chain(last)
                qpe = la_qn[:, :, NOPE:]
                chain(nc.vector.tensor_tensor(qpe, qpe, pe_g[:, 0:1, :].to_broadcast([P, TT, ROPE]), ALU.mult))
                turn(qpe).then_inc(LA["qpe"], 1)
                split(T_HEAD + i + 4)

            la_normed(0)
            for i in range(MH):
                dve.wait_ge(LA["s_ps"], i + 1)
                for t in range(TT):
                    last = nc.vector.tensor_reduce(st[:, 80 + t:81 + t], ps[4 + t][:, :], AX.X, ALU.max, negate=True)
                chain(last)
                nc.vector.tensor_scalar(st[:, 82:84], st[:, 80:82], QKD ** -0.5, None, ALU.mult).then_inc(LA["max"], 1)
                if i + 1 < MH:
                    la_normed(i + 1)
                dve.wait_ge(LA["exp"], 2 * i + 2)
                nc.vector.reciprocal(st[:, 86:88], st[:, 84:86]).then_inc(LA["rec"], 1)
                dve.wait_ge(LA["rec"], i + 1)
                for t in range(TT):
                    nc.vector.tensor_scalar(la_p[:, t, :], la_p[:, t, :], st[:, 86 + t:87 + t], None, ALU.mult).then_inc(LA["p"], 1)
                dve.wait_ge(LA["t_ps"], i + 1)
                nc.vector.tensor_copy(la_pt[:, 512:1024], ps[7][:, :]).then_inc(LA["pt_d"], 1)
                dve.wait_ge(LA["ohi"], i + 1)
                nc.vector.tensor_tensor(a_lo3[:, i, :], ps[4][:, 0:S], a_hi3[:, i, :].bitcast(F32), ALU.subtract)\
                    .then_inc(LA["a_ready"], 1)
            for j in range(4):
                split(T_WO + j + 4)
            residual(T_RELU0 - 1, acc[:, 0, :])

            def relu(n, base):
                g = RELU[n]

                def step(j, par, units):
                    f = j * 2 + (base - 1) if j.c else Aff(base)
                    dve.wait_ge(g["relu"], val(j + 1))
                    nc.vector.tensor_tensor(r_s[par], r_r, r_r, ALU.mult).then_inc(g["sq"], 1)
                    split(f + 4)
                    dve.wait_ge(g["ahi"], val(j + 1))
                    c = slice(par * 512, par * 512 + 512)
                    nc.vector.tensor_tensor(a_lo[:, c], r_s[par], a_hi[:, c].bitcast(F32), ALU.subtract).then_inc(g["a_ready"], 1)
                    if units:
                        kb = j - 2
                        for c in range(4):
                            ada(kb * 4 + (U_RELU0 + c), c, kb)
                    if j.c:
                        split(f + 5)

                for j in range(2):
                    step(Aff(j), j % 2, False)
                if n == 0:
                    dve.wait_ge(acc_zero, 3)
                with dve.Fori(0, 4) as i:
                    for m in range(2):
                        step(Aff(2 + m, i, 2), m, n == 0)
                with dve.Fori(0, 2) as i:
                    for m in range(2):
                        step(Aff(10 + m, i, 2), m, False)
                for j in range(14, R_STEPS):
                    step(Aff(j), j % 2, False)
                split(base + 2 * R_STEPS + 3)

            norm("relu0", h)
            relu(0, T_RELU0)
            residual(T_GMV - 1, acc[:, 4, :])
            dve.wait_ge(ada_ps, 3)
            g_mix1 = vec[:, ROW["norm_mix_g_2"] + 8:ROW["norm_mix_g_2"] + 16]
            g_ffn1 = vec[:, ROW["norm_ffn_g_2"] + 8:ROW["norm_ffn_g_2"] + 16]
            shift_cols(16, 0, 1, 0)
            shift_cols(32, 16, 1, 3)
            gate_rows(2, (0, 1), U_BC2)
            gain_cols(24, 8, 1, 1, g_mix1).then_inc(mod_ready, 1)

            norm("gm", h)
            dve.wait_ge(GM["ws_ps"], 1)
            for c in range(2):
                nc.vector.tensor_copy(gm_wst[:, 512 * c:512 * c + 512], ps[c][:, :]).then_inc(GM["ws"], 1)
            for j in range(8):
                split(T_GMV + j + 4)
            dve.wait_ge(GM["v"], 8)
            chain(nc.vector.tensor_reduce(st[:, 56:58], st[:, 48:56].rearrange("p (t c) -> p t c", t=TT), AX.X, ALU.add))
            nc.vector.tensor_scalar(st[:, 58:60], st[:, 56:58], -1.0 / GMH, None, ALU.mult).then_inc(GM["mu"], 1)
            dve.wait_ge(GM["mu"], 1)
            dve.wait_ge(GM["sq"], 8)
            nc.vector.tensor_reduce(st[:, 60:62], st[:, 64:72].rearrange("p (t c) -> p t c", t=TT), AX.X, ALU.add)\
                .then_inc(GM["norm"], 1)
            dve.wait_ge(GM["rstd"], 1)
            for t in range(TT):
                last = nc.vector.tensor_scalar(gm_v[:, t, :], gm_v[:, t, :], st[:, 58 + t:59 + t], rstd[:, 36 + t:37 + t],
                                               ALU.add, ALU.mult)
            chain(last)
            for op, u0 in ((ALU.mult, U_BC2 + 1), (ALU.add, U_BC2 + 3)):
                for c in range(2):
                    u = u0 + c
                    dve.wait_ge(side_full[u % SLOTS], 16 * (u // SLOTS + 1))
                    for t in range(TT):
                        vv = gm_v[:, t, 1024 * c:1024 * c + 1024]
                        last = nc.vector.tensor_tensor(vv, vv, side[:, u % SLOTS, :], op)
                    last.then_inc(side_used, 1)
                    dve.wait_ge(side_used, u + 1)

            def gm_slice(j):
                return nc.vector.tensor_copy(gm_vs, gm_v[:, :, bass.ds(val(j * 256), 256)]).then_inc(GM["vs"], 1)

            def gm_step(j, par, more=True):
                f = j * 2 + (T_GM - 1) if j.c else Aff(T_GM)
                dve.wait_ge(GM["m_ps"], val(j + 1))
                nc.vector.tensor_tensor(gm_t[par].rearrange("p (b q) -> p b q", b=4), ps[2 + par][:, :].rearrange("p (b q) -> p b q", b=4),
                                        gm_bs[:, bass.ds(val(j * P), P)].unsqueeze(1).to_broadcast([P, 4, P]), ALU.add)\
                    .then_inc(GM["t"], 1)
                if more:
                    gm_slice(j + 1)
                split(f + 4)
                dve.wait_ge(GM["t"], val(j + 1))
                dve.wait_ge(GM["u"], val(j + 1))
                nc.vector.tensor_tensor(gm_t[par], gm_t[par], gm_u, ALU.mult).then_inc(GM["prod"], 1)
                dve.wait_ge(GM["ahi"], val(j + 1))
                c = slice(par * 512, par * 512 + 512)
                nc.vector.tensor_tensor(a_lo[:, c], gm_t[par], a_hi[:, c].bitcast(F32), ALU.subtract).then_inc(GM["a_ready"], 1)
                for c in range(2):
                    ada(j * 2 + (U_GM + c), c, j)
                if j.c:
                    split(f + 5)

            gm_slice(Aff(0))
            dve.wait_ge(GM["bs_in"], 16)
            dve.wait_ge(acc_zero, 4)
            for j in range(2):
                gm_step(Aff(j), j % 2)
            with dve.Fori(0, 2) as i:
                for m in range(2):
                    gm_step(Aff(2 + m, i, 2), m)
            for j in range(6, GM_STEPS):
                gm_step(Aff(j), j % 2, j + 1 < GM_STEPS)
            split(T_GM + 2 * GM_STEPS + 3)
            residual(T_RELU1 - 1, acc[:, 2, :])
            dve.wait_ge(ada_ps, 4)
            gate_rows(1, (0, 1), U_BC3)
            gain_cols(40, 0, 1, 4, g_ffn1).then_inc(mod_ready, 1)
            norm("relu1", h)
            relu(1, T_RELU1)
            residual(N_TILES - 1, acc[:, 1, :])

        @block.tensor
        def _(pe):
            def parts(s, c, n):
                return w_hi[s][:, c:c + n], w_lo[s][:, c:c + n]

            def f_tile(t, bank):
                t = t if isinstance(t, Aff) else Aff(t)
                pe.wait_ge(lo_done, val(t + 1))
                for b in range(2):
                    o = ps[bank][:, b * S:b * S + S]
                    for k in range(KB):
                        hi, lo = parts(t.c % SLOTS, k * 256 + b * P, P)
                        nc.tensor.matmul(o, hi, xn_hi3[:, k, :], start=k == 0, stop=False)
                        nc.tensor.matmul(o, hi, xn_lo3[:, k, :], start=False, stop=False)
                        last = nc.tensor.matmul(o, lo, xn_hi3[:, k, :], start=False, stop=k == KB - 1)
                last.then_inc(w_used, 1)

            def t_tile(t, blocks, first, last, x=(a_hi3, a_lo3), free=True, bank0=4, n=D, done=None):
                t = t if isinstance(t, Aff) else Aff(t)
                pe.wait_ge(lo_done, val(t + 1))
                cuts = [(c, min(512, n - c)) for c in range(0, n, 512)]
                for m, k in enumerate(blocks):
                    for tt in range(TT):
                        xh, xl = (y[:, k, tt * P:tt * P + P] for y in x)
                        begin, end = first and m == 0, last and m == len(blocks) - 1
                        for x_part, w_part in ((xh, 0), (xh, 1), (xl, 0)):
                            for c, (c0, cn) in enumerate(cuts):
                                w = parts(t.c % SLOTS, m * n + c0, cn)[w_part]
                                o = ps[bank0 + len(cuts) * tt + c][:, 0:cn]
                                ins = nc.tensor.matmul(o, x_part, w, start=begin and x_part is xh and w_part == 0,
                                                       stop=end and x_part is xl)
                if free:
                    ins.then_inc(w_used, 1)
                elif done is not None:
                    ins.then_inc(done, 1)

            def norm(name):
                k = NORM[name]
                pe.wait_ge(hs_ready, 2 * k + 2)
                for i in range(4):
                    for m in range(2):
                        for t in range(TT):
                            b = 2 * i + m
                            last = nc.tensor.transpose(ps[i][:, m * S + t * P:m * S + t * P + P], hs[:, t, b * P:b * P + P], ident)
                    last.then_inc(xt_ps, 1)
                pe.wait_ge(xn_ready, 4 * k + 4)

            def columns(slot, c0):
                for b in range(8):
                    last = nc.tensor.matmul(ps[3][:, c0 + b:c0 + b + 1], acc[:, slot, b * P:b * P + P], ones[:, 0:1],
                                            start=True, stop=True)
                return last

            def rows(slot, banks):
                for c in range(2):
                    last = nc.tensor.matmul(ps[banks[c]][:, :], ones, acc[:, slot, 512 * c:512 * c + 512], start=True, stop=True)
                return last

            pe.wait_ge(in_cst, 16)
            pe.wait_ge(in_rows, 16 * N_ROW_DMAS)
            stage = wk(6144, ROW_TILES * P).rearrange("p (r c) -> p r c", r=ROW_TILES)
            for r in range(ROW_TILES):
                n = min(P, N_ROWS - r * P)
                last = nc.tensor.transpose(ps[0][:, r * P:r * P + n], stage[0:n, r, :], ident[0:n, 0:n])
            last.then_inc(vec_ps, 1)
            pe.wait_ge(in_small, 16 * 5)
            pe.wait_ge(rb_ready, 16)
            nc.tensor.matmul(ps[1][0:8, 0:511], rel[:, :], onehot, start=True, stop=True).then_inc(rows_ps, 1)
            pe.wait_ge(vec_ready, 1)
            pe.wait_ge(rows_sb, 1)
            norm("ev")

            free = {4: (EV["gate"], 1), 5: (EV["prod"], 1), 6: (EV["y"], 1), 7: (EV["gate"], 2)}
            for m in range(8):
                if m in free:
                    pe.wait_ge(*free[m])
                f_tile(T_EV + m, m % 4)
            for j in range(2):
                pe.wait_ge(EV["a_ready"], j + 1)
                t_tile(T_EVO + j, (2 * j, 2 * j + 1), j == 0, False)
            pe.wait_ge(EV["a_ready"], 3)
            pe.wait_ge(lo_done, T_POOL + 1)
            for g in range(4):
                o = ps[g // 2][:, (g % 2) * S:(g % 2) * S + S]
                hi, lo = parts(T_POOL % SLOTS, g * P, P)
                nc.tensor.matmul(o, hi, a_hi3[:, 4 + g, :], start=True, stop=False)
                nc.tensor.matmul(o, hi, a_lo3[:, 4 + g, :], start=False, stop=False)
                last = nc.tensor.matmul(o, lo, a_hi3[:, 4 + g, :], start=False, stop=True)
            last.then_inc(w_used, 1)
            pe.wait_ge(EV["a_ready"], 4)
            for j in range(2, 4):
                t_tile(T_POOL + j - 1, (2 * j, 2 * j + 1), False, j == 3)

            def gated(n, base):
                g = FFN[n]

                def f_step(j):
                    u = j * 4 + (base - 2) if j.c else Aff(base)
                    if j.c:
                        pe.wait_ge(g["conv"], val(j * 2))
                    f_tile(u, 0)
                    if j.c:
                        pe.wait_ge(g["prod"], val(j))
                    f_tile(u + 1, 1)

                def t_step(j, par, first=False, last=False):
                    pe.wait_ge(g["a_ready"], val(j + 1))
                    w = j * 4 + (base + 4) if j.c < G_STEPS - 1 else Aff(base + 4 * G_STEPS - 2)
                    t_tile(w, (2 * par,), first, False)
                    t_tile(w + 1, (2 * par + 1,), False, last)

                f_step(Aff(0))
                f_step(Aff(1))
                t_step(Aff(0), 0, first=True)
                with pe.Fori(0, TRIPS) as i:
                    for m in range(2):
                        j = Aff(LOOP0 + m, i, 2)
                        f_step(j)
                        t_step(j - 1, 1 - m)
                for j in range(LOOP1, G_STEPS):
                    f_step(Aff(j))
                    t_step(Aff(j - 1), (j - 1) % 2)
                t_step(Aff(G_STEPS - 1), (G_STEPS - 1) % 2, last=True)

            norm("ffn0")
            gated(0, T_FFN0)
            pe.wait_ge(side_used, U_FFN1)
            for c in range(4):
                last = columns(c, 8 * c)
            last.then_inc(ada_ps, 1)

            norm("od")
            for t in range(TT):
                for k in range(KB):
                    last = nc.tensor.matmul(ps[7][:, 8 * t:8 * t + 8], xf[:, k, t * P:t * P + P], wf[:, k, :],
                                            start=k == 0, stop=k == KB - 1)
            last.then_inc(AT["z_ps"], 1)
            for j in range(8):
                if j >= 4:
                    pe.wait_ge(AT["qk"], j - 3)
                f_tile(T_QK + j, j % 4)
            pe.wait_ge(AT["neg"], 1)
            nc.tensor.matmul(ps[6][:, 0:8], tri_ones[:, 0:P], zf[:, 3, 0:8], start=True, stop=True)
            nc.tensor.matmul(ps[6][:, 8:16], ones, zf[:, 3, 0:8], start=True, stop=False)
            nc.tensor.matmul(ps[6][:, 8:16], tri_ones[:, 0:P], zf[:, 3, 8:16], start=False, stop=True).then_inc(AT["f_ps"], 1)
            pe.wait_ge(AT["f"], 1)
            for j in range(4):
                t_tile(T_V + j, (2 * j, 2 * j + 1), j == 0, j == 3, x=(xn_hi3, xn_lo3))

            def at_scores(i):
                r, b, o = HD * (i % 2), i // 2, ps[i % 2]
                fox = i < FOX
                if 2 <= i < FOX + 2:
                    pe.wait_ge(AT["s_sb"], 3 * (i - 2) + 3)
                elif i >= 2:
                    pe.wait_ge(AT["exp"], 2 * (i - 2) + 2)
                if i == FOX:
                    pe.wait_ge(bias_in, 48)
                q, k = at_qk[r:r + HD, b, :], at_qk[r:r + HD, 8 + b, :]
                nc.tensor.matmul(o[:, 0:P], q[:, 0:P], k[:, 0:P], start=True, stop=False)
                if fox:
                    pe.wait_ge(AT["lbc"], 2 * i + 2)
                    nc.tensor.matmul(o[:, 0:P], at_l[:, i % 2, 0, :], tri_ones[:, 0:P], start=False, stop=True)
                else:
                    nc.tensor.matmul(o[:, 0:P], flip, t5_bias[:, i - FOX, 0:P], start=False, stop=True)
                nc.tensor.matmul(o[:, P:3 * P], q[:, P:S], k, start=True, stop=False)
                if fox:
                    nc.tensor.matmul(o[:, P:3 * P], at_l[:, i % 2, 0, :], tri_ones, start=False, stop=False)
                    last = nc.tensor.matmul(o[:, 2 * P:3 * P], at_l[:, i % 2, 1, :], tri_ones[:, 0:P], start=False, stop=True)
                else:
                    last = nc.tensor.matmul(o[:, P:3 * P], flip, t5_bias[:, i - FOX, P:3 * P], start=False, stop=True)
                last.then_inc(AT["s_ps"], 1)

            pe.wait_ge(AT["qk"], 8)
            at_scores(0)
            at_scores(1)
            pe.wait_ge(AT["v_sb"], 4)
            for i in range(HEADS):
                pe.wait_ge(AT["p"], 2 * i + 2)
                pv = at_s[:, i % 2, :]
                for b in range(3):
                    last = nc.tensor.transpose(ps[2 + i % 2][:, b * P:b * P + P], pv[:, b * P:b * P + P], ident)
                last.then_inc(AT["t_ps"], 1)
                if i + 2 < HEADS:
                    at_scores(i + 2)
                pe.wait_ge(AT["pt"], i + 1)
                if i >= 2:
                    pe.wait_ge(AT["a_ready"], i - 1)
                d = slice((i // 2) * P, (i // 2) * P + P)
                o = ps[4 + i % 2]
                nc.tensor.matmul(o[:, 0:S], at_v[:, 0, d], at_pt[:, 0:S], start=True, stop=False)
                nc.tensor.matmul(o[:, P:S], at_v[:, 1, d], at_pt[:, S:3 * P], start=False, stop=True).then_inc(AT["o_ps"], 1)
            pe.wait_ge(AT["a_ready"], HEADS)
            for j in range(4):
                t_tile(T_ODO + j, (2 * j, 2 * j + 1), j == 0, j == 3)

            norm("ffn1")
            gated(1, T_FFN1)
            pe.wait_ge(side_used, U_BC1)
            columns(1, 0)
            columns(2, 8)
            rows(0, (0, 1))
            pe.wait_ge(h_ready, H_READY["final"] + 1)
            rows(3, (4, 5)).then_inc(ada_ps, 1)

            norm("ctx")
            xn = (xn_hi3, xn_lo3)
            pe.wait_ge(lo_done, T_LA + 2)
            t_tile(T_LA, range(4), True, False, x=xn, free=False, bank0=4, n=KVL + ROPE)
            t_tile(T_LA + 1, range(4, 8), False, True, x=xn, free=False, bank0=4, n=KVL + ROPE, done=LA["a_ps"])
            norm("lat")
            t_tile(T_LA, range(4), True, False, x=xn, bank0=6, n=KVL + ROPE)
            t_tile(T_LA + 1, range(4, 8), False, True, x=xn, bank0=6, n=KVL + ROPE)
            pe.wait_ge(LA["kv_sb"], 2)
            t_tile(T_LA + 2, range(4), True, False, x=xn, bank0=4, n=QL)
            t_tile(T_LA + 3, range(4, 8), False, True, x=xn, bank0=4, n=QL)
            pe.wait_ge(LA["lscaled"], 6)
            for b in range(2):
                for t in range(KT):
                    nc.tensor.transpose(ps[b][:, t * P:t * P + P], kva[:, t, b * P:b * P + P], ident)
            for b in range(3):
                for t in range(TT):
                    c = S * (b % 2) + t * P
                    last = nc.tensor.transpose(ps[2 + b // 2][:, c:c + P], cq[:, t, b * P:b * P + P], ident)
            last.then_inc(LA["lt_ps"], 1)
            ckv = [y[:, 0:1024].rearrange("p (k t) -> p k t", k=2) for y in (xn_hi, xn_lo)]
            cqt = [y[:, 1024:1792].rearrange("p (k t) -> p k t", k=3) for y in (xn_hi, xn_lo)]
            pe.wait_ge(LA["l_ready"], 2)

            def la_project(i):
                t = T_HEAD + i
                pe.wait_ge(lo_done, t + 1)
                if i:
                    pe.wait_ge(LA["kq"], i)
                s = t % SLOTS
                for x, nk, tiles, base, n, where in (
                        (ckv, 2, KT, 0, 256, lambda m: ps[m // 2][:, 256 * (m % 2):256 * (m % 2) + 256]),
                        (cqt, 3, TT, 512, QKD, lambda m: ps[2][:, QKD * m:QKD * m + QKD])):
                    for m in range(tiles):
                        for k in range(nk):
                            hi, lo = parts(s, base + k * n, n)
                            xh, xl = (y[:, k, m * P:m * P + P] for y in x)
                            nc.tensor.matmul(where(m), xh, hi, start=k == 0, stop=False)
                            nc.tensor.matmul(where(m), xh, lo, start=False, stop=False)
                            last = nc.tensor.matmul(where(m), xl, hi, start=False, stop=k == nk - 1)
                last.then_inc(w_used, 1)

            def la_transpose(i):
                pe.wait_ge(LA["kn"], i + 1)
                for t in range(KT):
                    nc.tensor.transpose(ps[3][:, t * P:t * P + P], la_kn[:, t, 0:NOPE], ident)
                    nc.tensor.transpose(ps[0][0:ROPE, t * P:t * P + P], la_kn[:, t, NOPE:], ident)
                pe.wait_ge(LA["qpe"], i + 1)
                for t in range(TT):
                    nc.tensor.transpose(ps[1][:, t * P:t * P + P], la_qn[:, t, 0:NOPE], ident)
                    last = nc.tensor.transpose(ps[1][0:ROPE, S + t * P:S + t * P + P], la_qn[:, t, NOPE:], ident)
                last.then_inc(LA["kq_ps"], 1)

            la_project(0)
            la_transpose(0)
            for i in range(MH):
                p = i % 2
                if i + 1 < MH:
                    la_project(i + 1)
                else:
                    pe.wait_ge(LA["kq"], i + 1)
                if i:
                    pe.wait_ge(LA["a_ready"], i)
                for t in range(TT):
                    q = la_qt[p]
                    nc.tensor.matmul(ps[4 + t][:, :], q[:, t * P:t * P + P], la_kta[p], start=True, stop=False)
                    last = nc.tensor.matmul(ps[4 + t][:, :], q[0:ROPE, S + t * P:S + t * P + P], la_ktb[p][0:ROPE, :],
                                            start=False, stop=True)
                last.then_inc(LA["s_ps"], 1)
                if i + 1 < MH:
                    la_transpose(i + 1)
                pe.wait_ge(LA["p"], 2 * i + 2)
                for k in range(KT):
                    for t in range(TT):
                        last = nc.tensor.transpose(ps[6 + k // 2][:, (k % 2) * S + t * P:(k % 2) * S + t * P + P],
                                                   la_p[:, t, k * P:k * P + P], ident)
                last.then_inc(LA["t_ps"], 1)
                pe.wait_ge(LA["pt_a"], i + 1)
                pe.wait_ge(LA["pt_d"], i + 1)
                for k in range(KT):
                    last = nc.tensor.matmul(ps[4][:, 0:S], la_v[p][:, k, :], la_pt[:, k * S:k * S + S],
                                            start=k == 0, stop=k == KT - 1)
                last.then_inc(LA["o_ps"], 1)
            pe.wait_ge(LA["a_ready"], MH)
            for j in range(4):
                t_tile(T_WO + j, (2 * j, 2 * j + 1), j == 0, j == 3)

            def relu(n, base):
                g = RELU[n]

                def f_step(j, par):
                    if j.c >= 2:
                        pe.wait_ge(g["relu"], val(j - 1))
                    f_tile(j * 2 + (base - 1) if j.c else Aff(base), par)

                def t_step(j, par, first=False, last=False):
                    pe.wait_ge(g["a_ready"], val(j + 1))
                    w = j * 2 + (base + 2) if j.c < R_STEPS - 1 else Aff(base + 2 * R_STEPS - 1)
                    t_tile(w, (2 * par, 2 * par + 1), first, last)

                f_step(Aff(0), 0)
                f_step(Aff(1), 1)
                t_step(Aff(0), 0, first=True)
                with pe.Fori(0, 6) as i:
                    for m in range(2):
                        j = Aff(2 + m, i, 2)
                        f_step(j, m)
                        t_step(j - 1, 1 - m)
                for j in range(14, R_STEPS):
                    f_step(Aff(j), j % 2)
                    t_step(Aff(j - 1), (j - 1) % 2)
                t_step(Aff(R_STEPS - 1), 1, last=True)

            norm("relu0")
            relu(0, T_RELU0)
            pe.wait_ge(side_used, U_BC2)
            columns(0, 0)
            columns(1, 8)
            columns(3, 16)
            rows(2, (0, 1)).then_inc(ada_ps, 1)

            norm("gm")
            pe.wait_ge(GM["ws_in"], 16)
            for g in range(8):
                last = nc.tensor.transpose(ps[g // 4][:, (g % 4) * P:(g % 4) * P + P], gm_ws[:, g * P:g * P + P], ident)
            last.then_inc(GM["ws_ps"], 1)
            pe.wait_ge(GM["ws"], 2)
            for c in range(4):
                for m in range(2):
                    t_tile(T_GMV + 2 * c + m, range(4 * m, 4 * m + 4), m == 0, m == 1, x=xn, bank0=2 * c, n=512)

            def gm_f(j, par):
                if j.c == 0:
                    pe.wait_ge(GM["v"], 8)
                if j.c >= 2:
                    pe.wait_ge(GM["u"], val(j - 1))
                f_tile(j * 2 + (T_GM - 1) if j.c else Aff(T_GM), par)
                pe.wait_ge(GM["vs"], val(j + 1))
                if j.c >= 2:
                    pe.wait_ge(GM["t"], val(j - 1))
                for b in range(2):
                    for t in range(TT):
                        c = (2 * b + t) * P
                        last = nc.tensor.matmul(ps[2 + par][:, c:c + P], gm_vs[:, t, b * P:b * P + P],
                                                gm_wst[:, bass.ds(val(j * P), P)], start=True, stop=True)
                last.then_inc(GM["m_ps"], 1)

            def gm_t_step(j, par, first=False, last=False):
                pe.wait_ge(GM["a_ready"], val(j + 1))
                w = j * 2 + (T_GM + 2) if j.c < GM_STEPS - 1 else Aff(T_GM + 2 * GM_STEPS - 1)
                t_tile(w, (2 * par, 2 * par + 1), first, last)

            gm_f(Aff(0), 0)
            gm_f(Aff(1), 1)
            gm_t_step(Aff(0), 0, first=True)
            with pe.Fori(0, 2) as i:
                for m in range(2):
                    j = Aff(2 + m, i, 2)
                    gm_f(j, m)
                    gm_t_step(j - 1, 1 - m)
            for j in range(6, GM_STEPS):
                gm_f(Aff(j), j % 2)
                gm_t_step(Aff(j - 1), (j - 1) % 2)
            gm_t_step(Aff(GM_STEPS - 1), 1, last=True)
            pe.wait_ge(side_used, U_BC3)
            columns(0, 0)
            rows(1, (0, 1)).then_inc(ada_ps, 1)

            norm("relu1")
            relu(1, T_RELU1)

        @block.gpsimd
        def _(pool):
            done = [0]

            def chain(ins):
                done[0] += 1
                ins.then_inc(pool_step, 1)
                pool.wait_ge(pool_step, done[0])

            def root(c0, n, parts):
                at = c0
                for c, m, count in parts:
                    chain(nc.gpsimd.tensor_scalar(rs[:, at:at + m], st[:, c:c + m], 1.0 / count, EPS, ALU.mult, ALU.add))
                    at += m
                return nc.gpsimd.tensor_tensor(rstd[:, c0:c0 + n], rs[:, c0:c0 + n], half[:, 0:n], ALU.pow)

            def row_rstd(name):
                pool.wait_ge(sq_done, 2 * RSTD[name] + 2)
                c = RCOL[name]
                root(c, 2, [(c, 2, D)]).then_inc(rstd_ready, 1)

            def side_load(s, src, free=None):
                s = s if isinstance(s, Aff) else Aff(s)
                if s.c >= SLOTS:
                    pool.wait_ge(side_used, val(s - (SLOTS - 1)) if free is None else free)
                pool.dma_start(side[:, s.c % SLOTS, :], src).then_inc(side_full[s.c % SLOTS], 16)

            def ada_view(layer, comp, kb):
                v = I["ada_w_2"][layer].rearrange("(k p) (c n) -> p k c n", p=P, c=6)
                return v[:, bass.ds(val(kb), 1), comp, :].rearrange("p k n -> p (k n)")

            def side_loop(u0, layer, comp0, n_comp, trips):
                per = SLOTS // n_comp
                with pool.Fori(0, trips) as i:
                    for m in range(SLOTS):
                        s = Aff(u0 + SLOTS + m, i, SLOTS)
                        pool.wait_ge(side_used, val(s - (SLOTS - 1)))
                        kb = pool.snap(val(Aff(per + m // n_comp, i, per)))
                        pool.dma_start(side[:, s.c % SLOTS, :], ada_view(layer, comp0 + m % n_comp, kb))\
                            .then_inc(side_full[s.c % SLOTS], 16)

            def bias_row(layer, comp):
                return I["ada_b_2"][layer, comp * D:comp * D + D].partition_broadcast(P)

            chain(nc.gpsimd.memset(rel[:, :], 1.0))
            pool.dma_start(rel[0:32, :], I["rel_bias"]).then_inc(rb_ready, 16)
            nc.gpsimd.memset(half[:, :], -0.5).then_inc(half_ready, 1)
            pool.dma_start(onehot, I["onehot"]).then_inc(in_small, 16)
            pool.dma_start(bf[:, :], I["od_b_f"][0].partition_broadcast(P)).then_inc(in_small, 16)
            pool.dma_start(wf[:, :, :], I["od_w_in"][0].rearrange("(k p) n -> p k n", p=P)[:, :, 3 * D:3 * D + 8])\
                .then_inc(in_small, 16)
            pool.dma_start(pe_g[:, 0, :], I["mla_q_norm_2"][0, NOPE:QKD].partition_broadcast(P)).then_inc(in_small, 16)
            pool.dma_start(pe_g[:, 1, :], I["mla_k_norm_2"][0, NOPE:QKD].partition_broadcast(P)).then_inc(in_small, 16)
            nc.gpsimd.memset(acc[:, 0:4, :], 0.0).then_inc(acc_zero, 1)
            for s in range(SLOTS):
                side_load(U_FFN0 + s, ada_view(0, s % 2, s // 2))
            pool.wait_ge(half_ready, 1)
            row_rstd("ev")
            pool.wait_ge(rows_sb, 1)
            pool.dma_start(scratch[:, 0:511], bias_rows).then_inc(rows_out, 16)
            row_rstd("ffn0")
            side_loop(U_FFN0, 0, 0, 2, 3)
            pool.wait_ge(rows_out, 16)
            pool.wait_ge(mod_ready, 1)
            pool.dma_start(flip, I["consts"][:, C_ALL:]).then_inc(bias_in, 16)
            for t, (c0, c1) in enumerate(SEG):
                src = bass.AP(scratch.tensor, P - P * t, [[1, P], [512, 8], [1, c1 - c0]])
                pool.dma_start(t5_bias[:, :, c0:c1], src).then_inc(bias_in, 16)
            for c in range(SLOTS):
                side_load(U_FFN1 + c, ada_view(0, 2 + c, 0))
            row_rstd("od")
            pool.wait_ge(AT["a_ready"], HEADS)
            nc.gpsimd.memset(acc[:, 0:4, :], 0.0).then_inc(acc_zero, 1)
            row_rstd("ffn1")
            side_loop(U_FFN1, 0, 2, 4, 7)
            side_load(U_BC1, I["final_norm_g"].partition_broadcast(P))
            side_load(U_BC1 + 1, bias_row(0, 2))
            side_load(U_BC1 + 2, bias_row(0, 5))
            pool.wait_ge(FFN[1]["a_ready"], G_STEPS)
            pool.dma_start(ctxt, I["ctx_2"][0].rearrange("(t p) d -> p t d", p=P)).then_inc(ctx_in, 16)
            row_rstd("final")
            row_rstd("ctx")
            row_rstd("lat")
            pool.wait_ge(LA["lsq"], 10)
            root(20, 6, [(48, 4, KVL), (52, 2, QL)]).then_inc(LA["lrstd"], 1)
            for c in range(SLOTS):
                side_load(U_RELU0 + c, ada_view(1, c, 0))
            for i in range(MH):
                pool.wait_ge(LA["a_sq"], 6 * i + 6)
                chain(nc.gpsimd.tensor_tensor(rs[:, 28:32], st[:, 72:76], st[:, 64:68], ALU.add))
                chain(nc.gpsimd.tensor_scalar(rs[:, 28:32], rs[:, 28:32], 1.0 / QKD, EPS, ALU.mult, ALU.add))
                chain(nc.gpsimd.tensor_scalar(rs[:, 32:34], st[:, 76:78], 1.0 / QKD, EPS, ALU.mult, ALU.add))
                nc.gpsimd.tensor_tensor(rstd[:, 28:34], rs[:, 28:34], half[:, 0:6], ALU.pow).then_inc(LA["a_rstd"], 1)
            row_rstd("relu0")
            pool.wait_ge(h_ready, H_READY["relu0"] + 2)
            nc.gpsimd.memset(acc[:, 0:4, :], 0.0).then_inc(acc_zero, 1)
            side_loop(U_RELU0, 1, 0, 4, 7)
            side_load(U_BC2, bias_row(1, 2))
            for c in range(2):
                side_load(U_BC2 + 1 + c, I["gm_ln_g_2"][0, 1024 * c:1024 * c + 1024].partition_broadcast(P))
            pool.wait_ge(h_ready, H_READY["gm"] + 2)
            pool.dma_start(gm_ws.rearrange("p (g q) -> p g q", g=8), I["gm_ws_2"][0].rearrange("g p q -> p g q")).then_inc(GM["ws_in"], 16)
            row_rstd("gm")
            for c in range(2):
                side_load(U_BC2 + 3 + c, I["gm_ln_b_2"][0, 1024 * c:1024 * c + 1024].partition_broadcast(P))
            pool.wait_ge(mod_ready, 3)
            nc.gpsimd.memset(acc[:, 0:2, :], 0.0).then_inc(acc_zero, 1)
            pool.wait_ge(xn_ready, 4 * NORM["gm"] + 4)
            pool.dma_start(gm_bs, I["gm_bs_2"][0].rearrange("g p -> (g p)").partition_broadcast(P)).then_inc(GM["bs_in"], 16)
            pool.wait_ge(GM["norm"], 1)
            root(36, 2, [(60, 2, GMH)]).then_inc(GM["rstd"], 1)
            for c in range(SLOTS):
                side_load(U_GM + c, ada_view(1, 4 + c % 2, c // 2))
            side_loop(U_GM, 1, 4, 2, 3)
            side_load(U_BC3, bias_row(1, 5))
            row_rstd("relu1")


_INS = ["x", "mix_norm_g", "ffn_norm_g", "final_norm_g", "ev_w_in", "ev_conv_w", "ev_pool_w", "ev_pool_scale", "ev_w_out",
        "od_w_in", "od_b_f", "od_w_out", "rel_bias", "ffn_w_in", "ffn_conv_w", "ffn_conv_b", "ffn_w_out", "c_2", "ctx_2",
        "c_ctx_2", "ada_w_2", "ada_b_2", "norm_mix_g_2", "norm_ffn_g_2", "mla_wq_a_2", "mla_q_a_norm_2", "mla_wq_b_2",
        "mla_wkv_a_2", "mla_kv_a_norm_2", "mla_wkv_b_2", "mla_q_norm_2", "mla_k_norm_2", "mla_wo_2", "gm_w_in_2",
        "gm_ln_g_2", "gm_ln_b_2", "gm_ws_2", "gm_bs_2", "gm_w_out_2", "ffn_w1_2", "ffn_w2_2"]


def constants():
    import math

    import numpy as np

    c = np.zeros((P, C_ALL + P), np.float32)
    i = np.arange(P)
    c[:, C_ID:C_ID + P] = np.eye(P)
    c[:, C_ALL:] = np.eye(P)[::-1]
    c[:, C_U:C_U + P] = i[:, None] <= i[None, :]
    c[:, C_U + P:C_U + 2 * P] = 1.0
    c[:, C_MASK:C_MASK + P] = np.where(i[None, :] <= i[:, None], 0.0, NEG)
    for g in range(4):
        c[:, C_TAB + 16 * g:C_TAB + 16 * g + 16] = 1.0 / np.minimum(np.arange(16) + 1, 2 << g)
    half = ROPE // 2
    grid_w, theta = 64, 10000.0
    pos = np.arange(S)
    inv = (np.float32(theta) ** (-np.arange(0, half, 2, dtype=np.float32) / np.float32(half))).astype(np.float32)
    ang_r = (pos // grid_w).astype(np.float32)[:, None] * inv[None, :]
    ang_c = (pos % grid_w).astype(np.float32)[:, None] * inv[None, :]
    ang = np.concatenate([ang_r, ang_r, ang_c, ang_c], axis=-1).astype(np.float32)
    sign = np.tile(np.repeat([-1.0, 1.0], half // 2), 2)
    c[:, C_COS:C_COS + P] = np.cos(ang).reshape(TT, P, ROPE).transpose(1, 0, 2).reshape(P, P)
    c[:, C_SIN:C_SIN + P] = (np.sin(ang) * sign).reshape(TT, P, ROPE).transpose(1, 0, 2).reshape(P, P)

    buckets, far, exact = 32, 128, 16
    hot = np.zeros((33, 511), np.float32)
    for m in range(511):
        d = 255 - m
        if d < 0:
            hot[32, m] = NEG
        elif d < exact:
            hot[d, m] = 1.0
        else:
            b = exact + int(np.float32(np.log(np.float32(d) / np.float32(exact))) / np.float32(math.log(far / exact))
                            * np.float32(buckets - exact))
            hot[min(b, buckets - 1), m] = 1.0
    return c, hot


def kernel(**inputs):
    import numpy as _np
    import concourse.bacc as _bacc
    from concourse.bass_utils import run_bass_kernel_spmd as _run

    nc = _bacc.Bacc("TRN2", target_bir_lowering=False, num_devices=1)
    arrays, views = {}, {}

    def give(name, a):
        arrays[f"in_{name}"] = a
        views[name] = nc.dram_tensor(f"in_{name}", a.shape, mybir.dt.from_np(a.dtype), kind="ExternalInput").ap()

    for name in _INS:
        give(name, _np.ascontiguousarray(inputs[name]))
    consts, onehot = constants()
    give("consts", consts)
    give("onehot", onehot)
    out = nc.dram_tensor("out_0", (1, S, D), mybir.dt.from_np(_np.dtype("float32")), kind="ExternalOutput").ap()
    build(nc, views, out)
    r = _run(nc, [arrays], core_ids=[0])
    return r.results[0]["out_0"]
```

```python
from contextlib import ExitStack

import concourse.bass as bass
from concourse import mybir

F32 = mybir.dt.float32
F32R = mybir.dt.float32r
ALU = mybir.AluOpType
ACT = mybir.ActivationFunctionType
AX = mybir.AxisListType

P = 128
S = 256
TT = S // P
D = 1024
KB = D // P
FF = 2816
FFB = FF // P
HID = 4096
GMH = 2048
EPS = 1e-6
SLOTS = 4
SLOT_W = 2048
HD = 64
HEADS = 16
FOX = 8
MH = 8
NOPE, ROPE, VD = 128, 64, 128
QKD = NOPE + ROPE
QL, KVL = 384, 256
CTX = 256
KT = (CTX + S) // P
NEG = -1e30

C_ID, C_U, C_MASK, C_TAB, C_COS, C_SIN = 0, 128, 384, 512, 576, 704
C_ALL = 832
ROWS = [("mix_norm_g", 16), ("ffn_norm_g", 16), ("ev_conv_w", 12), ("ev_pool_scale", 4), ("ffn_conv_w", 132),
        ("ffn_conv_b", 44), ("norm_mix_g_2", 16), ("norm_ffn_g_2", 16), ("c_2", 8), ("c_ctx_2", 8),
        ("mla_q_a_norm_2", 3), ("mla_kv_a_norm_2", 2), ("mla_q_norm_2", 1), ("mla_k_norm_2", 1),
        ("ada_b_2", 96)]
ROW = {}
_n = 0
for _name, _k in ROWS:
    ROW[_name] = _n
    _n += _k
N_ROWS = _n
ROW_TILES = -(-N_ROWS // P)
N_ROW_DMAS = sum((ROW[_name] + _k - 1) // P - ROW[_name] // P + 1 for _name, _k in ROWS)


class Aff:

    def __init__(self, c, reg=None, k=0):
        self.c, self.reg, self.k = c, reg, k

    def __add__(self, n):
        return Aff(self.c + n, self.reg, self.k)

    def __sub__(self, n):
        return self + (-n)

    def __mul__(self, n):
        return Aff(self.c * n, self.reg, self.k * n)


def val(x):
    if not isinstance(x, Aff):
        return x
    return x.c if x.reg is None else x.reg * x.k + x.c


def build(nc, I, out):
    ctx = ExitStack()
    with ctx:
        def sb(name, shape, dt=F32):
            return ctx.enter_context(nc.sbuf_tensor(name, shape, dt))

        def sem(name):
            return ctx.enter_context(nc.semaphore(name))

        raw = [sb(f"raw{i}", [P, SLOT_W]) for i in range(SLOTS)]
        w_hi = [sb(f"w_hi{i}", [P, SLOT_W], F32R) for i in range(SLOTS)]
        w_lo = [sb(f"w_lo{i}", [P, SLOT_W], F32R) for i in range(SLOTS)]
        xn_hi, xn_lo = sb("xn_hi", [P, KB * S], F32R), sb("xn_lo", [P, KB * S], F32R)
        a_hi, a_lo = sb("a_hi", [P, KB * S], F32R), sb("a_lo", [P, KB * S], F32R)
        h = sb("h", [P, TT, D])
        side = sb("side", [P, SLOTS, 1024])
        acc = sb("acc", [P, 5, 1024])
        work = sb("work", [P, 7424])
        cst = sb("cst", [P, C_ALL])
        vec = sb("vec", [P, ROW_TILES * P])
        st = sb("st", [P, 88])
        mod = sb("mod", [P, 48])
        cs = sb("cs", [P, 16])
        pe_g = sb("pe_g", [P, 2, ROPE])
        bf = sb("bf", [P, 8])
        wf = sb("wf", [P, KB, 8])
        zf = sb("zf", [P, 5, 16])
        rs = sb("rs", [P, 40])
        rstd = sb("rstd", [P, 40])
        half = sb("half", [P, 8])
        rel = sb("rel", [33, 8])
        ps = [ctx.enter_context(nc.psum_tensor(f"ps{i}", [P, 512], F32)) for i in range(8)]

        ident = cst[:, C_ID:C_ID + P]
        tri_ones = cst[:, C_U:C_U + 2 * P]
        ones = cst[:, C_U + P:C_U + 2 * P]
        causal = cst[:, C_MASK:C_MASK + P]
        pool_tab = cst[:, C_TAB:C_TAB + 64].rearrange("p (g t) -> p g t", g=4)
        cos = cst[:, C_COS:C_COS + P].rearrange("p (t d) -> p t d", t=TT)
        sin = cst[:, C_SIN:C_SIN + P].rearrange("p (t d) -> p t d", t=TT)

        def wk(a, n):
            return work[:, a:a + n]

        hs = wk(0, 2048).rearrange("p (t d) -> p t d", t=TT)
        xf = wk(4096, 2048).rearrange("p (k t) -> p k t", k=KB)
        xn_hi3 = xn_hi[:, :].rearrange("p (k t) -> p k t", k=KB)
        xn_lo3 = xn_lo[:, :].rearrange("p (k t) -> p k t", k=KB)
        a_hi3 = a_hi[:, :].rearrange("p (k t) -> p k t", k=KB)
        a_lo3 = a_lo[:, :].rearrange("p (k t) -> p k t", k=KB)

        def col(name, n=0):
            c = ROW[name] + n
            return vec[:, c:c + 1]

        def vcol(name, n):
            return vec[:, bass.ds(val(n + ROW[name]), 1)]

        scratch = nc.dram_tensor("bias_rows", (8, 512), F32, kind="Internal").ap()

        def kview(w):
            return w.rearrange("(k p) n -> p k n", p=P)

        def f_src(w, c0=0, stride=256, n=256):
            v = kview(w)
            return lambda j: v[:, :, bass.ds(val(j * stride + c0), n)]

        def t_src(w, n):
            v = kview(w)
            return lambda j: v[:, bass.ds(val(j * n), n), :]

        width, straight = [], {}

        def add(src, kb, n, at=0):
            width.append(sum(k * m for _, k, m, _ in (src if isinstance(src, list) else [(0, kb, n, 0)])))
            straight[len(width) - 1] = src if isinstance(src, list) else [(src, kb, n, at)]

        ev_w = I["ev_w_in"][0]
        T_EV = len(width)
        EV_COLS = [1536, 1792, 512, 1024, 0, 768, 1280, 256]
        for c0 in EV_COLS:
            add(f_src(ev_w, c0), KB, 256)
        T_POOL = len(width)
        pool_v = I["ev_pool_w"][0].rearrange("g c d -> c g d")
        add(lambda j: pool_v, 4, P)
        T_EVO = len(width)
        for j in range(4):
            add(t_src(I["ev_w_out"][0], 2), 2, D, j)

        G_STEPS = FFB // 2

        def gated_sources(layer):
            w, wo = I["ffn_w_in"][layer], I["ffn_w_out"][layer]
            return f_src(w), f_src(w, FF), t_src(wo, 1)

        def add_gated(layer):
            u, g, t = gated_sources(layer)
            base = len(width)
            for j in range(G_STEPS + 1):
                if j < G_STEPS:
                    add(u, KB, 256, j)
                    add(g, KB, 256, j)
                if j:
                    add(t, 1, D, 2 * j - 2)
                    add(t, 1, D, 2 * j - 1)
            return base

        R_STEPS = HID // 256

        def relu_sources(layer):
            return f_src(I["ffn_w1_2"][layer]), t_src(I["ffn_w2_2"][layer], 2)

        def add_paired(f, t, steps):
            base = len(width)
            for j in range(steps + 1):
                if j < steps:
                    add(f, KB, 256, j)
                if j:
                    add(t, 2, D, j - 1)
            return base

        T_FFN0 = add_gated(0)
        od_w = I["od_w_in"][0]
        T_QK = len(width)
        for j in range(8):
            add(f_src(od_w), KB, 256, j)
        T_V = len(width)
        for j in range(4):
            add(t_src(od_w[:, 2 * D:3 * D], 2), 2, D, j)
        T_ODO = len(width)
        for j in range(4):
            add(t_src(I["od_w_out"][0], 2), 2, D, j)
        T_FFN1 = add_gated(1)
        T_LA = len(width)
        kva_v = kview(I["mla_wkv_a_2"][0])
        qa_v = kview(I["mla_wq_a_2"][0])
        for j in range(2):
            add(lambda j: kva_v[:, 4 * j:4 * j + 4, :], 4, KVL + ROPE, j)
        for j in range(2):
            add(lambda j: qa_v[:, 4 * j:4 * j + 4, :], 4, QL, j)
        T_HEAD = len(width)
        kvb_v = kview(I["mla_wkv_b_2"][0])
        qb_v = kview(I["mla_wq_b_2"][0])
        for j in range(MH):
            add([(lambda j: kvb_v[:, :, 256 * j:256 * j + 256], 2, 256, j),
                 (lambda j: qb_v[:, :, QKD * j:QKD * j + QKD], 3, QKD, j)], 0, 0)
        T_WO = len(width)
        for j in range(4):
            add(t_src(I["mla_wo_2"][0], 2), 2, D, j)
        T_RELU0 = add_paired(*relu_sources(0), R_STEPS)
        T_GMV = len(width)
        gm_w = I["gm_w_in_2"][0]
        gmv_v = kview(gm_w)
        for j in range(8):
            add(lambda j: gmv_v[:, 4 * (j % 2):4 * (j % 2) + 4, GMH + 512 * (j // 2):GMH + 512 * (j // 2) + 512],
                4, 512, j)
        GM_STEPS = GMH // 256
        T_GM = add_paired(f_src(gm_w), t_src(I["gm_w_out_2"][0], 2), GM_STEPS)
        T_RELU1 = add_paired(*relu_sources(1), R_STEPS)
        N_TILES = len(width)

        LOOP0, LOOP1 = 2, 10
        TRIPS = (LOOP1 - LOOP0) // 2

        U_FFN0 = 0
        U_FFN1 = U_FFN0 + 16
        U_BC1 = U_FFN1 + 32
        U_RELU0 = U_BC1 + 3
        U_BC2 = U_RELU0 + 32
        U_GM = U_BC2 + 5
        U_BC3 = U_GM + 16

        raw_full = [sem(f"raw_full{i}") for i in range(SLOTS)]
        hi_done, lo_done, w_used = sem("hi_done"), sem("lo_done"), sem("w_used")
        side_full = [sem(f"side_full{i}") for i in range(SLOTS)]
        side_used = sem("side_used")
        in_h, in_cst, in_rows, in_small = sem("in_h"), sem("in_cst"), sem("in_rows"), sem("in_small")
        vec_ps, vec_ready, cs_ready = sem("vec_ps"), sem("vec_ready"), sem("cs_ready")
        rb_ready, half_ready, rows_ps, rows_sb, rows_out = sem("rb_ready"), sem("half_ready"), sem("rows_ps"), sem("rows_sb"), sem("rows_out")
        bias_in, ctx_in = sem("bias_in"), sem("ctx_in")
        h_ready, sq_done, ms_step, rstd_ready = sem("h_ready"), sem("sq_done"), sem("ms_step"), sem("rstd_ready")
        hs_ready, xt_ps, xf_ready = sem("hs_ready"), sem("xt_ps"), sem("xf_ready")
        xhi_done, xn_ready = sem("xhi_done"), sem("xn_ready")
        acc_zero, ada_done, ada_ps, mod_step, mod_ready = (
            sem("acc_zero"), sem("ada_done"), sem("ada_ps"), sem("mod_step"), sem("mod_ready"))
        all_out = sem("all_out")
        tok0_done = sem("tok0_done")
        act_step, dve_step, pool_step = sem("act_step"), sem("dve_step"), sem("pool_step")

        def group(prefix, *names):
            return {n: sem(f"{prefix}_{n}") for n in names}

        EV = group("ev", "gate", "prod", "tap2", "tap1", "conv", "y", "yhi", "a_ready", "pin", "pool", "phi",
                   "pool_ready", "pool_a", "ybf", "ybhi")
        FFN = [group(f"ffn{n}", "a0", "tap", "conv", "silu", "prod", "ahi", "a_ready") for n in range(2)]
        RELU = [group(f"relu{n}", "relu", "sq", "ahi", "a_ready") for n in range(2)]
        AT = group("at", "qk", "v_sb", "z_ps", "z", "nabs", "ez", "ln", "neg", "f_ps", "f", "lbc", "s_ps", "s_sb",
                   "max", "exp", "rec", "p", "t_ps", "pt", "o_ps", "ohi", "a_ready")
        LA = group("la", "kv_sb", "q_sb", "lsq", "lrstd", "lscaled", "lt_ps", "lxf", "lhi", "l_ready", "kpe", "a_ps", "a_sq",
                   "a_ms", "a_rstd", "kn", "qpe", "kq_ps", "kq", "s_ps", "max", "exp", "rec", "p", "t_ps", "pt_a", "pt_d",
                   "o_ps", "ohi", "a_ready")
        GM = group("gm", "v", "mu", "sq", "rstd", "norm", "gain", "vn", "ws_in", "ws_ps", "ws", "bs_in", "u", "vs", "m_ps",
                   "t", "prod", "ahi", "a_ready")

        block = ctx.enter_context(nc.Block())

        NORM = {n: k for k, n in enumerate(
            ["ev", "ffn0", "od", "ffn1", "ctx", "lat", "relu0", "gm", "relu1"])}
        H_READY = {"ffn0": 0, "od": 2, "ffn1": 4, "final": 6, "lat": 8, "relu0": 10, "gm": 12, "relu1": 14, "out": 16}
        RSTD = {n: k for k, n in enumerate(
            ["ev", "ffn0", "od", "ffn1", "ctx", "final", "lat", "relu0", "gm", "relu1"])}
        RCOL = dict({n: 2 * k for n, k in NORM.items()}, final=18)
        RESIDUAL = {n: k for k, n in enumerate(["ffn0", "od", "ffn1", "final", "relu0", "gm", "relu1", "out"])}
        MOD_COUNT = {"ctx": 1, "lat": 1, "relu0": 2, "gm": 3, "relu1": 4}

        @block.sync
        def _(sp):
            sp.dma_start(h[:, :, :], I["x"][0].rearrange("(t p) d -> p t d", p=P)).then_inc(in_h, 16)

            def load(t):
                if t >= SLOTS:
                    sp.wait_ge(lo_done, t - SLOTS + 1)
                at, parts = 0, straight[t]
                for src, k, n, j in parts:
                    dst = raw[t % SLOTS][:, at:at + k * n].rearrange("p (k n) -> p k n", k=k)
                    sp.dma_start(dst, src(j)).then_inc(raw_full[t % SLOTS], 16)
                    at += k * n

            def load_gated(layer, base):
                u, g, w = gated_sources(layer)
                first = base + 4 * LOOP0 - 2
                for t in range(base, first):
                    load(t)
                with sp.Fori(0, LOOP1 - LOOP0) as i:
                    j = Aff(LOOP0, i, 1)
                    views = [(u(j), KB, 256), (g(j), KB, 256), (w(j * 2 - 2), 1, D), (w(j * 2 - 1), 1, D)]
                    free = [sp.snap(val(j * 4 + (base - 2 + m - SLOTS + 1))) for m in range(4)]
                    for m, (src, k, n) in enumerate(views):
                        s = (first + m) % SLOTS
                        sp.wait_ge(lo_done, free[m])
                        sp.dma_start(raw[s][:, 0:k * n].rearrange("p (k n) -> p k n", k=k), src)\
                            .then_inc(raw_full[s], 16)
                for t in range(base + 4 * LOOP1 - 2, base + 4 * G_STEPS):
                    load(t)

            def load_paired(f, w, base, steps, loop0, loop1):
                first = base + 2 * loop0 - 1
                for t in range(base, first):
                    load(t)
                with sp.Fori(0, (loop1 - loop0) // 2) as i:
                    js = [Aff(loop0 + m, i, 2) for m in range(2)]
                    views = []
                    for j in js:
                        views += [(f(j), KB, 256), (w(j - 1), 2, D)]
                    free = [sp.snap(val(js[0] * 2 + (base - 1 + m - SLOTS + 1))) for m in range(4)]
                    for m, (src, k, n) in enumerate(views):
                        s = (first + m) % SLOTS
                        sp.wait_ge(lo_done, free[m])
                        sp.dma_start(raw[s][:, 0:k * n].rearrange("p (k n) -> p k n", k=k), src)\
                            .then_inc(raw_full[s], 16)
                for t in range(base + 2 * loop1 - 1, base + 2 * steps):
                    load(t)

            load(T_EV)
            at = 0
            stage = wk(6144, ROW_TILES * P).rearrange("p (r c) -> p r c", r=ROW_TILES)
            for name, n in ROWS:
                src = I[name]
                if name.endswith(("q_norm_2", "k_norm_2")):
                    src = src[0:1, 0:P]
                else:
                    while len(src.shape) > 1:
                        src = src.rearrange("a b -> (a b)") if len(src.shape) == 2 else src.rearrange("a b c -> (a b c)")
                    src = src.rearrange("(r c) -> r c", c=P)
                done = 0
                while done < n:
                    m = min(n - done, P - (at % P))
                    sp.dma_start(stage[at % P:at % P + m, at // P, :], src[done:done + m, :]).then_inc(in_rows, 16)
                    done, at = done + m, at + m
            for t in range(T_EV + 1, T_FFN0):
                load(t)
            load_gated(0, T_FFN0)
            for t in range(T_QK, T_FFN1):
                load(t)
            load_gated(1, T_FFN1)
            for t in range(T_LA, T_RELU0):
                load(t)
            load_paired(*relu_sources(0), T_RELU0, R_STEPS, 2, 14)
            for t in range(T_GMV, T_GM):
                load(t)
            load_paired(f_src(gm_w), t_src(I["gm_w_out_2"][0], 2), T_GM, GM_STEPS, 2, 6)
            load_paired(*relu_sources(1), T_RELU1, R_STEPS, 2, 14)
            sp.wait_ge(h_ready, H_READY["out"] + 2)
            sp.dma_start(out[0].rearrange("(t p) d -> p t d", p=P), h[:, :, :]).then_inc(all_out, 16)
            sp.wait_ge(all_out, 16)
            sp.wait_ge(rows_out, 16)

        landed = []
        per_slot = [0] * SLOTS
        for t in range(N_TILES):
            per_slot[t % SLOTS] += 16 * len(straight[t])
            landed.append(per_slot[t % SLOTS])

        @block.scalar
        def _(act):
            def split(t):
                t = t if isinstance(t, Aff) else Aff(t)
                if t.c >= N_TILES:
                    return
                s, w = t.c % SLOTS, width[t.c]
                act.wait_ge(raw_full[s], val(Aff(landed[t.c], t.reg, t.k * 16 // SLOTS)))
                if t.c >= SLOTS:
                    act.wait_ge(w_used, val(t - (SLOTS - 1)))
                nc.scalar.activation(w_hi[s][:, 0:w], raw[s][:, 0:w], ACT.Copy).then_inc(hi_done, 1)

            act.dma_start(cst[:, :], I["consts"][:, 0:C_ALL]).then_inc(in_cst, 16)

            def squares(name, src):
                for t in range(TT):
                    if name == "ctx":
                        act.wait_ge(ctx_in, 16)
                    elif name == "ev":
                        act.wait_ge(in_h, 16)
                    else:
                        act.wait_ge(h_ready, H_READY[name] + t + 1)
                    c = RCOL[name] + t
                    junk = wk(4096 + D * t, D) if name in ("ctx", "final") else hs[:, t, :]
                    nc.scalar.activation(junk, src[:, t, :], ACT.Square, accum_out=st[:, c:c + 1]).then_inc(sq_done, 1)

            def gains(name, gain, shift=None):
                k = NORM[name]
                if name in MOD_COUNT:
                    act.wait_ge(mod_ready, MOD_COUNT[name])
                if name == "ev":
                    act.wait_ge(vec_ready, 1)
                for i in range(4):
                    act.wait_ge(xt_ps, 4 * k + i + 1)
                    for m in range(2):
                        b = 2 * i + m
                        if shift is None:
                            last = nc.scalar.activation(xf[:, b, :], ps[i][:, m * S:m * S + S], ACT.Copy, scale=gain(b))
                        else:
                            last = nc.scalar.activation(xf[:, b, :], ps[i][:, m * S:m * S + S], ACT.Identity,
                                                        scale=gain(b), bias=shift(b))
                    last.then_inc(xf_ready, 1)

            def norm(name, src, gain, shift=None, late=None):
                squares(name, src)
                if late is not None:
                    split(late)
                gains(name, gain, shift)

            squares("ev", h)
            split(T_EV)
            gains("ev", lambda b: col("mix_norm_g", b))
            split(T_EV + 1)
            split(T_EV + 2)
            split(T_EV + 3)
            nc.scalar.activation(cs[:, :], vec[:, ROW["c_2"]:ROW["c_2"] + 16], ACT.Silu).then_inc(cs_ready, 1)

            ev_c = wk(6144, 512)
            ev_cv = wk(2048, 2 * 258).rearrange("p (b t) -> p b t", b=2)
            ev_a = wk(6656, 512).rearrange("p (b t) -> p b t", b=2)
            ev_y = wk(0, 512)
            ev_u = wk(2564, 4 * 272).rearrange("p (g t) -> p g t", g=4)
            for m in range(2):
                act.wait_ge(w_used, T_EV + m + 1)
                if m == 0:
                    act.wait_ge(EV["pin"], 1)
                nc.scalar.activation(ev_u[:, 2 * m:2 * m + 2, 16:272], ps[m][:, :].rearrange("p (g t) -> p g t", g=2), ACT.Copy)\
                    .then_inc(EV["pool"], 1)
                split(T_EV + m + 4)
            for m in range(2):
                t = T_EV + 2 + 3 * m
                act.wait_ge(w_used, t + 1)
                nc.scalar.activation(ev_c, ps[(2 + 3 * m) % 4][:, :], ACT.Copy).then_inc(EV["gate"], 1)
                split(t + 4)
                act.wait_ge(EV["prod"], m + 1)
                for b in range(2):
                    nc.scalar.activation(ev_a[:, b, :], ev_cv[:, b, 2:258], ACT.Copy,
                                         scale=col("ev_conv_w", 8 + 2 * m + b)).then_inc(EV["tap2"], 1)
                split(t + 5)
                if m == 0:
                    act.wait_ge(EV["pool_ready"], 1)
                    nc.scalar.activation(a_hi[:, 1024:2048], wk(1024, 1024), ACT.Copy).then_inc(EV["phi"], 1)
                split(t + 6)
                act.wait_ge(EV["y"], m + 1)
                nc.scalar.activation(a_hi[:, 512 * m:512 * m + 512], ev_y, ACT.Copy).then_inc(EV["yhi"], 1)
            act.wait_ge(w_used, T_POOL + 1)
            for m in range(2):
                for g in range(2):
                    nc.scalar.activation(wk(1024 + (2 * m + g) * S, S), ps[m][:, g * S:g * S + S],
                                         ACT.Copy, scale=col("ev_pool_scale", 2 * m + g)).then_inc(EV["ybf"], 1)
            act.wait_ge(EV["ybf"], 4)
            nc.scalar.activation(a_hi[:, 1024:2048], wk(1024, 1024), ACT.Copy).then_inc(EV["ybhi"], 1)
            split(T_POOL + 4)
            for j in range(3):
                split(T_EVO + j + 4)

            f_a0 = wk(6144, 512).rearrange("p (b t) -> p b t", b=2)
            f_s, f_p = wk(6656, 512), wk(2048, 512)

            def gated(n, base):
                g = FFN[n]

                def step(j, par):
                    u = j * 4 + (base - 2) if j.c else Aff(base)
                    act.wait_ge(w_used, val(u + 1))
                    for b in range(2):
                        nc.scalar.activation(f_a0[:, b, :], ps[0][:, b * S:b * S + S], ACT.Identity,
                                             scale=vcol("ffn_conv_w", j * 2 + (n * 3 * FFB + 2 * FFB + b)),
                                             bias=vcol("ffn_conv_b", j * 2 + (n * FFB + b))).then_inc(g["a0"], 1)
                    split(u + 4)
                    act.wait_ge(g["conv"], val(j * 2 + 2))
                    nc.scalar.activation(f_s, wk(6144, 512), ACT.Silu).then_inc(g["silu"], 1)
                    split(u + 5)
                    act.wait_ge(g["prod"], val(j + 1))
                    nc.scalar.activation(a_hi[:, par * 512:par * 512 + 512], f_p, ACT.Copy).then_inc(g["ahi"], 1)
                    if j.c:
                        split(u + 6)
                        split(u + 7)

                for j in range(LOOP0):
                    step(Aff(j), j % 2)
                if n == 1:
                    squares("ctx", hs)
                with act.Fori(0, TRIPS) as i:
                    for m in range(2):
                        step(Aff(LOOP0 + m, i, 2), m)
                for j in range(LOOP1, G_STEPS):
                    step(Aff(j), j % 2)
                if n == 1:
                    gains("ctx", lambda b: mod[:, 8 + b:9 + b], lambda b: mod[:, b:b + 1])
                split(base + 4 * G_STEPS + 2)

            norm("ffn0", h, lambda b: col("ffn_norm_g", b), late=T_FFN0 + 3)
            gated(0, T_FFN0)

            norm("od", h, lambda b: col("mix_norm_g", 8 + b), late=T_QK + 3)
            act.wait_ge(AT["nabs"], 1)
            nc.scalar.activation(zf[:, 1, :], zf[:, 1, :], ACT.Exp).then_inc(AT["ez"], 1)
            act.wait_ge(AT["ez"], 1)
            nc.scalar.activation(zf[:, 1, :], zf[:, 1, :], ACT.Ln, bias=1.0).then_inc(AT["ln"], 1)
            for j in range(8):
                act.wait_ge(w_used, T_QK + j + 1)
                nc.scalar.activation(wk(512 * j, 512), ps[j % 4][:, :], ACT.Copy, scale=HD ** -0.5 if j < 4 else 1.0)\
                    .then_inc(AT["qk"], 1)
                split(T_QK + j + 4)
            at_s = wk(6144, 768).rearrange("p (b k) -> p b k", b=2)
            at_pt = wk(6912, 384)
            SEG = [(0, P), (P, 3 * P)]

            def at_exp(i):
                act.wait_ge(AT["max"], 2 * i + 2)
                src = at_s[:, i % 2, :] if i < FOX else ps[i % 2]
                for t, (c0, c1) in enumerate(SEG):
                    nc.scalar.activation(at_s[:, i % 2, c0:c1], src[:, c0:c1], ACT.Exp,
                                         bias=st[:, 32 + 4 * (i % 2) + t:33 + 4 * (i % 2) + t],
                                         accum_out=st[:, 34 + 4 * (i % 2) + t:35 + 4 * (i % 2) + t]).then_inc(AT["exp"], 1)

            at_exp(0)
            for j in range(4):
                split(T_V + j + 4)
            for i in range(HEADS):
                act.wait_ge(AT["t_ps"], i + 1)
                nc.scalar.activation(at_pt, ps[2 + i % 2][:, 0:384], ACT.Copy).then_inc(AT["pt"], 1)
                if i + 1 < HEADS:
                    at_exp(i + 1)
                act.wait_ge(AT["o_ps"], i + 1)
                r = HD * (i % 2)
                nc.scalar.activation(a_hi3[r:r + HD, i // 2, :], ps[4 + i % 2][r:r + HD, 0:S], ACT.Copy).then_inc(AT["ohi"], 1)
            for j in range(3):
                split(T_ODO + j + 4)

            norm("ffn1", h, lambda b: col("ffn_norm_g", 8 + b), late=T_FFN1 + 3)
            gated(1, T_FFN1)

            squares("final", h)

            kva = wk(6144, KT * (KVL + ROPE)).rearrange("p (t d) -> p t d", t=KT)
            cq = wk(2048, TT * QL).rearrange("p (t d) -> p t d", t=TT)
            act.wait_ge(LA["a_ps"], 1)
            for t in range(TT):
                nc.scalar.activation(kva[:, t, :], ps[t][:, 0:KVL + ROPE], ACT.Copy).then_inc(LA["kv_sb"], 1)
            norm("lat", h, lambda b: mod[:, 24 + b:25 + b], lambda b: mod[:, 16 + b:17 + b], late=T_LA + 3)
            act.wait_ge(w_used, T_LA + 2)
            for t in range(TT):
                nc.scalar.activation(kva[:, TT + t, :], ps[6 + t][:, 0:KVL + ROPE], ACT.Copy).then_inc(LA["kv_sb"], 1)
            split(T_LA + 4)
            split(T_LA + 5)
            act.wait_ge(w_used, T_LA + 4)
            for t in range(TT):
                nc.scalar.activation(cq[:, t, :], ps[4 + t][:, 0:QL], ACT.Copy).then_inc(LA["q_sb"], 1)
            split(T_LA + 6)
            split(T_LA + 7)
            act.wait_ge(LA["kv_sb"], 4)
            act.wait_ge(LA["q_sb"], 2)
            for t in range(KT):
                nc.scalar.activation(wk(KVL * t, KVL), kva[:, t, 0:KVL], ACT.Square, accum_out=st[:, 48 + t:49 + t]).then_inc(LA["lsq"], 1)
            for t in range(TT):
                nc.scalar.activation(wk(KT * KVL + QL * t, QL), cq[:, t, :], ACT.Square, accum_out=st[:, 52 + t:53 + t]).then_inc(LA["lsq"], 1)
            for t in range(KT):
                nc.scalar.activation(wk(KT * KVL + TT * QL + ROPE * t, ROPE), kva[:, t, KVL:], ACT.Square, accum_out=st[:, 64 + t:65 + t])\
                    .then_inc(LA["lsq"], 1)
            lf_kv, lf_q = wk(4096, 1024), wk(5120, 768)
            act.wait_ge(LA["lt_ps"], 1)
            for b in range(2):
                nc.scalar.activation(lf_kv[:, 512 * b:512 * b + 512], ps[6 + b][:, :], ACT.Copy, scale=col("mla_kv_a_norm_2", b))\
                    .then_inc(LA["lxf"], 1)
            for b in range(3):
                nc.scalar.activation(lf_q[:, S * b:S * b + S], ps[5 - b // 2][:, S * (b % 2):S * (b % 2) + S], ACT.Copy,
                                     scale=col("mla_q_a_norm_2", b)).then_inc(LA["lxf"], 1)

            la_kta = [wk(512 * p, 512) for p in range(2)]
            la_ktb = [wk(1024 + 512 * p, 512) for p in range(2)]
            la_qt = [wk(2048 + 512 * p, 512) for p in range(2)]
            la_v = [v.rearrange("p (t d) -> p t d", t=KT) for v in (wk(3072, 512), wk(3584, 512), acc[:, 2, 512:1024])]
            la_p = wk(4096, 1024).rearrange("p (t k) -> p t k", t=TT)
            la_pt = wk(5120, 1024)
            la_junk = acc[:, 1, :]

            def la_values(i):
                act.wait_ge(w_used, T_HEAD + i + 1)
                for m in range(2):
                    kv2 = ps[m][:, :].rearrange("p (t d) -> p t d", t=2)
                    nc.scalar.activation(la_v[i % 3][:, 2 * m:2 * m + 2, :], kv2[:, :, NOPE:], ACT.Copy)
                for t in range(KT):
                    nc.scalar.activation(la_junk[:, NOPE * t:NOPE * t + NOPE], ps[t // 2][:, 256 * (t % 2):256 * (t % 2) + NOPE], ACT.Square,
                                         accum_out=st[:, 72 + t:73 + t]).then_inc(LA["a_sq"], 1)
                for t in range(TT):
                    nc.scalar.activation(la_junk[:, KT * NOPE + QKD * t:KT * NOPE + QKD * t + QKD], ps[2][:, QKD * t:QKD * t + QKD], ACT.Square,
                                         accum_out=st[:, 76 + t:77 + t]).then_inc(LA["a_sq"], 1)
                split(T_HEAD + i + 4)

            def la_transposed(i):
                act.wait_ge(LA["kq_ps"], i + 1)
                p = i % 2
                nc.scalar.activation(la_kta[p], ps[3][:, :], ACT.Copy, scale=col("mla_k_norm_2"))
                nc.scalar.activation(la_ktb[p][0:ROPE, :], ps[0][0:ROPE, :], ACT.Copy)
                nc.scalar.activation(la_qt[p][:, 0:S], ps[1][:, 0:S], ACT.Copy, scale=col("mla_q_norm_2"))
                nc.scalar.activation(la_qt[p][0:ROPE, S:2 * S], ps[1][0:ROPE, S:2 * S], ACT.Copy).then_inc(LA["kq"], 1)

            la_values(0)
            la_transposed(0)
            for i in range(MH + 1):
                if i:
                    act.wait_ge(LA["t_ps"], i)
                    nc.scalar.activation(la_pt[:, 0:512], ps[6][:, :], ACT.Copy).then_inc(LA["pt_a"], 1)
                if i + 1 < MH:
                    la_values(i + 1)
                if i < MH:
                    act.wait_ge(LA["max"], i + 1)
                    for t in range(TT):
                        nc.scalar.activation(la_p[:, t, :], ps[4 + t][:, :], ACT.Exp, scale=QKD ** -0.5,
                                             bias=st[:, 82 + t:83 + t], accum_out=st[:, 84 + t:85 + t]).then_inc(LA["exp"], 1)
                if i:
                    act.wait_ge(LA["o_ps"], i)
                    nc.scalar.activation(a_hi3[:, i - 1, :], ps[6][:, 0:S], ACT.Copy).then_inc(LA["ohi"], 1)
                if i + 1 < MH:
                    la_transposed(i + 1)
            for j in range(3):
                split(T_WO + j + 4)

            r_r, r_s = wk(6144, 512), [wk(2048 + 512 * m, 512) for m in range(2)]

            def relu(n, base):
                g = RELU[n]

                def step(j, par):
                    f = j * 2 + (base - 1) if j.c else Aff(base)
                    act.wait_ge(w_used, val(f + 1))
                    nc.scalar.activation(r_r, ps[par][:, :], ACT.Relu).then_inc(g["relu"], 1)
                    split(f + 4)
                    act.wait_ge(g["sq"], val(j + 1))
                    nc.scalar.activation(a_hi[:, par * 512:par * 512 + 512], r_s[par], ACT.Copy).then_inc(g["ahi"], 1)
                    if j.c:
                        split(f + 5)

                for j in range(2):
                    step(Aff(j), j % 2)
                with act.Fori(0, 6) as i:
                    for m in range(2):
                        step(Aff(2 + m, i, 2), m)
                for j in range(14, R_STEPS):
                    step(Aff(j), j % 2)

            norm("relu0", h, lambda b: mod[:, 40 + b:41 + b], lambda b: mod[:, 32 + b:33 + b], late=T_RELU0 + 3)
            relu(0, T_RELU0)

            norm("gm", h, lambda b: mod[:, 24 + b:25 + b], lambda b: mod[:, 16 + b:17 + b], late=T_GMV + 3)
            gm_v = wk(0, 4096).rearrange("p (t d) -> p t d", t=TT)
            for c in range(4):
                act.wait_ge(w_used, T_GMV + 2 * c + 2)
                for t in range(TT):
                    nc.scalar.activation(gm_v[:, t, 512 * c:512 * c + 512], ps[2 * c + t][:, :], ACT.Gelu,
                                         accum_out=st[:, 48 + 4 * t + c:49 + 4 * t + c]).then_inc(GM["v"], 1)
                split(T_GMV + 2 * c + 4)
                split(T_GMV + 2 * c + 5)
            for t in range(TT):
                act.wait_ge(GM["mu"], 1)
                for c in range(4):
                    junk = ps[4 + c][:, :] if t else acc[:, 3 + c // 2, 512 * (c % 2):512 * (c % 2) + 512]
                    nc.scalar.activation(junk, gm_v[:, t, 512 * c:512 * c + 512], ACT.Square,
                                         bias=st[:, 58 + t:59 + t], accum_out=st[:, 64 + 4 * t + c:65 + 4 * t + c])\
                        .then_inc(GM["sq"], 1)
            gm_u = wk(6144, 512)
            gm_t = [acc[:, 4, 512 * m:512 * m + 512] for m in range(2)]

            def gm_step(j, par):
                f = j * 2 + (T_GM - 1) if j.c else Aff(T_GM)
                act.wait_ge(w_used, val(f + 1))
                nc.scalar.activation(gm_u, ps[par][:, :], ACT.Gelu).then_inc(GM["u"], 1)
                split(f + 4)
                act.wait_ge(GM["prod"], val(j + 1))
                nc.scalar.activation(a_hi[:, par * 512:par * 512 + 512], gm_t[par], ACT.Copy).then_inc(GM["ahi"], 1)
                if j.c:
                    split(f + 5)

            act.wait_ge(GM["ws"], 2)
            for j in range(2):
                gm_step(Aff(j), j % 2)
            with act.Fori(0, 2) as i:
                for m in range(2):
                    gm_step(Aff(2 + m, i, 2), m)
            for j in range(6, GM_STEPS):
                gm_step(Aff(j), j % 2)

            norm("relu1", h, lambda b: mod[:, 40 + b:41 + b], lambda b: mod[:, 32 + b:33 + b], late=T_RELU1 + 3)
            relu(1, T_RELU1)

        ev_c = wk(6144, 512).rearrange("p (b t) -> p b t", b=2)
        ev_cv = wk(2048, 2 * 258).rearrange("p (b t) -> p b t", b=2)
        ev_a = wk(6656, 512)
        ev_y = wk(0, 512)
        ev_u = wk(2564, 4 * 272).rearrange("p (g t) -> p g t", g=4)
        ev_s0 = wk(4096, 4 * 272).rearrange("p (g t) -> p g t", g=4)
        ev_s1 = wk(5184, 3 * 272).rearrange("p (g t) -> p g t", g=3)
        ev_p = wk(1024, 1024).rearrange("p (g t) -> p g t", g=4)
        onehot = acc[0:33, 4, 0:511]
        bias_rows = acc[0:8, 4, 512:1023]
        t5_bias = acc[:, 0:3, :].rearrange("p a b -> p (a b)").rearrange("p (h k) -> p h k", h=8)
        flip = acc[:, 3, 512:640]
        f_a0 = wk(6144, 512).rearrange("p (b t) -> p b t", b=2)
        f_s, f_p = wk(6656, 512), wk(2048, 512)
        at_qk = wk(0, 4096).rearrange("p (b t) -> p b t", b=16)
        at_v = wk(4096, 2048).rearrange("p (t d) -> p t d", t=TT)
        at_s = wk(6144, 768).rearrange("p (b k) -> p b k", b=2)
        at_pt = wk(6912, 384)
        at_l = acc[:, 3, 0:512].rearrange("p (b t q) -> p b t q", b=2, t=TT)
        kva = wk(6144, KT * (KVL + ROPE)).rearrange("p (t d) -> p t d", t=KT)
        cq = wk(2048, TT * QL).rearrange("p (t d) -> p t d", t=TT)
        lf_kv, lf_q = wk(4096, 1024), wk(5120, 768)
        la_kta = [wk(512 * p, 512) for p in range(2)]
        la_ktb = [wk(1024 + 512 * p, 512) for p in range(2)]
        la_qt = [wk(2048 + 512 * p, 512) for p in range(2)]
        la_v = [v.rearrange("p (t d) -> p t d", t=KT) for v in (wk(3072, 512), wk(3584, 512), acc[:, 2, 512:1024])]
        la_p = wk(4096, 1024).rearrange("p (t k) -> p t k", t=TT)
        la_pt = wk(5120, 1024)
        la_kn = wk(6144, KT * QKD).rearrange("p (t d) -> p t d", t=KT)
        la_qn = wk(6912, TT * QKD).rearrange("p (t d) -> p t d", t=TT)
        la_kpe = acc[:, 2, 0:KT * ROPE].rearrange("p (t d) -> p t d", t=KT)
        la_rot = acc[:, 2, 256:256 + TT * ROPE].rearrange("p (t d) -> p t d", t=TT)
        r_r, r_s = wk(6144, 512), [wk(2048 + 512 * m, 512) for m in range(2)]
        gm_v = wk(0, 4096).rearrange("p (t d) -> p t d", t=TT)
        gm_bs, gm_wst, gm_ws = wk(4096, 1024), wk(5120, 1024), wk(6144, 1024)
        gm_u = wk(6144, 512)
        gm_t = [acc[:, 4, 512 * m:512 * m + 512] for m in range(2)]
        gm_vs = acc[:, 3, 0:512].rearrange("p (t c) -> p t c", t=TT)
        SEG = [(0, P), (P, 3 * P)]

        @block.vector
        def _(dve):
            steps = [0]

            def chain(ins):
                steps[0] += 1
                ins.then_inc(dve_step, 1)
                dve.wait_ge(dve_step, steps[0])

            def split(t):
                t = t if isinstance(t, Aff) else Aff(t)
                if t.c >= N_TILES:
                    return
                s, w = t.c % SLOTS, width[t.c]
                dve.wait_ge(hi_done, val(t + 1))
                nc.vector.tensor_tensor(w_lo[s][:, 0:w], raw[s][:, 0:w], w_hi[s][:, 0:w].bitcast(F32), ALU.subtract)\
                    .then_inc(lo_done, 1)

            def scale(name, src):
                for t in range(TT):
                    dve.wait_ge(rstd_ready, 2 * RSTD[name] + t + 1)
                    c = RCOL[name] + t
                    nc.vector.tensor_scalar(hs[:, t, :], src[:, t, :], rstd[:, c:c + 1], None, ALU.mult).then_inc(hs_ready, 1)

            def take(name):
                k = NORM[name]
                for i in range(4):
                    dve.wait_ge(xf_ready, 4 * k + i + 1)
                    nc.vector.tensor_copy(xn_hi3[:, 2 * i:2 * i + 2, :], xf[:, 2 * i:2 * i + 2, :]).then_inc(xhi_done, 1)
                    dve.wait_ge(xhi_done, 4 * k + i + 1)
                    nc.vector.tensor_tensor(xn_lo3[:, 2 * i:2 * i + 2, :], xf[:, 2 * i:2 * i + 2, :],
                                            xn_hi3[:, 2 * i:2 * i + 2, :].bitcast(F32), ALU.subtract).then_inc(xn_ready, 1)

            def norm(name, src, late=None):
                scale(name, src)
                if late is not None:
                    split(late)
                take(name)

            def residual(name, last, gate=None):
                for t in range(TT):
                    if t == 0:
                        dve.wait_ge(tok0_done, RESIDUAL[name] + 1)
                    else:
                        dve.wait_ge(w_used, last + 1)
                    for c in range(2):
                        hv = h[:, t, 512 * c:512 * c + 512]
                        part = ps[4 + 2 * t + c][:, :]
                        if gate is not None:
                            tmp = wk(6144 + 512 * c, 512)
                            chain(nc.vector.tensor_tensor(tmp, part, gate[:, 512 * c:512 * c + 512], ALU.mult))
                            part = tmp
                        add = nc.vector.tensor_tensor(hv, part, hv, ALU.add)
                    add.then_inc(h_ready, 1)

            def ada(s, slot, kb, also=None):
                s = s if isinstance(s, Aff) else Aff(s)
                tile = side[:, s.c % SLOTS, :]
                dve.wait_ge(side_full[s.c % SLOTS], val(Aff(16 * (s.c // SLOTS + 1), s.reg, s.k * 4)))
                if also is not None:
                    nc.vector.scalar_tensor_tensor(acc[:, also, :], tile, cs[:, bass.ds(val(kb + 8), 1)], acc[:, also, :],
                                                   ALU.mult, ALU.add)
                nc.vector.scalar_tensor_tensor(acc[:, slot, :], tile, cs[:, bass.ds(val(kb), 1)], acc[:, slot, :],
                                               ALU.mult, ALU.add).then_inc(side_used, 1)

            def bias_cols(layer, comp):
                c = ROW["ada_b_2"] + 48 * layer + 8 * comp
                return vec[:, c:c + 8]

            def shift_cols(dst, sums, layer, comp):
                return nc.vector.tensor_tensor(mod[:, dst:dst + 8], sums, bias_cols(layer, comp), ALU.add)

            def gain_cols(dst, sums, layer, comp, g):
                chain(shift_cols(dst, sums, layer, comp))
                return nc.vector.scalar_tensor_tensor(mod[:, dst:dst + 8], mod[:, dst:dst + 8], 1.0, g, ALU.add, ALU.mult)

            def gate_rows(slot, banks, unit):
                dve.wait_ge(side_full[unit % SLOTS], 16 * (unit // SLOTS + 1))
                for c in range(2):
                    last = nc.vector.tensor_tensor(acc[:, slot, 512 * c:512 * c + 512], ps[banks[c]][:, :],
                                                   side[:, unit % SLOTS, 512 * c:512 * c + 512], ALU.add)
                last.then_inc(side_used, 1)

            dve.wait_ge(in_h, 16)
            scale("ev", h)
            split(T_EV)
            dve.wait_ge(vec_ps, 1)
            nc.vector.tensor_copy(vec[:, 0:N_ROWS], ps[4][:, 0:N_ROWS]).then_inc(vec_ready, 1)
            take("ev")
            nc.vector.memset(ev_cv[:, :, 0:2], 0.0)
            nc.vector.memset(ev_u[:, :, 0:16], 0.0).then_inc(EV["pin"], 1)
            split(T_EV + 1)
            split(T_EV + 2)
            split(T_EV + 3)
            dve.wait_ge(EV["pin"], 1)

            split(T_EV + 4)
            dve.wait_ge(EV["pool"], 2)
            split(T_EV + 5)
            chain(nc.vector.tensor_tensor(ev_s0[:, :, 1:272], ev_u[:, :, 1:272], ev_u[:, :, 0:271], ALU.add))
            chain(nc.vector.tensor_tensor(ev_s1[:, :, 3:272], ev_s0[:, 1:4, 3:272], ev_s0[:, 1:4, 1:270], ALU.add))
            chain(nc.vector.tensor_tensor(ev_s0[:, 2:4, 7:272], ev_s1[:, 1:3, 7:272], ev_s1[:, 1:3, 3:268], ALU.add))
            chain(nc.vector.tensor_tensor(ev_s1[:, 2, 15:272], ev_s0[:, 3, 15:272], ev_s0[:, 3, 7:264], ALU.add))
            sums = [ev_s0[:, 0, :], ev_s1[:, 0, :], ev_s0[:, 2, :], ev_s1[:, 2, :]]
            for g in range(4):
                nc.vector.tensor_tensor(ev_p[:, g, 0:16], sums[g][:, 16:32], pool_tab[:, g, :], ALU.mult)
                last = nc.vector.scalar_tensor_tensor(ev_p[:, g, 16:S], sums[g][:, 32:272], 1.0 / (2 << g),
                                                      ev_u[:, g, 32:272], ALU.mult, ALU.subtract)
            chain(last)
            nc.vector.tensor_tensor(ev_p[:, :, 0:16], ev_p[:, :, 0:16], ev_u[:, :, 16:32], ALU.subtract).then_inc(EV["pool_ready"], 1)
            for m in range(2):
                t = T_EV + 2 + 3 * m
                dve.wait_ge(EV["gate"], m + 1)
                dve.wait_ge(w_used, t + 2)
                nc.vector.tensor_tensor(ev_cv[:, :, 2:258], ps[(3 + 3 * m) % 4][:, :].rearrange("p (b t) -> p b t", b=2),
                                        ev_c, ALU.mult).then_inc(EV["prod"], 1)
                split(t + 4)
                dve.wait_ge(EV["tap2"], 2 * m + 2)
                for tap, done in ((1, EV["tap1"]), (0, EV["conv"])):
                    for b in range(2):
                        av = ev_a[:, b * S:b * S + S]
                        nc.vector.scalar_tensor_tensor(av, ev_cv[:, b, tap:tap + S], col("ev_conv_w", 4 * tap + 2 * m + b),
                                                       av, ALU.mult, ALU.add).then_inc(done, 1)
                    dve.wait_ge(done, 2 * m + 2)
                split(t + 5)
                if m == 0:
                    dve.wait_ge(EV["phi"], 1)
                    nc.vector.tensor_tensor(a_lo[:, 1024:2048], wk(1024, 1024), a_hi[:, 1024:2048].bitcast(F32), ALU.subtract)\
                        .then_inc(EV["pool_a"], 1)
                dve.wait_ge(w_used, t + 3)
                nc.vector.tensor_tensor(ev_y, ps[(4 + 3 * m) % 4][:, :], ev_a, ALU.mult).then_inc(EV["y"], 1)
                split(t + 6)
                dve.wait_ge(EV["yhi"], m + 1)
                c = slice(512 * m, 512 * m + 512)
                nc.vector.tensor_tensor(a_lo[:, c], ev_y, a_hi[:, c].bitcast(F32), ALU.subtract).then_inc(EV["a_ready"], 1)
            dve.wait_ge(EV["ybhi"], 1)
            nc.vector.tensor_tensor(a_lo[:, 1024:2048], wk(1024, 1024), a_hi[:, 1024:2048].bitcast(F32), ALU.subtract)\
                .then_inc(EV["a_ready"], 1)
            split(T_POOL + 4)
            dve.wait_ge(rows_ps, 1)
            nc.vector.tensor_copy(bias_rows, ps[2][0:8, 0:511]).then_inc(rows_sb, 1)
            for j in range(3):
                split(T_EVO + j + 4)
            residual("ffn0", T_FFN0 - 1)

            def gated(n, base):
                g = FFN[n]

                def step(j, par, units):
                    u = j * 4 + (base - 2) if j.c else Aff(base)
                    dve.wait_ge(g["a0"], val(j * 2 + 2))
                    for shift, done in ((1, g["tap"]), (2, g["conv"])):
                        for b in range(2):
                            av = f_a0[:, b, shift:S]
                            tap = 2 - shift
                            nc.vector.scalar_tensor_tensor(av, ps[0][:, b * S:b * S + S - shift],
                                                           vcol("ffn_conv_w", j * 2 + (n * 3 * FFB + tap * FFB + b)),
                                                           av, ALU.mult, ALU.add).then_inc(done, 1)
                        if shift == 1:
                            dve.wait_ge(done, val(j * 2 + 2))
                    split(u + 4)
                    dve.wait_ge(g["silu"], val(j + 1))
                    dve.wait_ge(w_used, val(u + 2))
                    nc.vector.tensor_tensor(f_p, ps[1][:, :], f_s, ALU.mult).then_inc(g["prod"], 1)
                    split(u + 5)
                    dve.wait_ge(g["ahi"], val(j + 1))
                    c = slice(par * 512, par * 512 + 512)
                    nc.vector.tensor_tensor(a_lo[:, c], f_p, a_hi[:, c].bitcast(F32), ALU.subtract).then_inc(g["a_ready"], 1)
                    if units:
                        kb = j - LOOP0
                        if n == 0:
                            ada(kb * 2 + U_FFN0, 0, kb, 2)
                            ada(kb * 2 + (U_FFN0 + 1), 1, kb, 3)
                        else:
                            for c in range(4):
                                ada(kb * 4 + (U_FFN1 + c), c, kb)
                    if j.c:
                        split(u + 6)
                        split(u + 7)

                for j in range(LOOP0):
                    step(Aff(j), j % 2, False)
                if n == 1:
                    scale("ctx", hs)
                dve.wait_ge(acc_zero, n + 1)
                dve.wait_ge(cs_ready, 1)
                with dve.Fori(0, TRIPS) as i:
                    for m in range(2):
                        step(Aff(LOOP0 + m, i, 2), m, True)
                for j in range(LOOP1, G_STEPS):
                    step(Aff(j), j % 2, False)
                if n == 1:
                    take("ctx")
                residual("od" if n == 0 else "final", base + 4 * G_STEPS - 1)
                split(base + 4 * G_STEPS + 2)

            norm("ffn0", h, late=T_FFN0 + 3)
            gated(0, T_FFN0)

            def at_out(i):
                dve.wait_ge(AT["ohi"], i + 1)
                r = HD * (i % 2)
                nc.vector.tensor_tensor(a_lo3[r:r + HD, i // 2, :], ps[4 + i % 2][r:r + HD, 0:S],
                                        a_hi3[r:r + HD, i // 2, :].bitcast(F32), ALU.subtract).then_inc(AT["a_ready"], 1)

            def at_decay(i):
                dve.wait_ge(AT["neg"], 1)
                for t in range(TT):
                    nc.vector.tensor_scalar(at_l[:, i % 2, t, :], ones, zf[:, 3, 8 * t + i:8 * t + i + 1], None, ALU.mult)\
                        .then_inc(AT["lbc"], 1)

            def at_scores(i):
                dve.wait_ge(AT["s_ps"], i + 1)
                s, bank = at_s[:, i % 2, :], ps[i % 2]
                if i < FOX:
                    if i == 0:
                        dve.wait_ge(AT["f"], 1)
                    f = [zf[:, 4, 8 * t + i:8 * t + i + 1] for t in range(TT)]
                    nc.vector.scalar_tensor_tensor(s[:, 0:P], bank[:, 0:P], f[0], causal, ALU.add, ALU.add).then_inc(AT["s_sb"], 1)
                    nc.vector.tensor_scalar(s[:, P:2 * P], bank[:, P:2 * P], f[1], None, ALU.add).then_inc(AT["s_sb"], 1)
                    nc.vector.scalar_tensor_tensor(s[:, 2 * P:3 * P], bank[:, 2 * P:3 * P], f[1], causal, ALU.add, ALU.add)\
                        .then_inc(AT["s_sb"], 1)
                    dve.wait_ge(AT["s_sb"], 3 * i + 3)
                else:
                    s = bank
                for t, (c0, c1) in enumerate(SEG):
                    c = 32 + 4 * (i % 2) + t
                    nc.vector.tensor_reduce(st[:, c:c + 1], s[:, c0:c1], AX.X, ALU.max, negate=True).then_inc(AT["max"], 1)

            norm("od", h, late=T_QK + 3)
            dve.wait_ge(in_small, 16 * 5)
            dve.wait_ge(AT["z_ps"], 1)
            for t in range(TT):
                nc.vector.tensor_tensor(zf[:, 0, 8 * t:8 * t + 8], ps[7][:, 8 * t:8 * t + 8], bf[:, :], ALU.add).then_inc(AT["z"], 1)
            dve.wait_ge(AT["z"], 2)
            chain(nc.vector.tensor_scalar(zf[:, 2, :], zf[:, 0, :], 0.0, None, ALU.min))
            nc.vector.scalar_tensor_tensor(zf[:, 1, :], zf[:, 2, :], 2.0, zf[:, 0, :], ALU.mult, ALU.subtract).then_inc(AT["nabs"], 1)
            dve.wait_ge(AT["ln"], 1)
            nc.vector.tensor_tensor(zf[:, 3, :], zf[:, 1, :], zf[:, 2, :], ALU.subtract).then_inc(AT["neg"], 1)
            dve.wait_ge(AT["f_ps"], 1)
            nc.vector.tensor_scalar(zf[:, 4, :], ps[6][:, 0:16], -1.0, None, ALU.mult).then_inc(AT["f"], 1)
            for j in range(8):
                split(T_QK + j + 4)
            dve.wait_ge(ada_ps, 1)
            g_mix = vec[:, ROW["norm_mix_g_2"]:ROW["norm_mix_g_2"] + 8]
            shift_cols(0, ps[7][:, 16:24], 0, 0)
            gain_cols(8, ps[7][:, 24:32], 0, 1, g_mix)
            shift_cols(16, ps[7][:, 0:8], 0, 0)
            gain_cols(24, ps[7][:, 8:16], 0, 1, g_mix).then_inc(mod_ready, 1)
            at_decay(0)
            at_decay(1)
            at_scores(0)
            for j in range(4):
                split(T_V + j + 4)
            for t in range(TT):
                for c in range(2):
                    dve.wait_ge(w_used, T_V + 4)
                    nc.vector.tensor_copy(at_v[:, t, 512 * c:512 * c + 512], ps[4 + 2 * t + c][:, :]).then_inc(AT["v_sb"], 1)

            for i in range(HEADS):
                dve.wait_ge(AT["exp"], 2 * i + 2)
                c = 34 + 4 * (i % 2)
                nc.vector.reciprocal(st[:, 40:42], st[:, c:c + 2]).then_inc(AT["rec"], 1)
                dve.wait_ge(AT["rec"], i + 1)
                for t, (c0, c1) in enumerate(SEG):
                    nc.vector.tensor_scalar(at_s[:, i % 2, c0:c1], at_s[:, i % 2, c0:c1], st[:, 40 + t:41 + t], None, ALU.mult)\
                        .then_inc(AT["p"], 1)
                if i + 2 < FOX:
                    at_decay(i + 2)
                if i + 1 < HEADS:
                    at_scores(i + 1)
                if i:
                    at_out(i - 1)
            at_out(HEADS - 1)
            for j in range(3):
                split(T_ODO + j + 4)
            residual("ffn1", T_FFN1 - 1)

            norm("ffn1", h, late=T_FFN1 + 3)
            gated(1, T_FFN1)

            dve.wait_ge(side_full[U_BC1 % SLOTS], 16 * (U_BC1 // SLOTS + 1))
            for t in range(TT):
                dve.wait_ge(rstd_ready, 2 * RSTD["final"] + t + 1)
                final = nc.vector.scalar_tensor_tensor(h[:, t, :], h[:, t, :], rstd[:, 18 + t:19 + t],
                                                       side[:, U_BC1 % SLOTS, :], ALU.mult, ALU.mult)
                final.then_inc(h_ready, 1)

            norm("lat", h, late=T_LA + 3)
            for j in range(4, 8):
                split(T_LA + j)
            dve.wait_ge(LA["lrstd"], 1)
            for t in range(KT):
                nc.vector.tensor_scalar(kva[:, t, 0:KVL], kva[:, t, 0:KVL], rstd[:, 20 + t:21 + t], None, ALU.mult)\
                    .then_inc(LA["lscaled"], 1)
            for t in range(TT):
                nc.vector.tensor_scalar(cq[:, t, :], cq[:, t, :], rstd[:, 24 + t:25 + t], None, ALU.mult).then_inc(LA["lscaled"], 1)
            dve.wait_ge(ada_ps, 2)
            g_ffn = vec[:, ROW["norm_ffn_g_2"]:ROW["norm_ffn_g_2"] + 8]
            shift_cols(32, ps[4][:, 0:8], 0, 3).then_inc(side_used, 1)
            gain_cols(40, ps[4][:, 8:16], 0, 4, g_ffn).then_inc(mod_ready, 1)
            gate_rows(0, (2, 3), U_BC1 + 1)
            gate_rows(4, (0, 1), U_BC1 + 2)
            dve.wait_ge(LA["kv_sb"], 4)
            chain(nc.vector.tensor_tensor(la_kpe, kva[:, :, KVL:], pe_g[:, 1:2, :].to_broadcast([P, KT, ROPE]), ALU.mult))

            def turn(x):
                v = [y.rearrange("p t (a s c) -> p t a s c", a=2, s=2) for y in (x, la_rot, sin)]
                for s in range(2):
                    last = nc.vector.tensor_tensor(v[1][:, :, :, s, :], v[0][:, :, :, 1 - s, :], v[2][:, :, :, s, :], ALU.mult)
                chain(last)
                chain(nc.vector.tensor_tensor(x, x, cos, ALU.mult))
                return nc.vector.tensor_tensor(x, x, la_rot, ALU.add)

            chain(turn(la_kpe[:, TT:KT, :]))
            dve.wait_ge(LA["lxf"], 5)
            nc.vector.tensor_copy(xn_hi[:, 0:1024], lf_kv).then_inc(LA["lhi"], 1)
            nc.vector.tensor_copy(xn_hi[:, 1024:1792], lf_q).then_inc(LA["lhi"], 1)
            dve.wait_ge(LA["lhi"], 2)
            nc.vector.tensor_tensor(xn_lo[:, 0:1024], lf_kv, xn_hi[:, 0:1024].bitcast(F32), ALU.subtract).then_inc(LA["l_ready"], 1)
            nc.vector.tensor_tensor(xn_lo[:, 1024:1792], lf_q, xn_hi[:, 1024:1792].bitcast(F32), ALU.subtract)\
                .then_inc(LA["l_ready"], 1)

            def la_normed(i):
                dve.wait_ge(LA["a_rstd"], i + 1)
                for m in range(2):
                    kv2 = ps[m][:, :].rearrange("p (t d) -> p t d", t=2)
                    r = rstd[:, 28 + 2 * m:30 + 2 * m].unsqueeze(2).to_broadcast([P, 2, NOPE])
                    nc.vector.tensor_tensor(la_kn[:, 2 * m:2 * m + 2, 0:NOPE], kv2[:, :, 0:NOPE], r, ALU.mult)
                nc.vector.tensor_tensor(la_kn[:, :, NOPE:], la_kpe, rstd[:, 28:32].unsqueeze(2).to_broadcast([P, KT, ROPE]),
                                        ALU.mult).then_inc(LA["kn"], 1)
                for t in range(TT):
                    last = nc.vector.tensor_scalar(la_qn[:, t, :], ps[2][:, QKD * t:QKD * t + QKD], rstd[:, 32 + t:33 + t],
                                                   None, ALU.mult)
                chain(last)
                qpe = la_qn[:, :, NOPE:]
                chain(nc.vector.tensor_tensor(qpe, qpe, pe_g[:, 0:1, :].to_broadcast([P, TT, ROPE]), ALU.mult))
                turn(qpe).then_inc(LA["qpe"], 1)

            la_normed(0)
            split(T_HEAD + 4)
            for i in range(MH + 1):
                if i:
                    dve.wait_ge(LA["t_ps"], i)
                    nc.vector.tensor_copy(la_pt[:, 512:1024], ps[7][:, :]).then_inc(LA["pt_d"], 1)
                if i < MH:
                    dve.wait_ge(LA["s_ps"], i + 1)
                    for t in range(TT):
                        last = nc.vector.tensor_reduce(st[:, 80 + t:81 + t], ps[4 + t][:, :], AX.X, ALU.max, negate=True)
                    chain(last)
                    nc.vector.tensor_scalar(st[:, 82:84], st[:, 80:82], QKD ** -0.5, None, ALU.mult).then_inc(LA["max"], 1)
                if i + 1 < MH:
                    la_normed(i + 1)
                if i:
                    dve.wait_ge(LA["ohi"], i)
                    nc.vector.tensor_tensor(a_lo3[:, i - 1, :], ps[6][:, 0:S], a_hi3[:, i - 1, :].bitcast(F32), ALU.subtract)\
                        .then_inc(LA["a_ready"], 1)
                if i < MH:
                    dve.wait_ge(LA["exp"], 2 * i + 2)
                    nc.vector.reciprocal(st[:, 86:88], st[:, 84:86]).then_inc(LA["rec"], 1)
                    dve.wait_ge(LA["rec"], i + 1)
                    for t in range(TT):
                        nc.vector.tensor_scalar(la_p[:, t, :], la_p[:, t, :], st[:, 86 + t:87 + t], None, ALU.mult)\
                            .then_inc(LA["p"], 1)
                if i + 1 < MH:
                    split(T_HEAD + i + 5)
            for j in range(3):
                split(T_WO + j + 4)
            residual("relu0", T_RELU0 - 1, acc[:, 0, :])

            def relu(n, base):
                g = RELU[n]

                def step(j, par, units):
                    f = j * 2 + (base - 1) if j.c else Aff(base)
                    dve.wait_ge(g["relu"], val(j + 1))
                    nc.vector.tensor_tensor(r_s[par], r_r, r_r, ALU.mult).then_inc(g["sq"], 1)
                    split(f + 4)
                    dve.wait_ge(g["ahi"], val(j + 1))
                    c = slice(par * 512, par * 512 + 512)
                    nc.vector.tensor_tensor(a_lo[:, c], r_s[par], a_hi[:, c].bitcast(F32), ALU.subtract).then_inc(g["a_ready"], 1)
                    if units:
                        kb = j - 2
                        for c in range(4):
                            ada(kb * 4 + (U_RELU0 + c), c, kb)
                    if j.c:
                        split(f + 5)

                for j in range(2):
                    step(Aff(j), j % 2, False)
                if n == 0:
                    dve.wait_ge(acc_zero, 3)
                else:
                    dve.wait_ge(ada_ps, 6)
                    gate_rows(1, (2, 3), U_BC3)
                with dve.Fori(0, 4) as i:
                    for m in range(2):
                        step(Aff(2 + m, i, 2), m, n == 0)
                with dve.Fori(0, 2) as i:
                    for m in range(2):
                        step(Aff(10 + m, i, 2), m, False)
                for j in range(14, R_STEPS):
                    step(Aff(j), j % 2, False)

            norm("relu0", h, late=T_RELU0 + 3)
            relu(0, T_RELU0)
            residual("gm", T_GMV - 1, acc[:, 4, :])
            dve.wait_ge(ada_ps, 3)
            g_mix1 = vec[:, ROW["norm_mix_g_2"] + 8:ROW["norm_mix_g_2"] + 16]
            g_ffn1 = vec[:, ROW["norm_ffn_g_2"] + 8:ROW["norm_ffn_g_2"] + 16]
            shift_cols(16, ps[3][:, 0:8], 1, 0)
            gain_cols(24, ps[3][:, 8:16], 1, 1, g_mix1).then_inc(mod_ready, 1)

            norm("gm", h, late=T_GMV + 3)
            dve.wait_ge(ada_ps, 4)
            shift_cols(32, ps[6][:, 0:8], 1, 3)
            gate_rows(2, (4, 5), U_BC2)
            dve.wait_ge(GM["ws_ps"], 1)
            for c in range(2):
                nc.vector.tensor_copy(gm_wst[:, 512 * c:512 * c + 512], ps[c][:, :]).then_inc(GM["ws"], 1)
            for j in range(8):
                split(T_GMV + j + 4)
            dve.wait_ge(GM["v"], 8)
            chain(nc.vector.tensor_reduce(st[:, 56:58], st[:, 48:56].rearrange("p (t c) -> p t c", t=TT), AX.X, ALU.add))
            nc.vector.tensor_scalar(st[:, 58:60], st[:, 56:58], -1.0 / GMH, None, ALU.mult).then_inc(GM["mu"], 1)
            dve.wait_ge(GM["mu"], 1)
            dve.wait_ge(GM["sq"], 8)
            nc.vector.tensor_reduce(st[:, 60:62], st[:, 64:72].rearrange("p (t c) -> p t c", t=TT), AX.X, ALU.add)\
                .then_inc(GM["norm"], 1)
            dve.wait_ge(GM["rstd"], 1)

            def gm_norm(c):
                vv = [gm_v[:, t, 1024 * c:1024 * c + 1024] for t in range(TT)]
                for t in range(TT):
                    last = nc.vector.tensor_scalar(vv[t], vv[t], st[:, 58 + t:59 + t], rstd[:, 36 + t:37 + t], ALU.add, ALU.mult)
                chain(last)
                for m, op in enumerate((ALU.mult, ALU.add)):
                    u = U_BC2 + 1 + 2 * c + m
                    dve.wait_ge(side_full[u % SLOTS], 16 * (u // SLOTS + 1))
                    for t in range(TT):
                        last = nc.vector.tensor_tensor(vv[t], vv[t], side[:, u % SLOTS, :], op)
                    last.then_inc(side_used, 1)
                    dve.wait_ge(side_used, u + 1)

            gm_norm(0)

            def gm_slice(j):
                return nc.vector.tensor_copy(gm_vs, gm_v[:, :, bass.ds(val(j * 256), 256)]).then_inc(GM["vs"], 1)

            def gm_step(j, par, more=True):
                f = j * 2 + (T_GM - 1) if j.c else Aff(T_GM)
                dve.wait_ge(GM["m_ps"], val(j + 1))
                nc.vector.tensor_tensor(gm_t[par].rearrange("p (b q) -> p b q", b=4), ps[2 + par][:, :].rearrange("p (b q) -> p b q", b=4),
                                        gm_bs[:, bass.ds(val(j * P), P)].unsqueeze(1).to_broadcast([P, 4, P]), ALU.add)\
                    .then_inc(GM["t"], 1)
                if more:
                    gm_slice(j + 1)
                split(f + 4)
                dve.wait_ge(GM["t"], val(j + 1))
                dve.wait_ge(GM["u"], val(j + 1))
                nc.vector.tensor_tensor(gm_t[par], gm_t[par], gm_u, ALU.mult).then_inc(GM["prod"], 1)
                dve.wait_ge(GM["ahi"], val(j + 1))
                c = slice(par * 512, par * 512 + 512)
                nc.vector.tensor_tensor(a_lo[:, c], gm_t[par], a_hi[:, c].bitcast(F32), ALU.subtract).then_inc(GM["a_ready"], 1)
                for c in range(2):
                    ada(j * 2 + (U_GM + c), c, j)
                if j.c:
                    split(f + 5)

            gm_slice(Aff(0))
            gm_norm(1)
            dve.wait_ge(GM["bs_in"], 16)
            dve.wait_ge(acc_zero, 4)
            for j in range(2):
                gm_step(Aff(j), j % 2)
            with dve.Fori(0, 2) as i:
                for m in range(2):
                    gm_step(Aff(2 + m, i, 2), m)
            for j in range(6, GM_STEPS):
                gm_step(Aff(j), j % 2, j + 1 < GM_STEPS)
            residual("relu1", T_RELU1 - 1, acc[:, 2, :])
            dve.wait_ge(ada_ps, 5)
            gain_cols(40, ps[3][:, 0:8], 1, 4, g_ffn1).then_inc(mod_ready, 1)
            norm("relu1", h, late=T_RELU1 + 3)
            relu(1, T_RELU1)
            residual("out", N_TILES - 1, acc[:, 1, :])

        @block.tensor
        def _(pe):
            def parts(s, c, n):
                return w_hi[s][:, c:c + n], w_lo[s][:, c:c + n]

            def f_tile(t, bank, fresh=None):
                t = t if isinstance(t, Aff) else Aff(t)
                pe.wait_ge(lo_done, val(t + 1))
                for b in range(2):
                    o = ps[bank][:, b * S:b * S + S]
                    for k in range(KB):
                        if fresh is not None and b == 0 and k % 2 == 0:
                            pe.wait_ge(xn_ready, 4 * NORM[fresh] + k // 2 + 1)
                        hi, lo = parts(t.c % SLOTS, k * 256 + b * P, P)
                        nc.tensor.matmul(o, hi, xn_hi3[:, k, :], start=k == 0, stop=False)
                        nc.tensor.matmul(o, hi, xn_lo3[:, k, :], start=False, stop=False)
                        last = nc.tensor.matmul(o, lo, xn_hi3[:, k, :], start=False, stop=k == KB - 1)
                last.then_inc(w_used, 1)

            def t_tile(t, blocks, first, last, x=(a_hi3, a_lo3), free=True, bank0=4, n=D, done=None, ends=False, fresh=None):
                t = t if isinstance(t, Aff) else Aff(t)
                pe.wait_ge(lo_done, val(t + 1))
                cuts = [(c, min(512, n - c)) for c in range(0, n, 512)]
                order = [(m, tt) for m in range(len(blocks)) for tt in range(TT)]
                if ends:
                    order.sort(key=lambda step: step[1])
                for at, (m, tt) in enumerate(order):
                    k = blocks[m]
                    if fresh is not None and tt == 0 and k % 2 == 0:
                        pe.wait_ge(xn_ready, 4 * NORM[fresh] + k // 2 + 1)
                    xh, xl = (y[:, k, tt * P:tt * P + P] for y in x)
                    begin, end = first and m == 0, last and m == len(blocks) - 1
                    for x_part, w_part in ((xh, 0), (xh, 1), (xl, 0)):
                        for c, (c0, cn) in enumerate(cuts):
                            w = parts(t.c % SLOTS, m * n + c0, cn)[w_part]
                            o = ps[bank0 + len(cuts) * tt + c][:, 0:cn]
                            ins = nc.tensor.matmul(o, x_part, w, start=begin and x_part is xh and w_part == 0,
                                                   stop=end and x_part is xl)
                    if ends and at == len(blocks) - 1:
                        ins.then_inc(tok0_done, 1)
                if free:
                    ins.then_inc(w_used, 1)
                elif done is not None:
                    ins.then_inc(done, 1)

            def norm(name):
                k = NORM[name]
                for t in range(TT):
                    pe.wait_ge(hs_ready, 2 * k + t + 1)
                    for b in range(KB):
                        c = (b % 2) * S + t * P
                        last = nc.tensor.transpose(ps[b // 2][:, c:c + P], hs[:, t, b * P:b * P + P], ident)
                        if t == TT - 1 and b % 2 == 1:
                            last.then_inc(xt_ps, 1)

            def columns(slot, bank, c0):
                for b in range(8):
                    last = nc.tensor.matmul(ps[bank][:, c0 + b:c0 + b + 1], acc[:, slot, b * P:b * P + P], ones[:, 0:1],
                                            start=True, stop=True)
                return last

            def rows(slot, banks):
                for c in range(2):
                    last = nc.tensor.matmul(ps[banks[c]][:, :], ones, acc[:, slot, 512 * c:512 * c + 512], start=True, stop=True)
                return last

            pe.wait_ge(in_cst, 16)
            norm("ev")
            pe.wait_ge(in_rows, 16 * N_ROW_DMAS)
            stage = wk(6144, ROW_TILES * P).rearrange("p (r c) -> p r c", r=ROW_TILES)
            for r in range(ROW_TILES):
                n = min(P, N_ROWS - r * P)
                last = nc.tensor.transpose(ps[4][:, r * P:r * P + n], stage[0:n, r, :], ident[0:n, 0:n])
            last.then_inc(vec_ps, 1)

            free = {4: (EV["pool"], 1), 5: (EV["pool"], 2), 6: (EV["gate"], 1), 7: (EV["prod"], 1)}
            for m in range(8):
                if m in free:
                    pe.wait_ge(*free[m])
                f_tile(T_EV + m, m % 4, fresh="ev" if m == 0 else None)
            pe.wait_ge(EV["pool_a"], 1)
            pe.wait_ge(EV["gate"], 2)
            pe.wait_ge(EV["y"], 1)
            pe.wait_ge(lo_done, T_POOL + 1)
            for g in range(4):
                o = ps[g // 2][:, (g % 2) * S:(g % 2) * S + S]
                hi, lo = parts(T_POOL % SLOTS, g * P, P)
                nc.tensor.matmul(o, hi, a_hi3[:, 4 + g, :], start=True, stop=False)
                nc.tensor.matmul(o, hi, a_lo3[:, 4 + g, :], start=False, stop=False)
                last = nc.tensor.matmul(o, lo, a_hi3[:, 4 + g, :], start=False, stop=True)
            last.then_inc(w_used, 1)
            for j in range(4):
                if j < 3:
                    pe.wait_ge(EV["a_ready"], j + 1)
                t_tile(T_EVO + j, (2 * j, 2 * j + 1), j == 0, j == 3, ends=j == 3)
                if j == 0:
                    pe.wait_ge(EV["prod"], 2)
                    pe.wait_ge(in_small, 16 * 5)
                    pe.wait_ge(rb_ready, 16)
                    nc.tensor.matmul(ps[2][0:8, 0:511], rel[:, :], onehot, start=True, stop=True).then_inc(rows_ps, 1)

            def gated(n, base):
                g = FFN[n]

                def f_step(j):
                    u = j * 4 + (base - 2) if j.c else Aff(base)
                    if j.c:
                        pe.wait_ge(g["conv"], val(j * 2))
                    f_tile(u, 0, fresh=f"ffn{n}" if j.c == 0 else None)
                    if j.c:
                        pe.wait_ge(g["prod"], val(j))
                    f_tile(u + 1, 1)

                def t_step(j, par, first=False, last=False):
                    pe.wait_ge(g["a_ready"], val(j + 1))
                    w = j * 4 + (base + 4) if j.c < G_STEPS - 1 else Aff(base + 4 * G_STEPS - 2)
                    t_tile(w, (2 * par,), first, False)
                    t_tile(w + 1, (2 * par + 1,), False, last, ends=last)

                f_step(Aff(0))
                f_step(Aff(1))
                t_step(Aff(0), 0, first=True)
                with pe.Fori(0, TRIPS) as i:
                    for m in range(2):
                        j = Aff(LOOP0 + m, i, 2)
                        f_step(j)
                        t_step(j - 1, 1 - m)
                for j in range(LOOP1, G_STEPS):
                    f_step(Aff(j))
                    t_step(Aff(j - 1), (j - 1) % 2)
                if n == 1:
                    pe.wait_ge(g["prod"], G_STEPS)
                    norm("ctx")
                t_step(Aff(G_STEPS - 1), (G_STEPS - 1) % 2, last=True)

            norm("ffn0")
            gated(0, T_FFN0)

            norm("od")
            pe.wait_ge(xn_ready, 4 * NORM["od"] + 4)
            for t in range(TT):
                for k in range(KB):
                    last = nc.tensor.matmul(ps[7][:, 8 * t:8 * t + 8], xf[:, k, t * P:t * P + P], wf[:, k, :],
                                            start=k == 0, stop=k == KB - 1)
            last.then_inc(AT["z_ps"], 1)
            for j in range(8):
                if j >= 4:
                    pe.wait_ge(AT["qk"], j - 3)
                f_tile(T_QK + j, j % 4)
                if j == 1:
                    pe.wait_ge(AT["neg"], 1)
                    nc.tensor.matmul(ps[6][:, 0:8], tri_ones[:, 0:P], zf[:, 3, 0:8], start=True, stop=True)
                    nc.tensor.matmul(ps[6][:, 8:16], ones, zf[:, 3, 0:8], start=True, stop=False)
                    nc.tensor.matmul(ps[6][:, 8:16], tri_ones[:, 0:P], zf[:, 3, 8:16], start=False, stop=True)\
                        .then_inc(AT["f_ps"], 1)
            pe.wait_ge(side_used, U_FFN1)
            for c in range(4):
                last = columns(c, 7, 8 * c)
            last.then_inc(ada_ps, 1)
            def at_scores(i):
                r, b, o = HD * (i % 2), i // 2, ps[i % 2]
                fox = i < FOX
                if 2 <= i < FOX + 2:
                    pe.wait_ge(AT["s_sb"], 3 * (i - 2) + 3)
                elif i >= 2:
                    pe.wait_ge(AT["exp"], 2 * (i - 2) + 2)
                if i == FOX:
                    pe.wait_ge(bias_in, 48)
                q, k = at_qk[r:r + HD, b, :], at_qk[r:r + HD, 8 + b, :]
                nc.tensor.matmul(o[:, 0:P], q[:, 0:P], k[:, 0:P], start=True, stop=False)
                if fox:
                    pe.wait_ge(AT["lbc"], 2 * i + 2)
                    nc.tensor.matmul(o[:, 0:P], at_l[:, i % 2, 0, :], tri_ones[:, 0:P], start=False, stop=True)
                else:
                    nc.tensor.matmul(o[:, 0:P], flip, t5_bias[:, i - FOX, 0:P], start=False, stop=True)
                nc.tensor.matmul(o[:, P:3 * P], q[:, P:S], k, start=True, stop=False)
                if fox:
                    nc.tensor.matmul(o[:, P:3 * P], at_l[:, i % 2, 0, :], tri_ones, start=False, stop=False)
                    last = nc.tensor.matmul(o[:, 2 * P:3 * P], at_l[:, i % 2, 1, :], tri_ones[:, 0:P], start=False, stop=True)
                else:
                    last = nc.tensor.matmul(o[:, P:3 * P], flip, t5_bias[:, i - FOX, P:3 * P], start=False, stop=True)
                last.then_inc(AT["s_ps"], 1)

            pe.wait_ge(AT["qk"], 8)
            at_scores(0)
            at_scores(1)
            pe.wait_ge(AT["f"], 1)
            pe.wait_ge(mod_ready, 1)
            for j in range(4):
                t_tile(T_V + j, (2 * j, 2 * j + 1), j == 0, j == 3, x=(xn_hi3, xn_lo3))

            pe.wait_ge(AT["v_sb"], 4)
            for i in range(HEADS):
                pe.wait_ge(AT["p"], 2 * i + 2)
                pv = at_s[:, i % 2, :]
                for b in range(3):
                    last = nc.tensor.transpose(ps[2 + i % 2][:, b * P:b * P + P], pv[:, b * P:b * P + P], ident)
                last.then_inc(AT["t_ps"], 1)
                if i + 2 < HEADS:
                    at_scores(i + 2)
                pe.wait_ge(AT["pt"], i + 1)
                if i >= 2:
                    pe.wait_ge(AT["a_ready"], i - 1)
                d = slice((i // 2) * P, (i // 2) * P + P)
                o = ps[4 + i % 2]
                nc.tensor.matmul(o[:, 0:S], at_v[:, 0, d], at_pt[:, 0:S], start=True, stop=False)
                nc.tensor.matmul(o[:, P:S], at_v[:, 1, d], at_pt[:, S:3 * P], start=False, stop=True).then_inc(AT["o_ps"], 1)
            pe.wait_ge(AT["a_ready"], HEADS)
            for j in range(4):
                t_tile(T_ODO + j, (2 * j, 2 * j + 1), j == 0, j == 3, ends=j == 3)

            norm("ffn1")
            gated(1, T_FFN1)

            xn = (xn_hi3, xn_lo3)
            kv_tile = dict(x=xn, n=KVL + ROPE)
            pe.wait_ge(xn_ready, 4 * NORM["ctx"] + 4)
            t_tile(T_LA, range(4), True, False, free=False, bank0=0, **kv_tile)
            t_tile(T_LA + 1, range(4, 8), False, True, free=False, bank0=0, done=LA["a_ps"], **kv_tile)
            pe.wait_ge(LA["kv_sb"], 2)
            norm("lat")
            t_tile(T_LA, range(4), True, False, bank0=6, fresh="lat", **kv_tile)
            t_tile(T_LA + 1, range(4, 8), False, True, bank0=6, fresh="lat", **kv_tile)
            t_tile(T_LA + 2, range(4), True, False, x=xn, bank0=4, n=QL)
            t_tile(T_LA + 3, range(4, 8), False, True, x=xn, bank0=4, n=QL)
            pe.wait_ge(side_used, U_BC1)
            rows(3, (0, 1))
            rows(0, (2, 3))
            pe.wait_ge(LA["q_sb"], TT)
            columns(1, 4, 0)
            columns(2, 4, 8).then_inc(ada_ps, 1)
            pe.wait_ge(LA["lscaled"], 6)
            for b in range(2):
                for t in range(KT):
                    nc.tensor.transpose(ps[6 + b][:, t * P:t * P + P], kva[:, t, b * P:b * P + P], ident)
            for b in range(3):
                if b == 2:
                    pe.wait_ge(mod_ready, 2)
                for t in range(TT):
                    c = S * (b % 2) + t * P
                    last = nc.tensor.transpose(ps[5 - b // 2][:, c:c + P], cq[:, t, b * P:b * P + P], ident)
            last.then_inc(LA["lt_ps"], 1)
            ckv = [y[:, 0:1024].rearrange("p (k t) -> p k t", k=2) for y in (xn_hi, xn_lo)]
            cqt = [y[:, 1024:1792].rearrange("p (k t) -> p k t", k=3) for y in (xn_hi, xn_lo)]
            pe.wait_ge(LA["l_ready"], 2)

            def la_project(i):
                t = T_HEAD + i
                pe.wait_ge(lo_done, t + 1)
                if i:
                    pe.wait_ge(LA["kq"], i)
                s = t % SLOTS
                for x, nk, tiles, base, n, where in (
                        (ckv, 2, KT, 0, 256, lambda m: ps[m // 2][:, 256 * (m % 2):256 * (m % 2) + 256]),
                        (cqt, 3, TT, 512, QKD, lambda m: ps[2][:, QKD * m:QKD * m + QKD])):
                    for m in range(tiles):
                        for k in range(nk):
                            hi, lo = parts(s, base + k * n, n)
                            xh, xl = (y[:, k, m * P:m * P + P] for y in x)
                            nc.tensor.matmul(where(m), xh, hi, start=k == 0, stop=False)
                            nc.tensor.matmul(where(m), xh, lo, start=False, stop=False)
                            last = nc.tensor.matmul(where(m), xl, hi, start=False, stop=k == nk - 1)
                last.then_inc(w_used, 1)

            def la_transpose(i):
                pe.wait_ge(LA["kn"], i + 1)
                for t in range(KT):
                    nc.tensor.transpose(ps[3][:, t * P:t * P + P], la_kn[:, t, 0:NOPE], ident)
                    nc.tensor.transpose(ps[0][0:ROPE, t * P:t * P + P], la_kn[:, t, NOPE:], ident)
                pe.wait_ge(LA["qpe"], i + 1)
                for t in range(TT):
                    nc.tensor.transpose(ps[1][:, t * P:t * P + P], la_qn[:, t, 0:NOPE], ident)
                    last = nc.tensor.transpose(ps[1][0:ROPE, S + t * P:S + t * P + P], la_qn[:, t, NOPE:], ident)
                last.then_inc(LA["kq_ps"], 1)

            def la_scores(i):
                q = la_qt[i % 2]
                pe.wait_ge(LA["kq"], i + 1)
                if i:
                    pe.wait_ge(LA["exp"], 2 * i)
                for t in range(TT):
                    nc.tensor.matmul(ps[4 + t][:, :], q[:, t * P:t * P + P], la_kta[i % 2], start=True, stop=False)
                    last = nc.tensor.matmul(ps[4 + t][:, :], q[0:ROPE, S + t * P:S + t * P + P], la_ktb[i % 2][0:ROPE, :],
                                            start=False, stop=True)
                last.then_inc(LA["s_ps"], 1)

            def la_weights(i):
                pe.wait_ge(LA["p"], 2 * i + 2)
                if i:
                    pe.wait_ge(LA["a_ready"], i)
                for k in range(KT):
                    for t in range(TT):
                        c = (k % 2) * S + t * P
                        last = nc.tensor.transpose(ps[6 + k // 2][:, c:c + P], la_p[:, t, k * P:k * P + P], ident)
                last.then_inc(LA["t_ps"], 1)

            def la_sums(i):
                pe.wait_ge(LA["pt_a"], i + 1)
                pe.wait_ge(LA["pt_d"], i + 1)
                for k in range(KT):
                    last = nc.tensor.matmul(ps[6][:, 0:S], la_v[i % 3][:, k, :], la_pt[:, k * S:k * S + S],
                                            start=k == 0, stop=k == KT - 1)
                last.then_inc(LA["o_ps"], 1)

            la_project(0)
            la_transpose(0)
            for i in range(MH + 1):
                if i:
                    la_weights(i - 1)
                if i + 1 < MH:
                    la_project(i + 1)
                if i < MH:
                    la_scores(i)
                if i:
                    la_sums(i - 1)
                if i + 1 < MH:
                    la_transpose(i + 1)
            pe.wait_ge(LA["a_ready"], MH)
            for j in range(4):
                t_tile(T_WO + j, (2 * j, 2 * j + 1), j == 0, j == 3, ends=j == 3)

            def relu(n, base):
                g = RELU[n]

                def f_step(j, par):
                    if j.c >= 2:
                        pe.wait_ge(g["relu"], val(j - 1))
                    f_tile(j * 2 + (base - 1) if j.c else Aff(base), par, fresh=f"relu{n}" if j.c == 0 else None)

                def t_step(j, par, first=False, last=False):
                    pe.wait_ge(g["a_ready"], val(j + 1))
                    w = j * 2 + (base + 2) if j.c < R_STEPS - 1 else Aff(base + 2 * R_STEPS - 1)
                    t_tile(w, (2 * par, 2 * par + 1), first, last, ends=last)

                f_step(Aff(0), 0)
                f_step(Aff(1), 1)
                if n == 1:
                    rows(1, (2, 3)).then_inc(ada_ps, 1)
                t_step(Aff(0), 0, first=True)
                with pe.Fori(0, 6) as i:
                    for m in range(2):
                        j = Aff(2 + m, i, 2)
                        f_step(j, m)
                        t_step(j - 1, 1 - m)
                for j in range(14, R_STEPS):
                    f_step(Aff(j), j % 2)
                    t_step(Aff(j - 1), (j - 1) % 2)
                t_step(Aff(R_STEPS - 1), 1, last=True)

            norm("relu0")
            relu(0, T_RELU0)
            pe.wait_ge(side_used, U_BC2)
            columns(0, 3, 0)
            columns(1, 3, 8).then_inc(ada_ps, 1)

            norm("gm")
            columns(3, 6, 0)
            rows(2, (4, 5)).then_inc(ada_ps, 1)
            pe.wait_ge(GM["ws_in"], 16)
            pe.wait_ge(xn_ready, 4 * NORM["gm"] + 4)
            for g in range(8):
                last = nc.tensor.transpose(ps[g // 4][:, (g % 4) * P:(g % 4) * P + P], gm_ws[:, g * P:g * P + P], ident)
            last.then_inc(GM["ws_ps"], 1)
            pe.wait_ge(GM["ws"], 2)
            pe.wait_ge(side_used, U_BC2 + 1)
            for c in range(4):
                for m in range(2):
                    t_tile(T_GMV + 2 * c + m, range(4 * m, 4 * m + 4), m == 0, m == 1, x=xn, bank0=2 * c, n=512)

            def gm_u(j, par):
                if j.c >= 2:
                    pe.wait_ge(GM["u"], val(j - 1))
                f_tile(j * 2 + (T_GM - 1) if j.c else Aff(T_GM), par)

            def gm_mix(j, par):
                pe.wait_ge(GM["vs"], val(j + 1))
                if j.c >= 2:
                    pe.wait_ge(GM["t"], val(j - 1))
                for b in range(2):
                    for t in range(TT):
                        c = (2 * b + t) * P
                        last = nc.tensor.matmul(ps[2 + par][:, c:c + P], gm_vs[:, t, b * P:b * P + P],
                                                gm_wst[:, bass.ds(val(j * P), P)], start=True, stop=True)
                last.then_inc(GM["m_ps"], 1)

            def gm_t_step(j, par, first=False, last=False):
                pe.wait_ge(GM["a_ready"], val(j + 1))
                w = j * 2 + (T_GM + 2) if j.c < GM_STEPS - 1 else Aff(T_GM + 2 * GM_STEPS - 1)
                t_tile(w, (2 * par, 2 * par + 1), first, last, ends=last)

            pe.wait_ge(GM["v"], 2)
            gm_u(Aff(0), 0)
            gm_u(Aff(1), 1)
            gm_mix(Aff(0), 0)
            gm_mix(Aff(1), 1)
            gm_t_step(Aff(0), 0, first=True)
            with pe.Fori(0, 2) as i:
                for m in range(2):
                    j = Aff(2 + m, i, 2)
                    gm_u(j, m)
                    gm_mix(j, m)
                    gm_t_step(j - 1, 1 - m)
            for j in range(6, GM_STEPS):
                gm_u(Aff(j), j % 2)
                gm_mix(Aff(j), j % 2)
                gm_t_step(Aff(j - 1), (j - 1) % 2)
            gm_t_step(Aff(GM_STEPS - 1), 1, last=True)
            pe.wait_ge(side_used, U_BC3)
            columns(0, 3, 0).then_inc(ada_ps, 1)

            norm("relu1")
            relu(1, T_RELU1)

        @block.gpsimd
        def _(pool):
            done = [0]

            def chain(ins):
                done[0] += 1
                ins.then_inc(pool_step, 1)
                pool.wait_ge(pool_step, done[0])

            def root(c0, n, parts):
                at = c0
                for c, m, count in parts:
                    chain(nc.gpsimd.tensor_scalar(rs[:, at:at + m], st[:, c:c + m], 1.0 / count, EPS, ALU.mult, ALU.add))
                    at += m
                return nc.gpsimd.tensor_tensor(rstd[:, c0:c0 + n], rs[:, c0:c0 + n], half[:, 0:n], ALU.pow)

            def row_rstd(name):
                for t in range(TT):
                    pool.wait_ge(sq_done, 2 * RSTD[name] + t + 1)
                    c = RCOL[name] + t
                    root(c, 1, [(c, 1, D)]).then_inc(rstd_ready, 1)

            def side_load(s, src, free=None):
                s = s if isinstance(s, Aff) else Aff(s)
                if s.c >= SLOTS:
                    pool.wait_ge(side_used, val(s - (SLOTS - 1)) if free is None else free)
                pool.dma_start(side[:, s.c % SLOTS, :], src).then_inc(side_full[s.c % SLOTS], 16)

            def ada_view(layer, comp, kb):
                v = I["ada_w_2"][layer].rearrange("(k p) (c n) -> p k c n", p=P, c=6)
                return v[:, bass.ds(val(kb), 1), comp, :].rearrange("p k n -> p (k n)")

            def side_loop(u0, layer, comp0, n_comp, trips):
                per = SLOTS // n_comp
                with pool.Fori(0, trips) as i:
                    for m in range(SLOTS):
                        s = Aff(u0 + SLOTS + m, i, SLOTS)
                        pool.wait_ge(side_used, val(s - (SLOTS - 1)))
                        kb = pool.snap(val(Aff(per + m // n_comp, i, per)))
                        pool.dma_start(side[:, s.c % SLOTS, :], ada_view(layer, comp0 + m % n_comp, kb))\
                            .then_inc(side_full[s.c % SLOTS], 16)

            def bias_row(layer, comp):
                return I["ada_b_2"][layer, comp * D:comp * D + D].partition_broadcast(P)

            nc.gpsimd.memset(half[:, :], -0.5).then_inc(half_ready, 1)
            chain(nc.gpsimd.memset(rel[:, :], 1.0))
            pool.dma_start(rel[0:32, :], I["rel_bias"]).then_inc(rb_ready, 16)
            pool.wait_ge(half_ready, 1)
            row_rstd("ev")
            pool.dma_start(onehot, I["onehot"]).then_inc(in_small, 16)
            pool.dma_start(bf[:, :], I["od_b_f"][0].partition_broadcast(P)).then_inc(in_small, 16)
            pool.dma_start(wf[:, :, :], I["od_w_in"][0].rearrange("(k p) n -> p k n", p=P)[:, :, 3 * D:3 * D + 8])\
                .then_inc(in_small, 16)
            pool.dma_start(pe_g[:, 0, :], I["mla_q_norm_2"][0, NOPE:QKD].partition_broadcast(P)).then_inc(in_small, 16)
            pool.dma_start(pe_g[:, 1, :], I["mla_k_norm_2"][0, NOPE:QKD].partition_broadcast(P)).then_inc(in_small, 16)
            nc.gpsimd.memset(acc[:, 0:4, :], 0.0).then_inc(acc_zero, 1)
            for s in range(SLOTS):
                side_load(U_FFN0 + s, ada_view(0, s % 2, s // 2))
            pool.wait_ge(rows_sb, 1)
            pool.dma_start(scratch[:, 0:511], bias_rows).then_inc(rows_out, 16)
            row_rstd("ffn0")
            side_loop(U_FFN0, 0, 0, 2, 3)
            row_rstd("od")
            pool.wait_ge(rows_out, 16)
            pool.wait_ge(mod_ready, 1)
            pool.dma_start(flip, I["consts"][:, C_ALL:]).then_inc(bias_in, 16)
            for t, (c0, c1) in enumerate(SEG):
                src = bass.AP(scratch.tensor, P - P * t, [[1, P], [512, 8], [1, c1 - c0]])
                pool.dma_start(t5_bias[:, :, c0:c1], src).then_inc(bias_in, 16)
            for c in range(SLOTS):
                side_load(U_FFN1 + c, ada_view(0, 2 + c, 0))
            pool.wait_ge(AT["a_ready"], HEADS)
            nc.gpsimd.memset(acc[:, 0:4, :], 0.0).then_inc(acc_zero, 1)
            row_rstd("ffn1")
            pool.wait_ge(xt_ps, 4 * NORM["ffn1"] + 4)
            pool.dma_start(hs, I["ctx_2"][0].rearrange("(t p) d -> p t d", p=P)).then_inc(ctx_in, 16)
            row_rstd("ctx")
            side_loop(U_FFN1, 0, 2, 4, 7)
            side_load(U_BC1, I["final_norm_g"].partition_broadcast(P))
            side_load(U_BC1 + 1, bias_row(0, 2))
            side_load(U_BC1 + 2, bias_row(0, 5))
            row_rstd("final")
            row_rstd("lat")
            pool.wait_ge(LA["lsq"], 10)
            root(20, 6, [(48, 4, KVL), (52, 2, QL)]).then_inc(LA["lrstd"], 1)
            for c in range(SLOTS):
                side_load(U_RELU0 + c, ada_view(1, c, 0))
            for i in range(MH):
                pool.wait_ge(LA["a_sq"], 6 * i + 6)
                chain(nc.gpsimd.tensor_tensor(rs[:, 28:32], st[:, 72:76], st[:, 64:68], ALU.add))
                chain(nc.gpsimd.tensor_scalar(rs[:, 28:32], rs[:, 28:32], 1.0 / QKD, EPS, ALU.mult, ALU.add))
                chain(nc.gpsimd.tensor_scalar(rs[:, 32:34], st[:, 76:78], 1.0 / QKD, EPS, ALU.mult, ALU.add))
                nc.gpsimd.tensor_tensor(rstd[:, 28:34], rs[:, 28:34], half[:, 0:6], ALU.pow).then_inc(LA["a_rstd"], 1)
            row_rstd("relu0")
            pool.wait_ge(h_ready, H_READY["relu0"] + 2)
            nc.gpsimd.memset(acc[:, 0:4, :], 0.0).then_inc(acc_zero, 1)
            side_loop(U_RELU0, 1, 0, 4, 7)
            side_load(U_BC2, bias_row(1, 2))
            for c, name in enumerate(("gm_ln_g_2", "gm_ln_b_2")):
                side_load(U_BC2 + 1 + c, I[name][0, 0:1024].partition_broadcast(P))
            pool.wait_ge(h_ready, H_READY["gm"] + 2)
            pool.dma_start(gm_ws.rearrange("p (g q) -> p g q", g=8), I["gm_ws_2"][0].rearrange("g p q -> p g q")).then_inc(GM["ws_in"], 16)
            row_rstd("gm")
            for c, name in enumerate(("gm_ln_g_2", "gm_ln_b_2")):
                side_load(U_BC2 + 3 + c, I[name][0, 1024:2048].partition_broadcast(P))
            pool.wait_ge(mod_ready, 3)
            nc.gpsimd.memset(acc[:, 0:2, :], 0.0).then_inc(acc_zero, 1)
            pool.wait_ge(xn_ready, 4 * NORM["gm"] + 4)
            pool.dma_start(gm_bs, I["gm_bs_2"][0].rearrange("g p -> (g p)").partition_broadcast(P)).then_inc(GM["bs_in"], 16)
            pool.wait_ge(GM["norm"], 1)
            root(36, 2, [(60, 2, GMH)]).then_inc(GM["rstd"], 1)
            for c in range(SLOTS):
                side_load(U_GM + c, ada_view(1, 4 + c % 2, c // 2))
            side_loop(U_GM, 1, 4, 2, 3)
            side_load(U_BC3, bias_row(1, 5))
            row_rstd("relu1")


_INS = ["x", "mix_norm_g", "ffn_norm_g", "final_norm_g", "ev_w_in", "ev_conv_w", "ev_pool_w", "ev_pool_scale", "ev_w_out",
        "od_w_in", "od_b_f", "od_w_out", "rel_bias", "ffn_w_in", "ffn_conv_w", "ffn_conv_b", "ffn_w_out", "c_2", "ctx_2",
        "c_ctx_2", "ada_w_2", "ada_b_2", "norm_mix_g_2", "norm_ffn_g_2", "mla_wq_a_2", "mla_q_a_norm_2", "mla_wq_b_2",
        "mla_wkv_a_2", "mla_kv_a_norm_2", "mla_wkv_b_2", "mla_q_norm_2", "mla_k_norm_2", "mla_wo_2", "gm_w_in_2",
        "gm_ln_g_2", "gm_ln_b_2", "gm_ws_2", "gm_bs_2", "gm_w_out_2", "ffn_w1_2", "ffn_w2_2"]


def constants():
    import math

    import numpy as np

    c = np.zeros((P, C_ALL + P), np.float32)
    i = np.arange(P)
    c[:, C_ID:C_ID + P] = np.eye(P)
    c[:, C_ALL:] = np.eye(P)[::-1]
    c[:, C_U:C_U + P] = i[:, None] <= i[None, :]
    c[:, C_U + P:C_U + 2 * P] = 1.0
    c[:, C_MASK:C_MASK + P] = np.where(i[None, :] <= i[:, None], 0.0, NEG)
    for g in range(4):
        c[:, C_TAB + 16 * g:C_TAB + 16 * g + 16] = 1.0 / np.minimum(np.arange(16) + 1, 2 << g)
    half = ROPE // 2
    grid_w, theta = 64, 10000.0
    pos = np.arange(S)
    inv = (np.float32(theta) ** (-np.arange(0, half, 2, dtype=np.float32) / np.float32(half))).astype(np.float32)
    ang_r = (pos // grid_w).astype(np.float32)[:, None] * inv[None, :]
    ang_c = (pos % grid_w).astype(np.float32)[:, None] * inv[None, :]
    ang = np.concatenate([ang_r, ang_r, ang_c, ang_c], axis=-1).astype(np.float32)
    sign = np.tile(np.repeat([-1.0, 1.0], half // 2), 2)
    c[:, C_COS:C_COS + P] = np.cos(ang).reshape(TT, P, ROPE).transpose(1, 0, 2).reshape(P, P)
    c[:, C_SIN:C_SIN + P] = (np.sin(ang) * sign).reshape(TT, P, ROPE).transpose(1, 0, 2).reshape(P, P)

    buckets, far, exact = 32, 128, 16
    hot = np.zeros((33, 511), np.float32)
    for m in range(511):
        d = 255 - m
        if d < 0:
            hot[32, m] = NEG
        elif d < exact:
            hot[d, m] = 1.0
        else:
            b = exact + int(np.float32(np.log(np.float32(d) / np.float32(exact))) / np.float32(math.log(far / exact))
                            * np.float32(buckets - exact))
            hot[min(b, buckets - 1), m] = 1.0
    return c, hot


def kernel(**inputs):
    import numpy as _np
    import concourse.bacc as _bacc
    from concourse.bass_utils import run_bass_kernel_spmd as _run

    nc = _bacc.Bacc("TRN2", target_bir_lowering=False, num_devices=1)
    arrays, views = {}, {}

    def give(name, a):
        arrays[f"in_{name}"] = a
        views[name] = nc.dram_tensor(f"in_{name}", a.shape, mybir.dt.from_np(a.dtype), kind="ExternalInput").ap()

    for name in _INS:
        give(name, _np.ascontiguousarray(inputs[name]))
    consts, onehot = constants()
    give("consts", consts)
    give("onehot", onehot)
    out = nc.dram_tensor("out_0", (1, S, D), mybir.dt.from_np(_np.dtype("float32")), kind="ExternalOutput").ap()
    build(nc, views, out)
    r = _run(nc, [arrays], core_ids=[0])
    return r.results[0]["out_0"]
```

```python
from contextlib import ExitStack

import concourse.bass as bass
from concourse import mybir

F32 = mybir.dt.float32
F32R = mybir.dt.float32r
ALU = mybir.AluOpType
ACT = mybir.ActivationFunctionType
AX = mybir.AxisListType

P = 128
S = 256
TT = S // P
D = 1024
KB = D // P
FF = 2816
FFB = FF // P
HID = 4096
GMH = 2048
EPS = 1e-6
SLOTS = 4
SLOT_W = 2048
HD = 64
HEADS = 16
FOX = 8
MH = 8
NOPE, ROPE, VD = 128, 64, 128
QKD = NOPE + ROPE
QL, KVL = 384, 256
CTX = 256
KT = (CTX + S) // P
NEG = -1e30

C_ID, C_U, C_MASK, C_TAB, C_COS, C_SIN = 0, 128, 384, 512, 576, 704
C_ALL = 832
ROWS = [("mix_norm_g", 16), ("ffn_norm_g", 16), ("ev_conv_w", 12), ("ev_pool_scale", 4), ("ffn_conv_w", 132),
        ("ffn_conv_b", 44), ("norm_mix_g_2", 16), ("norm_ffn_g_2", 16), ("c_2", 8), ("c_ctx_2", 8),
        ("mla_q_a_norm_2", 3), ("mla_kv_a_norm_2", 2), ("mla_q_norm_2", 1), ("mla_k_norm_2", 1),
        ("ada_b_2", 96)]
ROW = {}
_n = 0
for _name, _k in ROWS:
    ROW[_name] = _n
    _n += _k
N_ROWS = _n
ROW_TILES = -(-N_ROWS // P)
N_ROW_DMAS = sum((ROW[_name] + _k - 1) // P - ROW[_name] // P + 1 for _name, _k in ROWS)


class Aff:

    def __init__(self, c, reg=None, k=0):
        self.c, self.reg, self.k = c, reg, k

    def __add__(self, n):
        return Aff(self.c + n, self.reg, self.k)

    def __sub__(self, n):
        return self + (-n)

    def __mul__(self, n):
        return Aff(self.c * n, self.reg, self.k * n)


def val(x):
    if not isinstance(x, Aff):
        return x
    return x.c if x.reg is None else x.reg * x.k + x.c


def build(nc, I, out):
    ctx = ExitStack()
    with ctx:
        def sb(name, shape, dt=F32):
            return ctx.enter_context(nc.sbuf_tensor(name, shape, dt))

        def sem(name):
            return ctx.enter_context(nc.semaphore(name))

        raw = [sb(f"raw{i}", [P, SLOT_W]) for i in range(SLOTS)]
        w_hi = [sb(f"w_hi{i}", [P, SLOT_W], F32R) for i in range(SLOTS)]
        w_lo = [sb(f"w_lo{i}", [P, SLOT_W], F32R) for i in range(SLOTS)]
        xn_hi, xn_lo = sb("xn_hi", [P, KB * S], F32R), sb("xn_lo", [P, KB * S], F32R)
        a_hi, a_lo = sb("a_hi", [P, KB * S], F32R), sb("a_lo", [P, KB * S], F32R)
        h = sb("h", [P, TT, D])
        side = sb("side", [P, SLOTS, 1024])
        acc = sb("acc", [P, 5, 1024])
        work = sb("work", [P, 7424])
        cst = sb("cst", [P, C_ALL])
        vec = sb("vec", [P, ROW_TILES * P])
        st = sb("st", [P, 88])
        mod = sb("mod", [P, 48])
        cs = sb("cs", [P, 16])
        pe_g = sb("pe_g", [P, 2, ROPE])
        bf = sb("bf", [P, 8])
        wf = sb("wf", [P, KB, 8])
        zf = sb("zf", [P, 5, 16])
        rs = sb("rs", [P, 40])
        rstd = sb("rstd", [P, 40])
        half = sb("half", [P, 8])
        rel = sb("rel", [33, 8])
        ps = [ctx.enter_context(nc.psum_tensor(f"ps{i}", [P, 512], F32)) for i in range(8)]

        ident = cst[:, C_ID:C_ID + P]
        tri_ones = cst[:, C_U:C_U + 2 * P]
        ones = cst[:, C_U + P:C_U + 2 * P]
        causal = cst[:, C_MASK:C_MASK + P]
        pool_tab = cst[:, C_TAB:C_TAB + 64].rearrange("p (g t) -> p g t", g=4)
        cos = cst[:, C_COS:C_COS + P].rearrange("p (t d) -> p t d", t=TT)
        sin = cst[:, C_SIN:C_SIN + P].rearrange("p (t d) -> p t d", t=TT)

        def wk(a, n):
            return work[:, a:a + n]

        hs = wk(0, 2048).rearrange("p (t d) -> p t d", t=TT)
        xf = wk(4096, 2048).rearrange("p (k t) -> p k t", k=KB)
        xn_hi3 = xn_hi[:, :].rearrange("p (k t) -> p k t", k=KB)
        xn_lo3 = xn_lo[:, :].rearrange("p (k t) -> p k t", k=KB)
        a_hi3 = a_hi[:, :].rearrange("p (k t) -> p k t", k=KB)
        a_lo3 = a_lo[:, :].rearrange("p (k t) -> p k t", k=KB)

        def col(name, n=0):
            c = ROW[name] + n
            return vec[:, c:c + 1]

        def vcol(name, n):
            return vec[:, bass.ds(val(n + ROW[name]), 1)]

        scratch = nc.dram_tensor("bias_rows", (8, 512), F32, kind="Internal").ap()

        def kview(w):
            return w.rearrange("(k p) n -> p k n", p=P)

        def f_src(w, c0=0, stride=256, n=256):
            v = kview(w)
            return lambda j: v[:, :, bass.ds(val(j * stride + c0), n)]

        def t_src(w, n):
            v = kview(w)
            return lambda j: v[:, bass.ds(val(j * n), n), :]

        width, straight = [], {}

        def add(src, kb, n, at=0):
            width.append(sum(k * m for _, k, m, _ in (src if isinstance(src, list) else [(0, kb, n, 0)])))
            straight[len(width) - 1] = src if isinstance(src, list) else [(src, kb, n, at)]

        ev_w = I["ev_w_in"][0]
        T_EV = len(width)
        EV_COLS = [1536, 1792, 512, 1024, 0, 768, 1280, 256]
        for c0 in EV_COLS:
            add(f_src(ev_w, c0), KB, 256)
        T_POOL = len(width)
        pool_v = I["ev_pool_w"][0].rearrange("g c d -> c g d")
        add(lambda j: pool_v, 4, P)
        T_EVO = len(width)
        for j in range(4):
            add(t_src(I["ev_w_out"][0], 2), 2, D, j)

        G_STEPS = FFB // 2

        def gated_sources(layer):
            w, wo = I["ffn_w_in"][layer], I["ffn_w_out"][layer]
            return f_src(w), f_src(w, FF), t_src(wo, 1)

        def add_gated(layer):
            u, g, t = gated_sources(layer)
            base = len(width)
            for j in range(G_STEPS + 1):
                if j < G_STEPS:
                    add(u, KB, 256, j)
                    add(g, KB, 256, j)
                if j:
                    add(t, 1, D, 2 * j - 2)
                    add(t, 1, D, 2 * j - 1)
            return base

        R_STEPS = HID // 256

        def relu_sources(layer):
            return f_src(I["ffn_w1_2"][layer]), t_src(I["ffn_w2_2"][layer], 2)

        def add_paired(f, t, steps):
            base = len(width)
            for j in range(steps + 1):
                if j < steps:
                    add(f, KB, 256, j)
                if j:
                    add(t, 2, D, j - 1)
            return base

        T_FFN0 = add_gated(0)
        od_w = I["od_w_in"][0]
        T_QK = len(width)
        for j in range(8):
            add(f_src(od_w), KB, 256, j)
        T_V = len(width)
        for j in range(4):
            add(t_src(od_w[:, 2 * D:3 * D], 2), 2, D, j)
        T_ODO = len(width)
        for j in range(4):
            add(t_src(I["od_w_out"][0], 2), 2, D, j)
        T_FFN1 = add_gated(1)
        T_LA = len(width)
        kva_v = kview(I["mla_wkv_a_2"][0])
        qa_v = kview(I["mla_wq_a_2"][0])
        for j in range(2):
            add(lambda j: kva_v[:, 4 * j:4 * j + 4, :], 4, KVL + ROPE, j)
        for j in range(2):
            add(lambda j: qa_v[:, 4 * j:4 * j + 4, :], 4, QL, j)
        T_HEAD = len(width)
        kvb_v = kview(I["mla_wkv_b_2"][0])
        qb_v = kview(I["mla_wq_b_2"][0])
        for j in range(MH):
            add([(lambda j: kvb_v[:, :, 256 * j:256 * j + 256], 2, 256, j),
                 (lambda j: qb_v[:, :, QKD * j:QKD * j + QKD], 3, QKD, j)], 0, 0)
        T_WO = len(width)
        for j in range(4):
            add(t_src(I["mla_wo_2"][0], 2), 2, D, j)
        T_RELU0 = add_paired(*relu_sources(0), R_STEPS)
        T_GMV = len(width)
        gm_w = I["gm_w_in_2"][0]
        gmv_v = kview(gm_w)
        for j in range(8):
            add(lambda j: gmv_v[:, 4 * (j % 2):4 * (j % 2) + 4, GMH + 512 * (j // 2):GMH + 512 * (j // 2) + 512],
                4, 512, j)
        GM_STEPS = GMH // 256
        T_GM = add_paired(f_src(gm_w), t_src(I["gm_w_out_2"][0], 2), GM_STEPS)
        T_RELU1 = add_paired(*relu_sources(1), R_STEPS)
        N_TILES = len(width)

        GM_BANK = [6, 0, 2, 4]

        LOOP0, LOOP1 = 2, 10
        TRIPS = (LOOP1 - LOOP0) // 2

        U_FFN0 = 0
        U_FFN1 = U_FFN0 + 16
        U_BC1 = U_FFN1 + 32
        U_RELU0 = U_BC1 + 3
        U_BC2 = U_RELU0 + 32
        U_GM = U_BC2 + 5
        U_BC3 = U_GM + 16

        raw_full = [sem(f"raw_full{i}") for i in range(SLOTS)]
        hi_done, lo_done, w_used = sem("hi_done"), sem("lo_done"), sem("w_used")
        side_full = [sem(f"side_full{i}") for i in range(SLOTS)]
        side_used = sem("side_used")
        in_h, in_cst, in_rows, in_small = sem("in_h"), sem("in_cst"), sem("in_rows"), sem("in_small")
        vec_ps, vec_ready, cs_ready = sem("vec_ps"), sem("vec_ready"), sem("cs_ready")
        rb_ready, half_ready, rows_ps, rows_sb, rows_out = sem("rb_ready"), sem("half_ready"), sem("rows_ps"), sem("rows_sb"), sem("rows_out")
        bias_in, ctx_in = sem("bias_in"), sem("ctx_in")
        h_ready, sq_done, rstd_ready = sem("h_ready"), sem("sq_done"), sem("rstd_ready")
        hs_ready, xt_ps, xf_ready = sem("hs_ready"), sem("xt_ps"), sem("xf_ready")
        xhi_done, xn_ready = sem("xhi_done"), sem("xn_ready")
        acc_zero, ada_ps, mod_ready = sem("acc_zero"), sem("ada_ps"), sem("mod_ready")
        all_out, gated_sum = sem("all_out"), sem("gated_sum")
        tok0_done = sem("tok0_done")
        dve_step, pool_step = sem("dve_step"), sem("pool_step")

        def group(prefix, *names):
            return {n: sem(f"{prefix}_{n}") for n in names}

        EV = group("ev", "gate", "prod", "tap2", "tap1", "conv", "y", "yhi", "a_ready", "pin", "pool", "phi",
                   "pool_ready", "pool_a", "ybf", "ybhi")
        FFN = [group(f"ffn{n}", "a0", "tap", "conv", "silu", "prod", "ahi", "a_ready") for n in range(2)]
        RELU = [group(f"relu{n}", "relu", "sq", "ahi", "a_ready") for n in range(2)]
        AT = group("at", "qk", "v_sb", "v_act", "z_ps", "z", "nabs", "ez", "ln", "neg", "f_ps", "f", "lbc", "s_ps", "s_sb",
                   "max", "exp", "rec", "p", "t_ps", "pt", "o_ps", "ohi", "a_ready")
        LA = group("la", "kv_sb", "q_sb", "ksq", "qsq", "psq", "krstd", "qrstd", "kscaled", "qscaled", "lt_ps", "lxf", "lhi", "l_ready", "a_ps", "a_sq",
                   "head_q", "values", "a_rstd", "kn", "qpe", "kq_ps", "kq", "s_ps", "max", "exp", "rec", "p", "t_ps", "pt_a", "pt_d",
                   "o_ps", "ohi", "a_ready")
        GM = group("gm", "v", "mu", "sq", "rstd", "norm", "gain", "ws_in", "ws_ps", "ws", "bs_in", "u", "vs", "m_ps",
                   "t", "prod", "ahi", "a_ready")

        block = ctx.enter_context(nc.Block())

        NORM = {n: k for k, n in enumerate(
            ["ev", "ffn0", "od", "ffn1", "ctx", "lat", "relu0", "gm", "relu1"])}
        H_READY = {"ffn0": 0, "od": 2, "ffn1": 4, "final": 6, "lat": 8, "relu0": 10, "gm": 12, "relu1": 14, "out": 16}
        RSTD = {n: k for k, n in enumerate(
            ["ev", "ffn0", "od", "ffn1", "ctx", "final", "lat", "relu0", "gm", "relu1"])}
        RCOL = dict({n: 2 * k for n, k in NORM.items()}, final=18)
        RESIDUAL = {n: k for k, n in enumerate(["ffn0", "od", "ffn1", "final", "relu0", "gm", "relu1", "out"])}
        MOD_COUNT = {"ctx": 1, "lat": 1, "relu0": 2, "gm": 3, "relu1": 4}

        @block.sync
        def _(sp):
            sp.dma_start(h[:, :, :], I["x"][0].rearrange("(t p) d -> p t d", p=P)).then_inc(in_h, 16)

            def load(t):
                if t >= SLOTS:
                    sp.wait_ge(lo_done, t - SLOTS + 1)
                at, parts = 0, straight[t]
                for src, k, n, j in parts:
                    dst = raw[t % SLOTS][:, at:at + k * n].rearrange("p (k n) -> p k n", k=k)
                    sp.dma_start(dst, src(j)).then_inc(raw_full[t % SLOTS], 16)
                    at += k * n

            def load_gated(layer, base):
                u, g, w = gated_sources(layer)
                first = base + 4 * LOOP0 - 2
                for t in range(base, first):
                    load(t)
                with sp.Fori(0, LOOP1 - LOOP0) as i:
                    j = Aff(LOOP0, i, 1)
                    views = [(u(j), KB, 256), (g(j), KB, 256), (w(j * 2 - 2), 1, D), (w(j * 2 - 1), 1, D)]
                    free = [sp.snap(val(j * 4 + (base - 2 + m - SLOTS + 1))) for m in range(4)]
                    for m, (src, k, n) in enumerate(views):
                        s = (first + m) % SLOTS
                        sp.wait_ge(lo_done, free[m])
                        sp.dma_start(raw[s][:, 0:k * n].rearrange("p (k n) -> p k n", k=k), src)\
                            .then_inc(raw_full[s], 16)
                for t in range(base + 4 * LOOP1 - 2, base + 4 * G_STEPS):
                    load(t)

            def load_paired(f, w, base, steps, loop0, loop1):
                first = base + 2 * loop0 - 1
                for t in range(base, first):
                    load(t)
                with sp.Fori(0, (loop1 - loop0) // 2) as i:
                    js = [Aff(loop0 + m, i, 2) for m in range(2)]
                    views = []
                    for j in js:
                        views += [(f(j), KB, 256), (w(j - 1), 2, D)]
                    free = [sp.snap(val(js[0] * 2 + (base - 1 + m - SLOTS + 1))) for m in range(4)]
                    for m, (src, k, n) in enumerate(views):
                        s = (first + m) % SLOTS
                        sp.wait_ge(lo_done, free[m])
                        sp.dma_start(raw[s][:, 0:k * n].rearrange("p (k n) -> p k n", k=k), src)\
                            .then_inc(raw_full[s], 16)
                for t in range(base + 2 * loop1 - 1, base + 2 * steps):
                    load(t)

            load(T_EV)
            at = 0
            stage = wk(6144, ROW_TILES * P).rearrange("p (r c) -> p r c", r=ROW_TILES)
            for name, n in ROWS:
                src = I[name]
                if name.endswith(("q_norm_2", "k_norm_2")):
                    src = src[0:1, 0:P]
                else:
                    while len(src.shape) > 1:
                        src = src.rearrange("a b -> (a b)") if len(src.shape) == 2 else src.rearrange("a b c -> (a b c)")
                    src = src.rearrange("(r c) -> r c", c=P)
                done = 0
                while done < n:
                    m = min(n - done, P - (at % P))
                    sp.dma_start(stage[at % P:at % P + m, at // P, :], src[done:done + m, :]).then_inc(in_rows, 16)
                    done, at = done + m, at + m
            for t in range(T_EV + 1, T_FFN0):
                load(t)
            load_gated(0, T_FFN0)
            for t in range(T_QK, T_FFN1):
                load(t)
            load_gated(1, T_FFN1)
            for t in range(T_LA, T_RELU0):
                load(t)
            load_paired(*relu_sources(0), T_RELU0, R_STEPS, 2, 14)
            for t in range(T_GMV, T_GM):
                load(t)
            load_paired(f_src(gm_w), t_src(I["gm_w_out_2"][0], 2), T_GM, GM_STEPS, 2, 6)
            load_paired(*relu_sources(1), T_RELU1, R_STEPS, 2, 14)
            out_v = out[0].rearrange("(t p) d -> p t d", p=P)
            for t in range(TT):
                sp.wait_ge(h_ready, H_READY["out"] + t + 1)
                sp.dma_start(out_v[:, t, :], h[:, t, :]).then_inc(all_out, 16)
            sp.wait_ge(all_out, 16 * TT)
            sp.wait_ge(rows_out, 16)

        landed = []
        per_slot = [0] * SLOTS
        for t in range(N_TILES):
            per_slot[t % SLOTS] += 16 * len(straight[t])
            landed.append(per_slot[t % SLOTS])

        @block.scalar
        def _(act):
            def split(t):
                t = t if isinstance(t, Aff) else Aff(t)
                if t.c >= N_TILES:
                    return
                s, w = t.c % SLOTS, width[t.c]
                act.wait_ge(raw_full[s], val(Aff(landed[t.c], t.reg, t.k * 16 // SLOTS)))
                if t.c >= SLOTS:
                    act.wait_ge(w_used, val(t - (SLOTS - 1)))
                nc.scalar.activation(w_hi[s][:, 0:w], raw[s][:, 0:w], ACT.Copy).then_inc(hi_done, 1)

            act.dma_start(cst[:, :], I["consts"][:, 0:C_ALL]).then_inc(in_cst, 16)

            def squares(name, src):
                for t in range(TT):
                    if name == "ctx":
                        act.wait_ge(ctx_in, 16)
                    elif name == "ev":
                        act.wait_ge(in_h, 16)
                    else:
                        act.wait_ge(h_ready, H_READY[name] + t + 1)
                    c = RCOL[name] + t
                    junk = wk(4096 + D * t, D) if name in ("ctx", "final") else hs[:, t, :]
                    nc.scalar.activation(junk, src[:, t, :], ACT.Square, accum_out=st[:, c:c + 1]).then_inc(sq_done, 1)

            def gains(name, gain, shift=None):
                k = NORM[name]
                if name in MOD_COUNT:
                    act.wait_ge(mod_ready, MOD_COUNT[name])
                if name == "ev":
                    act.wait_ge(vec_ready, 1)
                for i in range(4):
                    act.wait_ge(xt_ps, 4 * k + i + 1)
                    for m in range(2):
                        b = 2 * i + m
                        if shift is None:
                            last = nc.scalar.activation(xf[:, b, :], ps[i][:, m * S:m * S + S], ACT.Copy, scale=gain(b))
                        else:
                            last = nc.scalar.activation(xf[:, b, :], ps[i][:, m * S:m * S + S], ACT.Identity,
                                                        scale=gain(b), bias=shift(b))
                    last.then_inc(xf_ready, 1)

            def norm(name, src, gain, shift=None, late=None):
                squares(name, src)
                if late is not None:
                    split(late)
                gains(name, gain, shift)

            squares("ev", h)
            split(T_EV)
            gains("ev", lambda b: col("mix_norm_g", b))
            split(T_EV + 1)
            split(T_EV + 2)
            split(T_EV + 3)
            nc.scalar.activation(cs[:, :], vec[:, ROW["c_2"]:ROW["c_2"] + 16], ACT.Silu).then_inc(cs_ready, 1)

            ev_c = wk(6144, 512)
            ev_cv = wk(2048, 2 * 258).rearrange("p (b t) -> p b t", b=2)
            ev_a = wk(6656, 512).rearrange("p (b t) -> p b t", b=2)
            ev_y = wk(0, 512)
            ev_u = wk(2564, 4 * 272).rearrange("p (g t) -> p g t", g=4)
            for m in range(2):
                act.wait_ge(w_used, T_EV + m + 1)
                if m == 0:
                    act.wait_ge(EV["pin"], 1)
                nc.scalar.activation(ev_u[:, 2 * m:2 * m + 2, 16:272], ps[m][:, :].rearrange("p (g t) -> p g t", g=2), ACT.Copy)\
                    .then_inc(EV["pool"], 1)
                split(T_EV + m + 4)
            for m in range(2):
                t = T_EV + 2 + 3 * m
                act.wait_ge(w_used, t + 1)
                nc.scalar.activation(ev_c, ps[(2 + 3 * m) % 4][:, :], ACT.Copy).then_inc(EV["gate"], 1)
                split(t + 4)
                act.wait_ge(EV["prod"], m + 1)
                for b in range(2):
                    nc.scalar.activation(ev_a[:, b, :], ev_cv[:, b, 2:258], ACT.Copy,
                                         scale=col("ev_conv_w", 8 + 2 * m + b)).then_inc(EV["tap2"], 1)
                split(t + 5)
                if m == 0:
                    act.wait_ge(EV["pool_ready"], 1)
                    nc.scalar.activation(a_hi[:, 1024:2048], wk(1024, 1024), ACT.Copy).then_inc(EV["phi"], 1)
                split(t + 6)
                act.wait_ge(EV["y"], m + 1)
                nc.scalar.activation(a_hi[:, 512 * m:512 * m + 512], ev_y, ACT.Copy).then_inc(EV["yhi"], 1)
            act.wait_ge(w_used, T_POOL + 1)
            for m in range(2):
                for g in range(2):
                    nc.scalar.activation(wk(1024 + (2 * m + g) * S, S), ps[m][:, g * S:g * S + S],
                                         ACT.Copy, scale=col("ev_pool_scale", 2 * m + g)).then_inc(EV["ybf"], 1)
            act.wait_ge(EV["ybf"], 4)
            nc.scalar.activation(a_hi[:, 1024:2048], wk(1024, 1024), ACT.Copy).then_inc(EV["ybhi"], 1)
            split(T_POOL + 4)
            for j in range(3):
                split(T_EVO + j + 4)

            f_a0 = wk(6144, 512).rearrange("p (b t) -> p b t", b=2)
            f_s, f_p = wk(6656, 512), wk(2048, 512)

            def gated(n, base):
                g = FFN[n]

                def step(j, par):
                    u = j * 4 + (base - 2) if j.c else Aff(base)
                    act.wait_ge(w_used, val(u + 1))
                    for b in range(2):
                        nc.scalar.activation(f_a0[:, b, :], ps[0][:, b * S:b * S + S], ACT.Identity,
                                             scale=vcol("ffn_conv_w", j * 2 + (n * 3 * FFB + 2 * FFB + b)),
                                             bias=vcol("ffn_conv_b", j * 2 + (n * FFB + b))).then_inc(g["a0"], 1)
                    split(u + 4)
                    act.wait_ge(g["conv"], val(j * 2 + 2))
                    nc.scalar.activation(f_s, wk(6144, 512), ACT.Silu).then_inc(g["silu"], 1)
                    split(u + 5)
                    act.wait_ge(g["prod"], val(j + 1))
                    nc.scalar.activation(a_hi[:, par * 512:par * 512 + 512], f_p, ACT.Copy).then_inc(g["ahi"], 1)
                    if j.c:
                        split(u + 6)
                        split(u + 7)

                for j in range(LOOP0):
                    step(Aff(j), j % 2)
                if n == 1:
                    squares("ctx", hs)
                with act.Fori(0, TRIPS) as i:
                    for m in range(2):
                        step(Aff(LOOP0 + m, i, 2), m)
                for j in range(LOOP1, G_STEPS):
                    step(Aff(j), j % 2)
                if n == 1:
                    gains("ctx", lambda b: mod[:, 8 + b:9 + b], lambda b: mod[:, b:b + 1])
                split(base + 4 * G_STEPS + 2)

            norm("ffn0", h, lambda b: col("ffn_norm_g", b), late=T_FFN0 + 3)
            gated(0, T_FFN0)

            norm("od", h, lambda b: col("mix_norm_g", 8 + b), late=T_QK + 3)
            for j in range(8):
                act.wait_ge(w_used, T_QK + j + 1)
                nc.scalar.activation(wk(512 * j, 512), ps[j % 4][:, :], ACT.Copy, scale=HD ** -0.5 if j < 4 else 1.0)\
                    .then_inc(AT["qk"], 1)
                split(T_QK + j + 4)
                if j == 0:
                    act.wait_ge(AT["nabs"], 1)
                    nc.scalar.activation(zf[:, 1, :], zf[:, 1, :], ACT.Exp).then_inc(AT["ez"], 1)
                    act.wait_ge(AT["ez"], 1)
                    nc.scalar.activation(zf[:, 1, :], zf[:, 1, :], ACT.Ln, bias=1.0).then_inc(AT["ln"], 1)
            at_s = wk(6144, 768).rearrange("p (b k) -> p b k", b=2)
            at_pt = wk(6912, 384)
            SEG = [(0, P), (P, 3 * P)]

            def at_exp(i):
                act.wait_ge(AT["max"], 2 * i + 2)
                src = at_s[:, i % 2, :] if i < FOX else ps[i % 2]
                for t, (c0, c1) in enumerate(SEG):
                    nc.scalar.activation(at_s[:, i % 2, c0:c1], src[:, c0:c1], ACT.Exp,
                                         bias=st[:, 32 + 4 * (i % 2) + t:33 + 4 * (i % 2) + t],
                                         accum_out=st[:, 34 + 4 * (i % 2) + t:35 + 4 * (i % 2) + t]).then_inc(AT["exp"], 1)

            at_exp(0)
            at_exp(1)
            for j in range(3):
                split(T_V + j + 4)
            act.wait_ge(w_used, T_V + 4)
            for c in range(2):
                nc.scalar.activation(wk(4096 + 512 * c, 512), ps[4 + c][:, :], ACT.Copy).then_inc(AT["v_act"], 1)
            for i in range(HEADS):
                act.wait_ge(AT["t_ps"], i + 1)
                nc.scalar.activation(at_pt, ps[2 + i % 2][:, 0:384], ACT.Copy).then_inc(AT["pt"], 1)
                if i and i + 1 < HEADS:
                    at_exp(i + 1)
                act.wait_ge(AT["o_ps"], i + 1)
                r = HD * (i % 2)
                nc.scalar.activation(a_hi3[r:r + HD, i // 2, :], ps[4 + i % 2][r:r + HD, 0:S], ACT.Copy).then_inc(AT["ohi"], 1)
            split(T_V + 7)
            for j in range(3):
                split(T_ODO + j + 4)

            norm("ffn1", h, lambda b: col("ffn_norm_g", 8 + b), late=T_FFN1 + 3)
            gated(1, T_FFN1)

            squares("final", h)

            kva = wk(6144, KT * (KVL + ROPE)).rearrange("p (t d) -> p t d", t=KT)
            cq = wk(2048, TT * QL).rearrange("p (t d) -> p t d", t=TT)
            act.wait_ge(LA["a_ps"], 1)
            for t in range(TT):
                nc.scalar.activation(kva[:, t, :], ps[t][:, 0:KVL + ROPE], ACT.Copy).then_inc(LA["kv_sb"], 1)
            norm("lat", h, lambda b: mod[:, 24 + b:25 + b], lambda b: mod[:, 16 + b:17 + b], late=T_LA + 3)

            def kv_squares(t):
                act.wait_ge(LA["kv_sb"], t + 1)
                nc.scalar.activation(wk(KVL * t, KVL), kva[:, t, 0:KVL], ACT.Square, accum_out=st[:, 48 + t:49 + t])\
                    .then_inc(LA["ksq"], 1)

            def rotary_squares(t):
                nc.scalar.activation(wk(KT * KVL + TT * QL + ROPE * t, ROPE), kva[:, t, KVL:], ACT.Square,
                                     accum_out=st[:, 64 + t:65 + t]).then_inc(LA["psq"], 1)

            for t in range(TT):
                kv_squares(t)
                rotary_squares(t)
            act.wait_ge(w_used, T_LA + 2)
            for t in range(TT):
                nc.scalar.activation(kva[:, TT + t, :], ps[6 + t][:, 0:KVL + ROPE], ACT.Copy).then_inc(LA["kv_sb"], 1)
            for t in range(TT, KT):
                kv_squares(t)
            split(T_LA + 4)
            split(T_LA + 5)
            act.wait_ge(w_used, T_LA + 4)
            for t in range(TT):
                nc.scalar.activation(cq[:, t, :], ps[4 + t][:, 0:QL], ACT.Copy).then_inc(LA["q_sb"], 1)
            for t in range(TT):
                act.wait_ge(LA["q_sb"], t + 1)
                nc.scalar.activation(wk(KT * KVL + QL * t, QL), cq[:, t, :], ACT.Square, accum_out=st[:, 52 + t:53 + t])\
                    .then_inc(LA["qsq"], 1)
            for t in range(TT, KT):
                rotary_squares(t)
            lf_kv, lf_q = wk(4096, 1024), wk(5120, 768)
            act.wait_ge(LA["lt_ps"], 1)
            for b in range(2):
                nc.scalar.activation(lf_kv[:, 512 * b:512 * b + 512], ps[6 + b][:, :], ACT.Copy, scale=col("mla_kv_a_norm_2", b))\
                    .then_inc(LA["lxf"], 1)
            act.wait_ge(LA["lt_ps"], 2)
            for b in range(3):
                nc.scalar.activation(lf_q[:, S * b:S * b + S], ps[5 - b // 2][:, S * (b % 2):S * (b % 2) + S], ACT.Copy,
                                     scale=col("mla_q_a_norm_2", b)).then_inc(LA["lxf"], 1)
            split(T_LA + 6)
            split(T_LA + 7)

            la_kta = [wk(512 * p, 512) for p in range(2)]
            la_ktb = [wk(1024 + 512 * p, 512) for p in range(2)]
            la_qt = [wk(2048 + 512 * p, 512) for p in range(2)]
            la_v = [v.rearrange("p (t d) -> p t d", t=KT) for v in (wk(3072, 512), wk(3584, 512), acc[:, 2, 512:1024])]
            la_p = wk(4096, 1024).rearrange("p (t k) -> p t k", t=TT)
            la_pt = wk(5120, 1024)
            la_junk = acc[:, 1, :]

            def la_values(i):
                act.wait_ge(LA["head_q"], i + 1)
                for t in range(TT):
                    nc.scalar.activation(la_junk[:, KT * NOPE + QKD * t:KT * NOPE + QKD * t + QKD], ps[2][:, QKD * t:QKD * t + QKD], ACT.Square,
                                         accum_out=st[:, 76 + t:77 + t]).then_inc(LA["a_sq"], 1)
                act.wait_ge(w_used, T_HEAD + i + 1)
                for t in range(KT):
                    nc.scalar.activation(la_junk[:, NOPE * t:NOPE * t + NOPE], ps[t // 2][:, 256 * (t % 2):256 * (t % 2) + NOPE], ACT.Square,
                                         accum_out=st[:, 72 + t:73 + t]).then_inc(LA["a_sq"], 1)
                for m in range(2):
                    kv2 = ps[m][:, :].rearrange("p (t d) -> p t d", t=2)
                    last = nc.scalar.activation(la_v[i % 3][:, 2 * m:2 * m + 2, :], kv2[:, :, NOPE:], ACT.Copy)
                last.then_inc(LA["values"], 1)
                split(T_HEAD + i + 4)

            def la_transposed(i):
                act.wait_ge(LA["kq_ps"], i + 1)
                p = i % 2
                nc.scalar.activation(la_kta[p], ps[3][:, :], ACT.Copy, scale=col("mla_k_norm_2"))
                nc.scalar.activation(la_ktb[p][0:ROPE, :], ps[0][0:ROPE, :], ACT.Copy)
                nc.scalar.activation(la_qt[p][:, 0:S], ps[1][:, 0:S], ACT.Copy, scale=col("mla_q_norm_2"))
                nc.scalar.activation(la_qt[p][0:ROPE, S:2 * S], ps[1][0:ROPE, S:2 * S], ACT.Copy).then_inc(LA["kq"], 1)

            la_values(0)
            la_transposed(0)
            for i in range(MH + 1):
                if i:
                    act.wait_ge(LA["t_ps"], i)
                    nc.scalar.activation(la_pt[:, 0:512], ps[6][:, :], ACT.Copy).then_inc(LA["pt_a"], 1)
                if i == MH:
                    split(T_WO + 4)
                    split(T_WO + 5)
                if i + 1 < MH:
                    la_values(i + 1)
                if i < MH:
                    act.wait_ge(LA["max"], i + 1)
                    for t in range(TT):
                        nc.scalar.activation(la_p[:, t, :], ps[4 + t][:, :], ACT.Exp, scale=QKD ** -0.5,
                                             bias=st[:, 82 + t:83 + t], accum_out=st[:, 84 + t:85 + t]).then_inc(LA["exp"], 1)
                if i:
                    act.wait_ge(LA["o_ps"], i)
                    nc.scalar.activation(a_hi3[:, i - 1, :], ps[6][:, 0:S], ACT.Copy).then_inc(LA["ohi"], 1)
                if i + 1 < MH:
                    la_transposed(i + 1)
            split(T_WO + 6)

            r_r, r_s = wk(6144, 512), [wk(2048 + 512 * m, 512) for m in range(2)]

            def relu(n, base):
                g = RELU[n]

                def step(j, par):
                    f = j * 2 + (base - 1) if j.c else Aff(base)
                    act.wait_ge(w_used, val(f + 1))
                    nc.scalar.activation(r_r, ps[par][:, :], ACT.Relu).then_inc(g["relu"], 1)
                    split(f + 4)
                    act.wait_ge(g["sq"], val(j + 1))
                    nc.scalar.activation(a_hi[:, par * 512:par * 512 + 512], r_s[par], ACT.Copy).then_inc(g["ahi"], 1)
                    if j.c:
                        split(f + 5)

                for j in range(2):
                    step(Aff(j), j % 2)
                with act.Fori(0, 6) as i:
                    for m in range(2):
                        step(Aff(2 + m, i, 2), m)
                for j in range(14, R_STEPS):
                    step(Aff(j), j % 2)

            norm("relu0", h, lambda b: mod[:, 40 + b:41 + b], lambda b: mod[:, 32 + b:33 + b], late=T_RELU0 + 3)
            relu(0, T_RELU0)

            norm("gm", h, lambda b: mod[:, 24 + b:25 + b], lambda b: mod[:, 16 + b:17 + b], late=T_GMV + 3)
            gm_v = wk(0, 4096).rearrange("p (t d) -> p t d", t=TT)
            for c in range(4):
                act.wait_ge(w_used, T_GMV + 2 * c + 2)
                for t in range(TT):
                    nc.scalar.activation(gm_v[:, t, 512 * c:512 * c + 512], ps[GM_BANK[c] + t][:, :], ACT.Gelu,
                                         accum_out=st[:, 48 + 4 * t + c:49 + 4 * t + c]).then_inc(GM["v"], 1)
                if c < 3:
                    split(T_GMV + 2 * c + 4)
                    split(T_GMV + 2 * c + 5)
            for t in range(TT):
                act.wait_ge(GM["mu"], 1)
                for c in range(4):
                    junk = ps[4 + c][:, :] if t else acc[:, 3 + c // 2, 512 * (c % 2):512 * (c % 2) + 512]
                    nc.scalar.activation(junk, gm_v[:, t, 512 * c:512 * c + 512], ACT.Square,
                                         bias=st[:, 58 + t:59 + t], accum_out=st[:, 64 + 4 * t + c:65 + 4 * t + c])\
                        .then_inc(GM["sq"], 1)
            split(T_GMV + 10)
            split(T_GMV + 11)
            gm_u = wk(6144, 512)
            gm_t = [acc[:, 4, 512 * m:512 * m + 512] for m in range(2)]

            def gm_step(j, par):
                f = j * 2 + (T_GM - 1) if j.c else Aff(T_GM)
                act.wait_ge(w_used, val(f + 1))
                nc.scalar.activation(gm_u, ps[par][:, :], ACT.Gelu).then_inc(GM["u"], 1)
                split(f + 4)
                act.wait_ge(GM["prod"], val(j + 1))
                nc.scalar.activation(a_hi[:, par * 512:par * 512 + 512], gm_t[par], ACT.Copy).then_inc(GM["ahi"], 1)
                if j.c:
                    split(f + 5)

            act.wait_ge(GM["ws"], 2)
            for j in range(2):
                gm_step(Aff(j), j % 2)
            with act.Fori(0, 2) as i:
                for m in range(2):
                    gm_step(Aff(2 + m, i, 2), m)
            for j in range(6, GM_STEPS):
                gm_step(Aff(j), j % 2)

            norm("relu1", h, lambda b: mod[:, 40 + b:41 + b], lambda b: mod[:, 32 + b:33 + b], late=T_RELU1 + 3)
            relu(1, T_RELU1)

        ev_c = wk(6144, 512).rearrange("p (b t) -> p b t", b=2)
        ev_cv = wk(2048, 2 * 258).rearrange("p (b t) -> p b t", b=2)
        ev_a = wk(6656, 512)
        ev_y = wk(0, 512)
        ev_u = wk(2564, 4 * 272).rearrange("p (g t) -> p g t", g=4)
        ev_s0 = wk(4096, 4 * 272).rearrange("p (g t) -> p g t", g=4)
        ev_s1 = wk(5184, 3 * 272).rearrange("p (g t) -> p g t", g=3)
        ev_p = wk(1024, 1024).rearrange("p (g t) -> p g t", g=4)
        onehot = acc[0:33, 4, 0:511]
        bias_rows = acc[0:8, 4, 512:1023]
        t5_bias = acc[:, 0:3, :].rearrange("p a b -> p (a b)").rearrange("p (h k) -> p h k", h=8)
        flip = acc[:, 3, 512:640]
        f_a0 = wk(6144, 512).rearrange("p (b t) -> p b t", b=2)
        f_s, f_p = wk(6656, 512), wk(2048, 512)
        at_qk = wk(0, 4096).rearrange("p (b t) -> p b t", b=16)
        at_v = wk(4096, 2048).rearrange("p (t d) -> p t d", t=TT)
        at_s = wk(6144, 768).rearrange("p (b k) -> p b k", b=2)
        at_pt = wk(6912, 384)
        at_l = acc[:, 4, 0:512].rearrange("p (b t q) -> p b t q", b=2, t=TT)
        kva = wk(6144, KT * (KVL + ROPE)).rearrange("p (t d) -> p t d", t=KT)
        cq = wk(2048, TT * QL).rearrange("p (t d) -> p t d", t=TT)
        lf_kv, lf_q = wk(4096, 1024), wk(5120, 768)
        la_kta = [wk(512 * p, 512) for p in range(2)]
        la_ktb = [wk(1024 + 512 * p, 512) for p in range(2)]
        la_qt = [wk(2048 + 512 * p, 512) for p in range(2)]
        la_v = [v.rearrange("p (t d) -> p t d", t=KT) for v in (wk(3072, 512), wk(3584, 512), acc[:, 2, 512:1024])]
        la_p = wk(4096, 1024).rearrange("p (t k) -> p t k", t=TT)
        la_pt = wk(5120, 1024)
        la_kn = wk(6144, KT * QKD).rearrange("p (t d) -> p t d", t=KT)
        la_qn = wk(6912, TT * QKD).rearrange("p (t d) -> p t d", t=TT)
        la_kpe = acc[:, 2, 0:KT * ROPE].rearrange("p (t d) -> p t d", t=KT)
        la_rot = acc[:, 2, 256:256 + TT * ROPE].rearrange("p (t d) -> p t d", t=TT)
        r_r, r_s = wk(6144, 512), [wk(2048 + 512 * m, 512) for m in range(2)]
        gm_v = wk(0, 4096).rearrange("p (t d) -> p t d", t=TT)
        gm_bs, gm_wst, gm_ws = wk(4096, 1024), wk(5120, 1024), wk(6144, 1024)
        gm_u = wk(6144, 512)
        gm_t = [acc[:, 4, 512 * m:512 * m + 512] for m in range(2)]
        gm_vs = acc[:, 3, 0:512].rearrange("p (t c) -> p t c", t=TT)
        SEG = [(0, P), (P, 3 * P)]

        @block.vector
        def _(dve):
            steps = [0]

            def chain(ins):
                steps[0] += 1
                ins.then_inc(dve_step, 1)
                dve.wait_ge(dve_step, steps[0])

            def split(t):
                t = t if isinstance(t, Aff) else Aff(t)
                if t.c >= N_TILES:
                    return
                s, w = t.c % SLOTS, width[t.c]
                dve.wait_ge(hi_done, val(t + 1))
                nc.vector.tensor_tensor(w_lo[s][:, 0:w], raw[s][:, 0:w], w_hi[s][:, 0:w].bitcast(F32), ALU.subtract)\
                    .then_inc(lo_done, 1)

            def scale(name, src):
                for t in range(TT):
                    dve.wait_ge(rstd_ready, 2 * RSTD[name] + t + 1)
                    c = RCOL[name] + t
                    nc.vector.tensor_scalar(hs[:, t, :], src[:, t, :], rstd[:, c:c + 1], None, ALU.mult).then_inc(hs_ready, 1)

            def take(name):
                k = NORM[name]
                for i in range(4):
                    dve.wait_ge(xf_ready, 4 * k + i + 1)
                    nc.vector.tensor_copy(xn_hi3[:, 2 * i:2 * i + 2, :], xf[:, 2 * i:2 * i + 2, :]).then_inc(xhi_done, 1)
                    dve.wait_ge(xhi_done, 4 * k + i + 1)
                    nc.vector.tensor_tensor(xn_lo3[:, 2 * i:2 * i + 2, :], xf[:, 2 * i:2 * i + 2, :],
                                            xn_hi3[:, 2 * i:2 * i + 2, :].bitcast(F32), ALU.subtract).then_inc(xn_ready, 1)

            def norm(name, src, late=()):
                scale(name, src)
                take(name)
                for t in late:
                    split(t)

            products = [0]

            def residual(name, last, gate=None, bank0=4):
                for t in range(TT):
                    if t == 0:
                        dve.wait_ge(tok0_done, RESIDUAL[name] + 1)
                    else:
                        dve.wait_ge(w_used, last + 1)
                    parts = [ps[bank0 + 2 * t + c][:, :] for c in range(2)]
                    if gate is not None:
                        for c in range(2):
                            tmp = wk(4096 + D * t + 512 * c, 512)
                            nc.vector.tensor_tensor(tmp, parts[c], gate[:, 512 * c:512 * c + 512], ALU.mult).then_inc(gated_sum, 1)
                            parts[c] = tmp
                    for c in range(2):
                        if gate is not None:
                            products[0] += 1
                            dve.wait_ge(gated_sum, products[0])
                        hv = h[:, t, 512 * c:512 * c + 512]
                        add = nc.vector.tensor_tensor(hv, parts[c], hv, ALU.add)
                    add.then_inc(h_ready, 1)

            def ada(s, slot, kb, also=None):
                s = s if isinstance(s, Aff) else Aff(s)
                tile = side[:, s.c % SLOTS, :]
                dve.wait_ge(side_full[s.c % SLOTS], val(Aff(16 * (s.c // SLOTS + 1), s.reg, s.k * 4)))
                if also is not None:
                    nc.vector.scalar_tensor_tensor(acc[:, also, :], tile, cs[:, bass.ds(val(kb + 8), 1)], acc[:, also, :],
                                                   ALU.mult, ALU.add)
                nc.vector.scalar_tensor_tensor(acc[:, slot, :], tile, cs[:, bass.ds(val(kb), 1)], acc[:, slot, :],
                                               ALU.mult, ALU.add).then_inc(side_used, 1)

            def bias_cols(layer, comp):
                c = ROW["ada_b_2"] + 48 * layer + 8 * comp
                return vec[:, c:c + 8]

            def shift_cols(dst, sums, layer, comp):
                return nc.vector.tensor_tensor(mod[:, dst:dst + 8], sums, bias_cols(layer, comp), ALU.add)

            def gain_cols(dst, sums, layer, comp, g):
                chain(shift_cols(dst, sums, layer, comp))
                return nc.vector.scalar_tensor_tensor(mod[:, dst:dst + 8], mod[:, dst:dst + 8], 1.0, g, ALU.add, ALU.mult)

            def gate_rows(slot, banks, unit):
                dve.wait_ge(side_full[unit % SLOTS], 16 * (unit // SLOTS + 1))
                for c in range(2):
                    last = nc.vector.tensor_tensor(acc[:, slot, 512 * c:512 * c + 512], ps[banks[c]][:, :],
                                                   side[:, unit % SLOTS, 512 * c:512 * c + 512], ALU.add)
                last.then_inc(side_used, 1)

            dve.wait_ge(in_h, 16)
            scale("ev", h)
            split(T_EV)
            dve.wait_ge(vec_ps, 1)
            nc.vector.tensor_copy(vec[:, 0:N_ROWS], ps[4][:, 0:N_ROWS]).then_inc(vec_ready, 1)
            take("ev")
            nc.vector.memset(ev_cv[:, :, 0:2], 0.0)
            nc.vector.memset(ev_u[:, :, 0:16], 0.0).then_inc(EV["pin"], 1)
            split(T_EV + 1)
            split(T_EV + 2)
            split(T_EV + 3)
            dve.wait_ge(EV["pin"], 1)

            split(T_EV + 4)
            dve.wait_ge(EV["pool"], 2)
            split(T_EV + 5)
            chain(nc.vector.tensor_tensor(ev_s0[:, :, 1:272], ev_u[:, :, 1:272], ev_u[:, :, 0:271], ALU.add))
            chain(nc.vector.tensor_tensor(ev_s1[:, :, 3:272], ev_s0[:, 1:4, 3:272], ev_s0[:, 1:4, 1:270], ALU.add))
            chain(nc.vector.tensor_tensor(ev_s0[:, 2:4, 7:272], ev_s1[:, 1:3, 7:272], ev_s1[:, 1:3, 3:268], ALU.add))
            chain(nc.vector.tensor_tensor(ev_s1[:, 2, 15:272], ev_s0[:, 3, 15:272], ev_s0[:, 3, 7:264], ALU.add))
            sums = [ev_s0[:, 0, :], ev_s1[:, 0, :], ev_s0[:, 2, :], ev_s1[:, 2, :]]
            for g in range(4):
                nc.vector.tensor_tensor(ev_p[:, g, 0:16], sums[g][:, 16:32], pool_tab[:, g, :], ALU.mult)
                last = nc.vector.scalar_tensor_tensor(ev_p[:, g, 16:S], sums[g][:, 32:272], 1.0 / (2 << g),
                                                      ev_u[:, g, 32:272], ALU.mult, ALU.subtract)
            chain(last)
            nc.vector.tensor_tensor(ev_p[:, :, 0:16], ev_p[:, :, 0:16], ev_u[:, :, 16:32], ALU.subtract).then_inc(EV["pool_ready"], 1)
            for m in range(2):
                t = T_EV + 2 + 3 * m
                dve.wait_ge(EV["gate"], m + 1)
                dve.wait_ge(w_used, t + 2)
                nc.vector.tensor_tensor(ev_cv[:, :, 2:258], ps[(3 + 3 * m) % 4][:, :].rearrange("p (b t) -> p b t", b=2),
                                        ev_c, ALU.mult).then_inc(EV["prod"], 1)
                split(t + 4)
                dve.wait_ge(EV["tap2"], 2 * m + 2)
                for tap, done in ((1, EV["tap1"]), (0, EV["conv"])):
                    for b in range(2):
                        av = ev_a[:, b * S:b * S + S]
                        nc.vector.scalar_tensor_tensor(av, ev_cv[:, b, tap:tap + S], col("ev_conv_w", 4 * tap + 2 * m + b),
                                                       av, ALU.mult, ALU.add).then_inc(done, 1)
                    dve.wait_ge(done, 2 * m + 2)
                split(t + 5)
                if m == 0:
                    dve.wait_ge(EV["phi"], 1)
                    nc.vector.tensor_tensor(a_lo[:, 1024:2048], wk(1024, 1024), a_hi[:, 1024:2048].bitcast(F32), ALU.subtract)\
                        .then_inc(EV["pool_a"], 1)
                dve.wait_ge(w_used, t + 3)
                nc.vector.tensor_tensor(ev_y, ps[(4 + 3 * m) % 4][:, :], ev_a, ALU.mult).then_inc(EV["y"], 1)
                split(t + 6)
                dve.wait_ge(EV["yhi"], m + 1)
                c = slice(512 * m, 512 * m + 512)
                nc.vector.tensor_tensor(a_lo[:, c], ev_y, a_hi[:, c].bitcast(F32), ALU.subtract).then_inc(EV["a_ready"], 1)
            dve.wait_ge(EV["ybhi"], 1)
            nc.vector.tensor_tensor(a_lo[:, 1024:2048], wk(1024, 1024), a_hi[:, 1024:2048].bitcast(F32), ALU.subtract)\
                .then_inc(EV["a_ready"], 1)
            split(T_POOL + 4)
            dve.wait_ge(rows_ps, 1)
            nc.vector.tensor_copy(bias_rows, ps[2][0:8, 0:511]).then_inc(rows_sb, 1)
            for j in range(2):
                split(T_EVO + j + 4)
            residual("ffn0", T_FFN0 - 1)

            def gated(n, base):
                g = FFN[n]

                def step(j, par, units):
                    u = j * 4 + (base - 2) if j.c else Aff(base)
                    dve.wait_ge(g["a0"], val(j * 2 + 2))
                    for shift, done in ((1, g["tap"]), (2, g["conv"])):
                        for b in range(2):
                            av = f_a0[:, b, shift:S]
                            tap = 2 - shift
                            nc.vector.scalar_tensor_tensor(av, ps[0][:, b * S:b * S + S - shift],
                                                           vcol("ffn_conv_w", j * 2 + (n * 3 * FFB + tap * FFB + b)),
                                                           av, ALU.mult, ALU.add).then_inc(done, 1)
                        if shift == 1:
                            dve.wait_ge(done, val(j * 2 + 2))
                    split(u + 4)
                    dve.wait_ge(g["silu"], val(j + 1))
                    dve.wait_ge(w_used, val(u + 2))
                    nc.vector.tensor_tensor(f_p, ps[1][:, :], f_s, ALU.mult).then_inc(g["prod"], 1)
                    split(u + 5)
                    dve.wait_ge(g["ahi"], val(j + 1))
                    c = slice(par * 512, par * 512 + 512)
                    nc.vector.tensor_tensor(a_lo[:, c], f_p, a_hi[:, c].bitcast(F32), ALU.subtract).then_inc(g["a_ready"], 1)
                    if units:
                        kb = j - LOOP0
                        if n == 0:
                            ada(kb * 2 + U_FFN0, 0, kb, 2)
                            ada(kb * 2 + (U_FFN0 + 1), 1, kb, 3)
                        else:
                            for c in range(4):
                                ada(kb * 4 + (U_FFN1 + c), c, kb)
                    if j.c:
                        split(u + 6)
                        split(u + 7)

                for j in range(LOOP0):
                    step(Aff(j), j % 2, False)
                if n == 1:
                    scale("ctx", hs)
                dve.wait_ge(acc_zero, n + 1)
                dve.wait_ge(cs_ready, 1)
                with dve.Fori(0, TRIPS) as i:
                    for m in range(2):
                        step(Aff(LOOP0 + m, i, 2), m, True)
                for j in range(LOOP1, G_STEPS):
                    step(Aff(j), j % 2, False)
                if n == 1:
                    take("ctx")
                residual("od" if n == 0 else "final", base + 4 * G_STEPS - 1)
                if n == 1:
                    split(base + 4 * G_STEPS + 2)

            norm("ffn0", h, late=[T_FFN0 + 2, T_FFN0 + 3])
            gated(0, T_FFN0)

            def at_probs(i):
                dve.wait_ge(AT["exp"], 2 * i + 2)
                c = 34 + 4 * (i % 2)
                one_over = 40 + 2 * (i % 2)
                nc.vector.reciprocal(st[:, one_over:one_over + 2], st[:, c:c + 2]).then_inc(AT["rec"], 1)
                dve.wait_ge(AT["rec"], i + 1)
                for t, (c0, c1) in enumerate(SEG):
                    nc.vector.tensor_scalar(at_s[:, i % 2, c0:c1], at_s[:, i % 2, c0:c1],
                                            st[:, one_over + t:one_over + t + 1], None, ALU.mult)\
                        .then_inc(AT["p"], 1)

            def at_out(i):
                dve.wait_ge(AT["ohi"], i + 1)
                r = HD * (i % 2)
                nc.vector.tensor_tensor(a_lo3[r:r + HD, i // 2, :], ps[4 + i % 2][r:r + HD, 0:S],
                                        a_hi3[r:r + HD, i // 2, :].bitcast(F32), ALU.subtract).then_inc(AT["a_ready"], 1)

            def at_decay(i):
                dve.wait_ge(AT["neg"], 1)
                dve.wait_ge(rows_out, 16)
                for t in range(TT):
                    nc.vector.tensor_scalar(at_l[:, i % 2, t, :], ones, zf[:, 3, 8 * t + i:8 * t + i + 1], None, ALU.mult)\
                        .then_inc(AT["lbc"], 1)

            def at_scores(i):
                dve.wait_ge(AT["s_ps"], i + 1)
                s, bank = at_s[:, i % 2, :], ps[i % 2]
                if i < FOX:
                    if i == 0:
                        dve.wait_ge(AT["f"], 1)
                    f = [zf[:, 4, 8 * t + i:8 * t + i + 1] for t in range(TT)]
                    nc.vector.scalar_tensor_tensor(s[:, 0:P], bank[:, 0:P], f[0], causal, ALU.add, ALU.add).then_inc(AT["s_sb"], 1)
                    nc.vector.tensor_scalar(s[:, P:2 * P], bank[:, P:2 * P], f[1], None, ALU.add).then_inc(AT["s_sb"], 1)
                    nc.vector.scalar_tensor_tensor(s[:, 2 * P:3 * P], bank[:, 2 * P:3 * P], f[1], causal, ALU.add, ALU.add)\
                        .then_inc(AT["s_sb"], 1)
                    dve.wait_ge(AT["s_sb"], 3 * i + 3)
                else:
                    s = bank
                for t, (c0, c1) in enumerate(SEG):
                    c = 32 + 4 * (i % 2) + t
                    nc.vector.tensor_reduce(st[:, c:c + 1], s[:, c0:c1], AX.X, ALU.max, negate=True).then_inc(AT["max"], 1)

            norm("od", h, late=[T_QK + 2, T_QK + 3])
            dve.wait_ge(ada_ps, 1)
            g_mix = vec[:, ROW["norm_mix_g_2"]:ROW["norm_mix_g_2"] + 8]
            shift_cols(0, ps[4][:, 16:24], 0, 0)
            gain_cols(8, ps[4][:, 24:32], 0, 1, g_mix)
            shift_cols(16, ps[4][:, 0:8], 0, 0)
            gain_cols(24, ps[4][:, 8:16], 0, 1, g_mix).then_inc(mod_ready, 1)
            dve.wait_ge(in_small, 16 * 5)
            dve.wait_ge(AT["z_ps"], 1)
            for t in range(TT):
                nc.vector.tensor_tensor(zf[:, 0, 8 * t:8 * t + 8], ps[7][:, 8 * t:8 * t + 8], bf[:, :], ALU.add).then_inc(AT["z"], 1)
            dve.wait_ge(AT["z"], 2)
            chain(nc.vector.tensor_scalar(zf[:, 2, :], zf[:, 0, :], 0.0, None, ALU.min))
            nc.vector.scalar_tensor_tensor(zf[:, 1, :], zf[:, 2, :], 2.0, zf[:, 0, :], ALU.mult, ALU.subtract).then_inc(AT["nabs"], 1)
            split(T_QK + 4)
            dve.wait_ge(AT["ln"], 1)
            nc.vector.tensor_tensor(zf[:, 3, :], zf[:, 1, :], zf[:, 2, :], ALU.subtract).then_inc(AT["neg"], 1)
            for j in range(1, 4):
                split(T_QK + j + 4)
            dve.wait_ge(AT["f_ps"], 1)
            nc.vector.tensor_scalar(zf[:, 4, :], ps[6][:, 0:16], -1.0, None, ALU.mult).then_inc(AT["f"], 1)
            at_decay(0)
            at_decay(1)
            for j in range(4, 8):
                split(T_QK + j + 4)
            at_scores(0)
            at_scores(1)
            at_probs(0)
            for j in range(3):
                split(T_V + j + 4)
            dve.wait_ge(w_used, T_V + 4)
            for c in range(2):
                nc.vector.tensor_copy(at_v[:, 1, 512 * c:512 * c + 512], ps[6 + c][:, :]).then_inc(AT["v_sb"], 1)
            for i in range(HEADS):
                if i:
                    at_probs(i)
                if i == 0:
                    at_decay(2)
                if i and i + 1 < HEADS:
                    at_scores(i + 1)
                if i:
                    at_out(i - 1)
                if i + 3 < FOX:
                    at_decay(i + 3)
            at_out(HEADS - 1)
            split(T_V + 7)
            for j in range(2):
                split(T_ODO + j + 4)
            residual("ffn1", T_FFN1 - 1)

            norm("ffn1", h, late=[T_FFN1 + 2, T_FFN1 + 3])
            gated(1, T_FFN1)

            dve.wait_ge(side_full[U_BC1 % SLOTS], 16 * (U_BC1 // SLOTS + 1))
            for t in range(TT):
                dve.wait_ge(rstd_ready, 2 * RSTD["final"] + t + 1)
                final = nc.vector.scalar_tensor_tensor(h[:, t, :], h[:, t, :], rstd[:, 18 + t:19 + t],
                                                       side[:, U_BC1 % SLOTS, :], ALU.mult, ALU.mult)
                final.then_inc(h_ready, 1)

            dve.wait_ge(ada_ps, 2)
            g_ffn = vec[:, ROW["norm_ffn_g_2"]:ROW["norm_ffn_g_2"] + 8]
            shift_cols(32, ps[3][:, 0:8], 0, 3).then_inc(side_used, 1)
            gain_cols(40, ps[3][:, 8:16], 0, 4, g_ffn).then_inc(mod_ready, 1)
            norm("lat", h, late=[T_LA + 3])
            for j in range(4, 6):
                split(T_LA + j)
            dve.wait_ge(LA["krstd"], 1)
            for t in range(KT):
                nc.vector.tensor_scalar(kva[:, t, 0:KVL], kva[:, t, 0:KVL], rstd[:, 20 + t:21 + t], None, ALU.mult)\
                    .then_inc(LA["kscaled"], 1)
            dve.wait_ge(LA["qrstd"], 1)
            for t in range(TT):
                nc.vector.tensor_scalar(cq[:, t, :], cq[:, t, :], rstd[:, 24 + t:25 + t], None, ALU.mult).then_inc(LA["qscaled"], 1)
            def turn(x):
                v = [y.rearrange("p t (a s c) -> p t a s c", a=2, s=2) for y in (x, la_rot, sin)]
                for s in range(2):
                    last = nc.vector.tensor_tensor(v[1][:, :, :, s, :], v[0][:, :, :, 1 - s, :], v[2][:, :, :, s, :], ALU.mult)
                chain(last)
                chain(nc.vector.tensor_tensor(x, x, cos, ALU.mult))
                return nc.vector.tensor_tensor(x, x, la_rot, ALU.add)

            for n, (c, lf) in enumerate(((slice(0, 1024), lf_kv), (slice(1024, 1792), lf_q))):
                dve.wait_ge(LA["lxf"], 5 if n else 2)
                nc.vector.tensor_copy(xn_hi[:, c], lf).then_inc(LA["lhi"], 1)
                dve.wait_ge(LA["lhi"], n + 1)
                nc.vector.tensor_tensor(xn_lo[:, c], lf, xn_hi[:, c].bitcast(F32), ALU.subtract).then_inc(LA["l_ready"], 1)
            dve.wait_ge(LA["kv_sb"], 4)
            chain(nc.vector.tensor_tensor(la_kpe, kva[:, :, KVL:], pe_g[:, 1:2, :].to_broadcast([P, KT, ROPE]), ALU.mult))
            chain(turn(la_kpe[:, TT:KT, :]))
            split(T_LA + 6)
            split(T_LA + 7)
            dve.wait_ge(ada_ps, 3)
            gate_rows(0, (6, 7), U_BC1 + 1)
            gate_rows(4, (4, 5), U_BC1 + 2)

            def la_keys(i):
                dve.wait_ge(LA["a_rstd"], 2 * i + 2)
                dve.wait_ge(LA["values"], i + 1)
                for m in range(2):
                    kv2 = ps[m][:, :].rearrange("p (t d) -> p t d", t=2)
                    r = rstd[:, 28 + 2 * m:30 + 2 * m].unsqueeze(2).to_broadcast([P, 2, NOPE])
                    nc.vector.tensor_tensor(la_kn[:, 2 * m:2 * m + 2, 0:NOPE], kv2[:, :, 0:NOPE], r, ALU.mult)
                nc.vector.tensor_tensor(la_kn[:, :, NOPE:], la_kpe, rstd[:, 28:32].unsqueeze(2).to_broadcast([P, KT, ROPE]),
                                        ALU.mult).then_inc(LA["kn"], 1)

            def la_queries(i):
                dve.wait_ge(LA["a_rstd"], 2 * i + 1)
                for t in range(TT):
                    last = nc.vector.tensor_scalar(la_qn[:, t, :], ps[2][:, QKD * t:QKD * t + QKD], rstd[:, 32 + t:33 + t],
                                                   None, ALU.mult)
                chain(last)
                qpe = la_qn[:, :, NOPE:]
                chain(nc.vector.tensor_tensor(qpe, qpe, pe_g[:, 0:1, :].to_broadcast([P, TT, ROPE]), ALU.mult))
                turn(qpe).then_inc(LA["qpe"], 1)

            la_queries(0)
            la_keys(0)
            split(T_HEAD + 4)
            for i in range(MH + 1):
                if i:
                    dve.wait_ge(LA["t_ps"], i)
                    nc.vector.tensor_copy(la_pt[:, 512:1024], ps[7][:, :]).then_inc(LA["pt_d"], 1)
                    if i < MH:
                        split(T_HEAD + i + 4)
                    else:
                        split(T_WO + 4)
                        split(T_WO + 5)
                if i + 1 < MH:
                    la_queries(i + 1)
                    la_keys(i + 1)
                if i < MH:
                    dve.wait_ge(LA["s_ps"], i + 1)
                    for t in range(TT):
                        last = nc.vector.tensor_reduce(st[:, 80 + t:81 + t], ps[4 + t][:, :], AX.X, ALU.max, negate=True)
                    chain(last)
                    nc.vector.tensor_scalar(st[:, 82:84], st[:, 80:82], QKD ** -0.5, None, ALU.mult).then_inc(LA["max"], 1)
                if i:
                    dve.wait_ge(LA["ohi"], i)
                    nc.vector.tensor_tensor(a_lo3[:, i - 1, :], ps[6][:, 0:S], a_hi3[:, i - 1, :].bitcast(F32), ALU.subtract)\
                        .then_inc(LA["a_ready"], 1)
                if i < MH:
                    dve.wait_ge(LA["exp"], 2 * i + 2)
                    nc.vector.reciprocal(st[:, 86:88], st[:, 84:86]).then_inc(LA["rec"], 1)
                    dve.wait_ge(LA["rec"], i + 1)
                    for t in range(TT):
                        nc.vector.tensor_scalar(la_p[:, t, :], la_p[:, t, :], st[:, 86 + t:87 + t], None, ALU.mult)\
                            .then_inc(LA["p"], 1)
            residual("relu0", T_RELU0 - 1, acc[:, 0, :], bank0=0)

            def relu(n, base):
                g = RELU[n]

                def step(j, par, units):
                    f = j * 2 + (base - 1) if j.c else Aff(base)
                    dve.wait_ge(g["relu"], val(j + 1))
                    nc.vector.tensor_tensor(r_s[par], r_r, r_r, ALU.mult).then_inc(g["sq"], 1)
                    split(f + 4)
                    dve.wait_ge(g["ahi"], val(j + 1))
                    c = slice(par * 512, par * 512 + 512)
                    nc.vector.tensor_tensor(a_lo[:, c], r_s[par], a_hi[:, c].bitcast(F32), ALU.subtract).then_inc(g["a_ready"], 1)
                    if units:
                        kb = j - 2
                        for c in range(4):
                            ada(kb * 4 + (U_RELU0 + c), c, kb)
                    if j.c:
                        split(f + 5)

                for j in range(2):
                    step(Aff(j), j % 2, False)
                if n == 0:
                    dve.wait_ge(acc_zero, 3)
                else:
                    dve.wait_ge(ada_ps, 7)
                    gate_rows(1, (2, 3), U_BC3)
                with dve.Fori(0, 4) as i:
                    for m in range(2):
                        step(Aff(2 + m, i, 2), m, n == 0)
                with dve.Fori(0, 2) as i:
                    for m in range(2):
                        step(Aff(10 + m, i, 2), m, False)
                for j in range(14, R_STEPS):
                    step(Aff(j), j % 2, False)

            norm("relu0", h, late=[T_RELU0 + 2, T_RELU0 + 3])
            relu(0, T_RELU0)
            residual("gm", T_GMV - 1, acc[:, 4, :])
            dve.wait_ge(ada_ps, 4)
            g_mix1 = vec[:, ROW["norm_mix_g_2"] + 8:ROW["norm_mix_g_2"] + 16]
            g_ffn1 = vec[:, ROW["norm_ffn_g_2"] + 8:ROW["norm_ffn_g_2"] + 16]
            shift_cols(16, ps[3][:, 0:8], 1, 0)
            shift_cols(32, ps[3][:, 16:24], 1, 3)
            gain_cols(24, ps[3][:, 8:16], 1, 1, g_mix1).then_inc(mod_ready, 1)

            norm("gm", h, late=[T_GMV + 3])
            dve.wait_ge(ada_ps, 5)
            gate_rows(2, (4, 5), U_BC2)
            split(T_GMV + 4)
            split(T_GMV + 5)
            dve.wait_ge(GM["ws_ps"], 1)
            for c in range(2):
                nc.vector.tensor_copy(gm_wst[:, 512 * c:512 * c + 512], ps[2 + c][:, :]).then_inc(GM["ws"], 1)
            for j in range(2, 6):
                split(T_GMV + j + 4)
            dve.wait_ge(GM["v"], 8)
            chain(nc.vector.tensor_reduce(st[:, 56:58], st[:, 48:56].rearrange("p (t c) -> p t c", t=TT), AX.X, ALU.add))
            nc.vector.tensor_scalar(st[:, 58:60], st[:, 56:58], -1.0 / GMH, None, ALU.mult).then_inc(GM["mu"], 1)
            dve.wait_ge(GM["mu"], 1)
            dve.wait_ge(GM["sq"], 8)
            nc.vector.tensor_reduce(st[:, 60:62], st[:, 64:72].rearrange("p (t c) -> p t c", t=TT), AX.X, ALU.add)\
                .then_inc(GM["norm"], 1)
            dve.wait_ge(GM["rstd"], 1)

            def gm_norm(q):
                vv = [gm_v[:, t, 512 * q:512 * q + 512] for t in range(TT)]
                units = [U_BC2 + 1 + 2 * (q // 2) + m for m in range(2)]
                gain, shift = (side[:, u % SLOTS, 512 * (q % 2):512 * (q % 2) + 512] for u in units)
                for u in units:
                    dve.wait_ge(side_full[u % SLOTS], 16 * (u // SLOTS + 1))
                for t in range(TT):
                    last = nc.vector.scalar_tensor_tensor(vv[t], vv[t], st[:, 58 + t:59 + t], gain, ALU.add, ALU.mult)
                if q % 2:
                    last.then_inc(side_used, 1)
                    dve.wait_ge(side_used, units[0] + 1)
                else:
                    chain(last)
                for t in range(TT):
                    last = nc.vector.scalar_tensor_tensor(vv[t], vv[t], rstd[:, 36 + t:37 + t], shift, ALU.mult, ALU.add)
                if q % 2:
                    last.then_inc(side_used, 1)
                    dve.wait_ge(side_used, units[1] + 1)
                else:
                    chain(last)

            gm_norm(0)

            def gm_slice(j):
                return nc.vector.tensor_copy(gm_vs, gm_v[:, :, bass.ds(val(j * 256), 256)]).then_inc(GM["vs"], 1)

            def gm_step(j, par, blocks=(), more=True):
                f = j * 2 + (T_GM - 1) if j.c else Aff(T_GM)
                dve.wait_ge(GM["m_ps"], val(j + 1))
                nc.vector.tensor_tensor(gm_t[par].rearrange("p (b q) -> p b q", b=4), ps[2 + par][:, :].rearrange("p (b q) -> p b q", b=4),
                                        gm_bs[:, bass.ds(val(j * P), P)].unsqueeze(1).to_broadcast([P, 4, P]), ALU.add)\
                    .then_inc(GM["t"], 1)
                if more:
                    gm_slice(j + 1)
                if j.c == 0:
                    split(T_GMV + 10)
                else:
                    split(f + 4)
                dve.wait_ge(GM["t"], val(j + 1))
                dve.wait_ge(GM["u"], val(j + 1))
                nc.vector.tensor_tensor(gm_t[par], gm_t[par], gm_u, ALU.mult).then_inc(GM["prod"], 1)
                dve.wait_ge(GM["ahi"], val(j + 1))
                c = slice(par * 512, par * 512 + 512)
                nc.vector.tensor_tensor(a_lo[:, c], gm_t[par], a_hi[:, c].bitcast(F32), ALU.subtract).then_inc(GM["a_ready"], 1)
                for n, kb in enumerate(blocks):
                    if n:
                        dve.wait_ge(side_used, U_GM + 2 * kb.c)
                    for c in range(2):
                        ada(kb * 2 + (U_GM + c), c, kb)
                if j.c == 0:
                    split(T_GMV + 11)
                    split(f + 4)
                elif more:
                    split(f + 5)

            gm_slice(Aff(0))
            dve.wait_ge(GM["bs_in"], 16)
            gm_step(Aff(0), 0)
            gm_norm(1)
            gm_step(Aff(1), 1)
            gm_norm(2)
            gm_norm(3)
            dve.wait_ge(acc_zero, 4)
            with dve.Fori(0, 2) as i:
                for m in range(2):
                    gm_step(Aff(2 + m, i, 2), m, (Aff(m, i, 2),))
            for j in range(6, GM_STEPS):
                gm_step(Aff(j), j % 2, [Aff(2 * j - 8), Aff(2 * j - 7)], j + 1 < GM_STEPS)
            residual("relu1", T_RELU1 - 1, acc[:, 2, :])
            dve.wait_ge(ada_ps, 6)
            gain_cols(40, ps[3][:, 0:8], 1, 4, g_ffn1).then_inc(mod_ready, 1)
            norm("relu1", h, late=[T_RELU1 + 2, T_RELU1 + 3])
            relu(1, T_RELU1)
            residual("out", N_TILES - 1, acc[:, 1, :])

        @block.tensor
        def _(pe):
            def parts(s, c, n):
                return w_hi[s][:, c:c + n], w_lo[s][:, c:c + n]

            def f_tile(t, bank, fresh=None):
                t = t if isinstance(t, Aff) else Aff(t)
                pe.wait_ge(lo_done, val(t + 1))
                for b in range(2):
                    o = ps[bank][:, b * S:b * S + S]
                    for k in range(KB):
                        if fresh is not None and b == 0 and k % 2 == 0:
                            pe.wait_ge(xn_ready, 4 * NORM[fresh] + k // 2 + 1)
                        hi, lo = parts(t.c % SLOTS, k * 256 + b * P, P)
                        nc.tensor.matmul(o, hi, xn_hi3[:, k, :], start=k == 0, stop=False)
                        nc.tensor.matmul(o, hi, xn_lo3[:, k, :], start=False, stop=False)
                        last = nc.tensor.matmul(o, lo, xn_hi3[:, k, :], start=False, stop=k == KB - 1)
                last.then_inc(w_used, 1)

            def t_tile(t, blocks, first, last, x=(a_hi3, a_lo3), free=True, bank0=4, n=D, done=None, ends=False, fresh=None):
                t = t if isinstance(t, Aff) else Aff(t)
                pe.wait_ge(lo_done, val(t + 1))
                cuts = [(c, min(512, n - c)) for c in range(0, n, 512)]
                order = [(m, tt) for m in range(len(blocks)) for tt in range(TT)]
                if ends:
                    order.sort(key=lambda step: step[1])
                for at, (m, tt) in enumerate(order):
                    k = blocks[m]
                    if fresh is not None and tt == 0 and k % 2 == 0:
                        pe.wait_ge(xn_ready, 4 * NORM[fresh] + k // 2 + 1)
                    xh, xl = (y[:, k, tt * P:tt * P + P] for y in x)
                    begin, end = first and m == 0, last and m == len(blocks) - 1
                    for x_part, w_part in ((xh, 0), (xh, 1), (xl, 0)):
                        for c, (c0, cn) in enumerate(cuts):
                            w = parts(t.c % SLOTS, m * n + c0, cn)[w_part]
                            o = ps[bank0 + len(cuts) * tt + c][:, 0:cn]
                            ins = nc.tensor.matmul(o, x_part, w, start=begin and x_part is xh and w_part == 0,
                                                   stop=end and x_part is xl)
                    if ends and at == len(blocks) - 1:
                        ins.then_inc(tok0_done, 1)
                if free:
                    ins.then_inc(w_used, 1)
                elif done is not None:
                    ins.then_inc(done, 1)

            def norm(name):
                k = NORM[name]
                for t in range(TT):
                    pe.wait_ge(hs_ready, 2 * k + t + 1)
                    for b in range(KB):
                        c = (b % 2) * S + t * P
                        last = nc.tensor.transpose(ps[b // 2][:, c:c + P], hs[:, t, b * P:b * P + P], ident)
                        if t == TT - 1 and b % 2 == 1:
                            last.then_inc(xt_ps, 1)

            def columns(slot, bank, c0):
                for b in range(8):
                    last = nc.tensor.matmul(ps[bank][:, c0 + b:c0 + b + 1], acc[:, slot, b * P:b * P + P], ones[:, 0:1],
                                            start=True, stop=True)
                return last

            def rows(slot, banks):
                for c in range(2):
                    last = nc.tensor.matmul(ps[banks[c]][:, :], ones, acc[:, slot, 512 * c:512 * c + 512], start=True, stop=True)
                return last

            pe.wait_ge(in_cst, 16)
            norm("ev")
            pe.wait_ge(in_rows, 16 * N_ROW_DMAS)
            stage = wk(6144, ROW_TILES * P).rearrange("p (r c) -> p r c", r=ROW_TILES)
            for r in range(ROW_TILES):
                n = min(P, N_ROWS - r * P)
                last = nc.tensor.transpose(ps[4][:, r * P:r * P + n], stage[0:n, r, :], ident[0:n, 0:n])
            last.then_inc(vec_ps, 1)

            free = {4: (EV["pool"], 1), 5: (EV["pool"], 2), 6: (EV["gate"], 1), 7: (EV["prod"], 1)}
            for m in range(8):
                if m in free:
                    pe.wait_ge(*free[m])
                f_tile(T_EV + m, m % 4, fresh="ev" if m == 0 else None)
            pe.wait_ge(EV["pool_a"], 1)
            pe.wait_ge(EV["gate"], 2)
            pe.wait_ge(EV["y"], 1)
            pe.wait_ge(lo_done, T_POOL + 1)
            for g in range(4):
                o = ps[g // 2][:, (g % 2) * S:(g % 2) * S + S]
                hi, lo = parts(T_POOL % SLOTS, g * P, P)
                nc.tensor.matmul(o, hi, a_hi3[:, 4 + g, :], start=True, stop=False)
                nc.tensor.matmul(o, hi, a_lo3[:, 4 + g, :], start=False, stop=False)
                last = nc.tensor.matmul(o, lo, a_hi3[:, 4 + g, :], start=False, stop=True)
            last.then_inc(w_used, 1)
            for j in range(4):
                if j < 3:
                    pe.wait_ge(EV["a_ready"], j + 1)
                t_tile(T_EVO + j, (2 * j, 2 * j + 1), j == 0, j == 3, ends=j == 3)
                if j == 0:
                    pe.wait_ge(EV["prod"], 2)
                    pe.wait_ge(in_small, 16 * 5)
                    pe.wait_ge(rb_ready, 16)
                    nc.tensor.matmul(ps[2][0:8, 0:511], rel[:, :], onehot, start=True, stop=True).then_inc(rows_ps, 1)

            def gated(n, base):
                g = FFN[n]

                def f_step(j):
                    u = j * 4 + (base - 2) if j.c else Aff(base)
                    if j.c:
                        pe.wait_ge(g["conv"], val(j * 2))
                    f_tile(u, 0, fresh=f"ffn{n}" if j.c == 0 else None)
                    if j.c:
                        pe.wait_ge(g["prod"], val(j))
                    f_tile(u + 1, 1)

                def t_step(j, par, first=False, last=False):
                    pe.wait_ge(g["a_ready"], val(j + 1))
                    w = j * 4 + (base + 4) if j.c < G_STEPS - 1 else Aff(base + 4 * G_STEPS - 2)
                    t_tile(w, (2 * par,), first, False)
                    t_tile(w + 1, (2 * par + 1,), False, last, ends=last)

                f_step(Aff(0))
                f_step(Aff(1))
                t_step(Aff(0), 0, first=True)
                with pe.Fori(0, TRIPS) as i:
                    for m in range(2):
                        j = Aff(LOOP0 + m, i, 2)
                        f_step(j)
                        t_step(j - 1, 1 - m)
                for j in range(LOOP1, G_STEPS):
                    f_step(Aff(j))
                    t_step(Aff(j - 1), (j - 1) % 2)
                if n == 1:
                    pe.wait_ge(g["prod"], G_STEPS)
                    norm("ctx")
                t_step(Aff(G_STEPS - 1), (G_STEPS - 1) % 2, last=True)

            norm("ffn0")
            gated(0, T_FFN0)

            pe.wait_ge(side_used, U_FFN1)
            pe.wait_ge(h_ready, H_READY["od"] + 1)
            columns(0, 4, 0)
            columns(1, 4, 8)
            norm("od")
            columns(2, 4, 16)
            columns(3, 4, 24).then_inc(ada_ps, 1)
            for j in range(8):
                if j >= 4:
                    pe.wait_ge(AT["qk"], j - 3)
                f_tile(T_QK + j, j % 4, fresh="od" if j == 0 else None)
                if j == 0:
                    for t in range(TT):
                        for k in range(KB):
                            last = nc.tensor.matmul(ps[7][:, 8 * t:8 * t + 8], xf[:, k, t * P:t * P + P], wf[:, k, :],
                                                    start=k == 0, stop=k == KB - 1)
                    last.then_inc(AT["z_ps"], 1)
                if j == 3:
                    pe.wait_ge(AT["neg"], 1)
                    nc.tensor.matmul(ps[6][:, 0:8], tri_ones[:, 0:P], zf[:, 3, 0:8], start=True, stop=True)
                    nc.tensor.matmul(ps[6][:, 8:16], ones, zf[:, 3, 0:8], start=True, stop=False)
                    nc.tensor.matmul(ps[6][:, 8:16], tri_ones[:, 0:P], zf[:, 3, 8:16], start=False, stop=True)\
                        .then_inc(AT["f_ps"], 1)
            def at_scores(i):
                r, b, o = HD * (i % 2), i // 2, ps[i % 2]
                fox = i < FOX
                if 2 <= i < FOX + 2:
                    pe.wait_ge(AT["s_sb"], 3 * (i - 2) + 3)
                elif i >= 2:
                    pe.wait_ge(AT["exp"], 2 * (i - 2) + 2)
                if i == FOX:
                    pe.wait_ge(bias_in, 48)
                q, k = at_qk[r:r + HD, b, :], at_qk[r:r + HD, 8 + b, :]
                nc.tensor.matmul(o[:, 0:P], q[:, 0:P], k[:, 0:P], start=True, stop=False)
                if fox:
                    pe.wait_ge(AT["lbc"], 2 * i + 2)
                    nc.tensor.matmul(o[:, 0:P], at_l[:, i % 2, 0, :], tri_ones[:, 0:P], start=False, stop=True)
                else:
                    nc.tensor.matmul(o[:, 0:P], flip, t5_bias[:, i - FOX, 0:P], start=False, stop=True)
                nc.tensor.matmul(o[:, P:3 * P], q[:, P:S], k, start=True, stop=False)
                if fox:
                    nc.tensor.matmul(o[:, P:3 * P], at_l[:, i % 2, 0, :], tri_ones, start=False, stop=False)
                    last = nc.tensor.matmul(o[:, 2 * P:3 * P], at_l[:, i % 2, 1, :], tri_ones[:, 0:P], start=False, stop=True)
                else:
                    last = nc.tensor.matmul(o[:, P:3 * P], flip, t5_bias[:, i - FOX, P:3 * P], start=False, stop=True)
                last.then_inc(AT["s_ps"], 1)

            pe.wait_ge(AT["qk"], 8)
            at_scores(0)
            at_scores(1)
            pe.wait_ge(AT["f"], 1)
            pe.wait_ge(mod_ready, 1)
            for j in range(4):
                t_tile(T_V + j, (2 * j, 2 * j + 1), j == 0, j == 3, x=(xn_hi3, xn_lo3))

            pe.wait_ge(AT["v_sb"], 2)
            pe.wait_ge(AT["v_act"], 2)
            for i in range(HEADS):
                pe.wait_ge(AT["p"], 2 * i + 2)
                pv = at_s[:, i % 2, :]
                for b in range(3):
                    last = nc.tensor.transpose(ps[2 + i % 2][:, b * P:b * P + P], pv[:, b * P:b * P + P], ident)
                last.then_inc(AT["t_ps"], 1)
                if i + 2 < HEADS:
                    at_scores(i + 2)
                pe.wait_ge(AT["pt"], i + 1)
                if i >= 2:
                    pe.wait_ge(AT["a_ready"], i - 1)
                d = slice((i // 2) * P, (i // 2) * P + P)
                o = ps[4 + i % 2]
                nc.tensor.matmul(o[:, 0:S], at_v[:, 0, d], at_pt[:, 0:S], start=True, stop=False)
                nc.tensor.matmul(o[:, P:S], at_v[:, 1, d], at_pt[:, S:3 * P], start=False, stop=True).then_inc(AT["o_ps"], 1)
            pe.wait_ge(AT["a_ready"], HEADS)
            for j in range(4):
                t_tile(T_ODO + j, (2 * j, 2 * j + 1), j == 0, j == 3, ends=j == 3)

            norm("ffn1")
            gated(1, T_FFN1)

            xn = (xn_hi3, xn_lo3)
            kv_tile = dict(x=xn, n=KVL + ROPE)
            pe.wait_ge(xn_ready, 4 * NORM["ctx"] + 4)
            t_tile(T_LA, range(4), True, False, free=False, bank0=0, **kv_tile)
            t_tile(T_LA + 1, range(4, 8), False, True, free=False, bank0=0, done=LA["a_ps"], **kv_tile)
            pe.wait_ge(side_used, U_BC1)
            columns(1, 3, 0)
            columns(2, 3, 8).then_inc(ada_ps, 1)
            pe.wait_ge(LA["kv_sb"], 2)
            norm("lat")
            t_tile(T_LA, range(4), True, False, bank0=6, fresh="lat", **kv_tile)
            t_tile(T_LA + 1, range(4, 8), False, True, bank0=6, fresh="lat", **kv_tile)
            t_tile(T_LA + 2, range(4), True, False, x=xn, bank0=4, n=QL)
            t_tile(T_LA + 3, range(4, 8), False, True, x=xn, bank0=4, n=QL)
            pe.wait_ge(LA["kscaled"], KT)
            for b in range(2):
                for t in range(KT):
                    last = nc.tensor.transpose(ps[6 + b][:, t * P:t * P + P], kva[:, t, b * P:b * P + P], ident)
            last.then_inc(LA["lt_ps"], 1)
            pe.wait_ge(LA["qscaled"], TT)
            for b in range(3):
                for t in range(TT):
                    c = S * (b % 2) + t * P
                    last = nc.tensor.transpose(ps[5 - b // 2][:, c:c + P], cq[:, t, b * P:b * P + P], ident)
            last.then_inc(LA["lt_ps"], 1)
            pe.wait_ge(LA["lxf"], 2)
            rows(0, (6, 7))
            ckv = [y[:, 0:1024].rearrange("p (k t) -> p k t", k=2) for y in (xn_hi, xn_lo)]
            cqt = [y[:, 1024:1792].rearrange("p (k t) -> p k t", k=3) for y in (xn_hi, xn_lo)]

            def la_project(i, x, nk, tiles, base, n, where):
                for m in range(tiles):
                    for k in range(nk):
                        hi, lo = parts((T_HEAD + i) % SLOTS, base + k * n, n)
                        xh, xl = (y[:, k, m * P:m * P + P] for y in x)
                        nc.tensor.matmul(where(m), xh, hi, start=k == 0, stop=False)
                        nc.tensor.matmul(where(m), xh, lo, start=False, stop=False)
                        last = nc.tensor.matmul(where(m), xl, hi, start=False, stop=k == nk - 1)
                return last

            def la_project_q(i):
                if i:
                    pe.wait_ge(lo_done, T_HEAD + i + 1)
                la_project(i, cqt, 3, TT, 512, QKD, lambda m: ps[2][:, QKD * m:QKD * m + QKD]).then_inc(LA["head_q"], 1)

            def la_project_kv(i):
                if i:
                    pe.wait_ge(LA["kq"], i)
                else:
                    pe.wait_ge(lo_done, T_HEAD + 1)
                la_project(i, ckv, 2, KT, 0, 256, lambda m: ps[m // 2][:, 256 * (m % 2):256 * (m % 2) + 256])\
                    .then_inc(w_used, 1)

            def la_transpose(i):
                pe.wait_ge(LA["kn"], i + 1)
                for t in range(KT):
                    nc.tensor.transpose(ps[3][:, t * P:t * P + P], la_kn[:, t, 0:NOPE], ident)
                    nc.tensor.transpose(ps[0][0:ROPE, t * P:t * P + P], la_kn[:, t, NOPE:], ident)
                pe.wait_ge(LA["qpe"], i + 1)
                for t in range(TT):
                    nc.tensor.transpose(ps[1][:, t * P:t * P + P], la_qn[:, t, 0:NOPE], ident)
                    last = nc.tensor.transpose(ps[1][0:ROPE, S + t * P:S + t * P + P], la_qn[:, t, NOPE:], ident)
                last.then_inc(LA["kq_ps"], 1)

            def la_scores(i):
                q = la_qt[i % 2]
                pe.wait_ge(LA["kq"], i + 1)
                if i:
                    pe.wait_ge(LA["exp"], 2 * i)
                for t in range(TT):
                    nc.tensor.matmul(ps[4 + t][:, :], q[:, t * P:t * P + P], la_kta[i % 2], start=True, stop=False)
                    last = nc.tensor.matmul(ps[4 + t][:, :], q[0:ROPE, S + t * P:S + t * P + P], la_ktb[i % 2][0:ROPE, :],
                                            start=False, stop=True)
                last.then_inc(LA["s_ps"], 1)

            def la_weights(i):
                pe.wait_ge(LA["p"], 2 * i + 2)
                if i:
                    pe.wait_ge(LA["a_ready"], i)
                for k in range(KT):
                    for t in range(TT):
                        c = (k % 2) * S + t * P
                        last = nc.tensor.transpose(ps[6 + k // 2][:, c:c + P], la_p[:, t, k * P:k * P + P], ident)
                last.then_inc(LA["t_ps"], 1)

            def la_sums(i):
                pe.wait_ge(LA["pt_a"], i + 1)
                pe.wait_ge(LA["pt_d"], i + 1)
                for k in range(KT):
                    last = nc.tensor.matmul(ps[6][:, 0:S], la_v[i % 3][:, k, :], la_pt[:, k * S:k * S + S],
                                            start=k == 0, stop=k == KT - 1)
                last.then_inc(LA["o_ps"], 1)

            def la_output(j):
                pe.wait_ge(LA["a_ready"], 2 * j + 2)
                t_tile(T_WO + j, (2 * j, 2 * j + 1), j == 0, j == 3, bank0=0, ends=j == 3)

            pe.wait_ge(LA["l_ready"], 1)
            la_project_kv(0)
            pe.wait_ge(LA["lxf"], 5)
            rows(3, (4, 5)).then_inc(ada_ps, 1)
            pe.wait_ge(LA["l_ready"], 2)
            la_project_q(0)
            pe.wait_ge(side_used, U_BC1 + 3)
            la_transpose(0)
            for i in range(MH - 1):
                la_project_q(i + 1)
                if i:
                    la_weights(i - 1)
                la_project_kv(i + 1)
                la_scores(i)
                if i:
                    la_sums(i - 1)
                la_transpose(i + 1)
            la_scores(MH - 1)
            la_weights(MH - 2)
            la_output(0)
            la_sums(MH - 2)
            la_output(1)
            la_weights(MH - 1)
            la_output(2)
            la_sums(MH - 1)
            la_output(3)

            def relu(n, base):
                g = RELU[n]

                def f_step(j, par):
                    if j.c >= 2:
                        pe.wait_ge(g["relu"], val(j - 1))
                    f_tile(j * 2 + (base - 1) if j.c else Aff(base), par, fresh=f"relu{n}" if j.c == 0 else None)

                def t_step(j, par, first=False, last=False):
                    pe.wait_ge(g["a_ready"], val(j + 1))
                    w = j * 2 + (base + 2) if j.c < R_STEPS - 1 else Aff(base + 2 * R_STEPS - 1)
                    t_tile(w, (2 * par, 2 * par + 1), first, last, ends=last)

                f_step(Aff(0), 0)
                f_step(Aff(1), 1)
                if n == 1:
                    rows(1, (2, 3)).then_inc(ada_ps, 1)
                t_step(Aff(0), 0, first=True)
                with pe.Fori(0, 6) as i:
                    for m in range(2):
                        j = Aff(2 + m, i, 2)
                        f_step(j, m)
                        t_step(j - 1, 1 - m)
                for j in range(14, R_STEPS):
                    f_step(Aff(j), j % 2)
                    t_step(Aff(j - 1), (j - 1) % 2)
                t_step(Aff(R_STEPS - 1), 1, last=True)

            norm("relu0")
            relu(0, T_RELU0)
            pe.wait_ge(side_used, U_BC2)
            columns(0, 3, 0)
            columns(1, 3, 8)
            columns(3, 3, 16).then_inc(ada_ps, 1)

            norm("gm")
            rows(2, (4, 5)).then_inc(ada_ps, 1)
            for c in range(4):
                if c == 3:
                    pe.wait_ge(side_used, U_BC2 + 1)
                if c == 2:
                    pe.wait_ge(GM["ws"], 2)
                for m in range(2):
                    t_tile(T_GMV + 2 * c + m, range(4 * m, 4 * m + 4), m == 0, m == 1, x=xn, bank0=GM_BANK[c], n=512,
                           fresh="gm" if c == 0 else None)
                if c == 0:
                    pe.wait_ge(GM["ws_in"], 16)
                    for g in range(8):
                        last = nc.tensor.transpose(ps[2 + g // 4][:, (g % 4) * P:(g % 4) * P + P], gm_ws[:, g * P:g * P + P], ident)
                    last.then_inc(GM["ws_ps"], 1)

            def gm_u(j, par):
                if j.c >= 2:
                    pe.wait_ge(GM["u"], val(j - 1))
                f_tile(j * 2 + (T_GM - 1) if j.c else Aff(T_GM), par)

            def gm_mix(j, par):
                pe.wait_ge(GM["vs"], val(j + 1))
                if j.c >= 2:
                    pe.wait_ge(GM["t"], val(j - 1))
                for b in range(2):
                    for t in range(TT):
                        c = (2 * b + t) * P
                        last = nc.tensor.matmul(ps[2 + par][:, c:c + P], gm_vs[:, t, b * P:b * P + P],
                                                gm_wst[:, bass.ds(val(j * P), P)], start=True, stop=True)
                last.then_inc(GM["m_ps"], 1)

            def gm_t_step(j, par, first=False, last=False):
                pe.wait_ge(GM["a_ready"], val(j + 1))
                w = j * 2 + (T_GM + 2) if j.c < GM_STEPS - 1 else Aff(T_GM + 2 * GM_STEPS - 1)
                t_tile(w, (2 * par, 2 * par + 1), first, last, ends=last)

            pe.wait_ge(GM["v"], 4)
            gm_u(Aff(0), 0)
            gm_u(Aff(1), 1)
            gm_mix(Aff(0), 0)
            gm_mix(Aff(1), 1)
            gm_t_step(Aff(0), 0, first=True)
            with pe.Fori(0, 2) as i:
                for m in range(2):
                    j = Aff(2 + m, i, 2)
                    gm_u(j, m)
                    gm_mix(j, m)
                    gm_t_step(j - 1, 1 - m)
            for j in range(6, GM_STEPS):
                gm_u(Aff(j), j % 2)
                gm_mix(Aff(j), j % 2)
                gm_t_step(Aff(j - 1), (j - 1) % 2)
            gm_t_step(Aff(GM_STEPS - 1), 1, last=True)
            pe.wait_ge(side_used, U_BC3)
            columns(0, 3, 0).then_inc(ada_ps, 1)

            norm("relu1")
            relu(1, T_RELU1)

        @block.gpsimd
        def _(pool):
            done = [0]

            def chain(ins):
                done[0] += 1
                ins.then_inc(pool_step, 1)
                pool.wait_ge(pool_step, done[0])

            def root(c0, n, parts):
                at = c0
                for c, m, count in parts:
                    chain(nc.gpsimd.tensor_scalar(rs[:, at:at + m], st[:, c:c + m], 1.0 / count, EPS, ALU.mult, ALU.add))
                    at += m
                return nc.gpsimd.tensor_tensor(rstd[:, c0:c0 + n], rs[:, c0:c0 + n], half[:, 0:n], ALU.pow)

            def row_rstd(name):
                for t in range(TT):
                    pool.wait_ge(sq_done, 2 * RSTD[name] + t + 1)
                    c = RCOL[name] + t
                    root(c, 1, [(c, 1, D)]).then_inc(rstd_ready, 1)

            def side_load(s, src, free=None):
                s = s if isinstance(s, Aff) else Aff(s)
                if s.c >= SLOTS:
                    pool.wait_ge(side_used, val(s - (SLOTS - 1)) if free is None else free)
                pool.dma_start(side[:, s.c % SLOTS, :], src).then_inc(side_full[s.c % SLOTS], 16)

            def ada_view(layer, comp, kb):
                v = I["ada_w_2"][layer].rearrange("(k p) (c n) -> p k c n", p=P, c=6)
                return v[:, bass.ds(val(kb), 1), comp, :].rearrange("p k n -> p (k n)")

            def side_loop(u0, layer, comp0, n_comp, trips):
                per = SLOTS // n_comp
                with pool.Fori(0, trips) as i:
                    for m in range(SLOTS):
                        s = Aff(u0 + SLOTS + m, i, SLOTS)
                        pool.wait_ge(side_used, val(s - (SLOTS - 1)))
                        kb = pool.snap(val(Aff(per + m // n_comp, i, per)))
                        pool.dma_start(side[:, s.c % SLOTS, :], ada_view(layer, comp0 + m % n_comp, kb))\
                            .then_inc(side_full[s.c % SLOTS], 16)

            def bias_row(layer, comp):
                return I["ada_b_2"][layer, comp * D:comp * D + D].partition_broadcast(P)

            nc.gpsimd.memset(half[:, :], -0.5).then_inc(half_ready, 1)
            chain(nc.gpsimd.memset(rel[:, :], 1.0))
            pool.dma_start(rel[0:32, :], I["rel_bias"]).then_inc(rb_ready, 16)
            pool.wait_ge(half_ready, 1)
            row_rstd("ev")
            pool.dma_start(onehot, I["onehot"]).then_inc(in_small, 16)
            pool.dma_start(bf[:, :], I["od_b_f"][0].partition_broadcast(P)).then_inc(in_small, 16)
            pool.dma_start(wf[:, :, :], I["od_w_in"][0].rearrange("(k p) n -> p k n", p=P)[:, :, 3 * D:3 * D + 8])\
                .then_inc(in_small, 16)
            pool.dma_start(pe_g[:, 0, :], I["mla_q_norm_2"][0, NOPE:QKD].partition_broadcast(P)).then_inc(in_small, 16)
            pool.dma_start(pe_g[:, 1, :], I["mla_k_norm_2"][0, NOPE:QKD].partition_broadcast(P)).then_inc(in_small, 16)
            nc.gpsimd.memset(acc[:, 0:4, :], 0.0).then_inc(acc_zero, 1)
            for s in range(SLOTS):
                side_load(U_FFN0 + s, ada_view(0, s % 2, s // 2))
            pool.wait_ge(rows_sb, 1)
            pool.dma_start(scratch[:, 0:511], bias_rows).then_inc(rows_out, 16)
            row_rstd("ffn0")
            side_loop(U_FFN0, 0, 0, 2, 3)
            row_rstd("od")
            pool.wait_ge(rows_out, 16)
            pool.wait_ge(mod_ready, 1)
            pool.dma_start(flip, I["consts"][:, C_ALL:]).then_inc(bias_in, 16)
            for t, (c0, c1) in enumerate(SEG):
                src = bass.AP(scratch.tensor, P - P * t, [[1, P], [512, 8], [1, c1 - c0]])
                pool.dma_start(t5_bias[:, :, c0:c1], src).then_inc(bias_in, 16)
            for c in range(SLOTS):
                side_load(U_FFN1 + c, ada_view(0, 2 + c, 0))
            pool.wait_ge(AT["a_ready"], HEADS)
            nc.gpsimd.memset(acc[:, 0:4, :], 0.0).then_inc(acc_zero, 1)
            row_rstd("ffn1")
            pool.wait_ge(xt_ps, 4 * NORM["ffn1"] + 4)
            pool.dma_start(hs, I["ctx_2"][0].rearrange("(t p) d -> p t d", p=P)).then_inc(ctx_in, 16)
            row_rstd("ctx")
            side_loop(U_FFN1, 0, 2, 4, 7)
            side_load(U_BC1, I["final_norm_g"].partition_broadcast(P))
            side_load(U_BC1 + 1, bias_row(0, 2))
            side_load(U_BC1 + 2, bias_row(0, 5))
            row_rstd("final")
            row_rstd("lat")
            pool.wait_ge(LA["ksq"], KT)
            root(20, KT, [(48, KT, KVL)]).then_inc(LA["krstd"], 1)
            pool.wait_ge(LA["qsq"], TT)
            root(24, TT, [(52, TT, QL)]).then_inc(LA["qrstd"], 1)
            pool.wait_ge(LA["psq"], KT)
            for i in range(MH):
                pool.wait_ge(LA["a_sq"], 6 * i + 2)
                chain(nc.gpsimd.tensor_scalar(rs[:, 32:34], st[:, 76:78], 1.0 / QKD, EPS, ALU.mult, ALU.add))
                nc.gpsimd.tensor_tensor(rstd[:, 32:34], rs[:, 32:34], half[:, 0:2], ALU.pow).then_inc(LA["a_rstd"], 1)
                pool.wait_ge(LA["a_sq"], 6 * i + 6)
                chain(nc.gpsimd.tensor_tensor(rs[:, 28:32], st[:, 72:76], st[:, 64:68], ALU.add))
                chain(nc.gpsimd.tensor_scalar(rs[:, 28:32], rs[:, 28:32], 1.0 / QKD, EPS, ALU.mult, ALU.add))
                nc.gpsimd.tensor_tensor(rstd[:, 28:32], rs[:, 28:32], half[:, 0:4], ALU.pow).then_inc(LA["a_rstd"], 1)
            for c in range(SLOTS):
                side_load(U_RELU0 + c, ada_view(1, c, 0))
            row_rstd("relu0")
            pool.wait_ge(h_ready, H_READY["relu0"] + 2)
            nc.gpsimd.memset(acc[:, 0:4, :], 0.0).then_inc(acc_zero, 1)
            side_loop(U_RELU0, 1, 0, 4, 7)
            side_load(U_BC2, bias_row(1, 2))
            for c, name in enumerate(("gm_ln_g_2", "gm_ln_b_2")):
                side_load(U_BC2 + 1 + c, I[name][0, 0:1024].partition_broadcast(P))
            pool.wait_ge(h_ready, H_READY["gm"] + 2)
            pool.dma_start(gm_ws.rearrange("p (g q) -> p g q", g=8), I["gm_ws_2"][0].rearrange("g p q -> p g q")).then_inc(GM["ws_in"], 16)
            row_rstd("gm")
            for c, name in enumerate(("gm_ln_g_2", "gm_ln_b_2")):
                side_load(U_BC2 + 3 + c, I[name][0, 1024:2048].partition_broadcast(P))
            pool.wait_ge(mod_ready, 3)
            nc.gpsimd.memset(acc[:, 0:2, :], 0.0).then_inc(acc_zero, 1)
            pool.wait_ge(xn_ready, 4 * NORM["gm"] + 4)
            pool.dma_start(gm_bs, I["gm_bs_2"][0].rearrange("g p -> (g p)").partition_broadcast(P)).then_inc(GM["bs_in"], 16)
            pool.wait_ge(GM["norm"], 1)
            root(36, 2, [(60, 2, GMH)]).then_inc(GM["rstd"], 1)
            for c in range(SLOTS):
                side_load(U_GM + c, ada_view(1, 4 + c % 2, c // 2))
            side_loop(U_GM, 1, 4, 2, 3)
            side_load(U_BC3, bias_row(1, 5))
            row_rstd("relu1")


_INS = ["x", "mix_norm_g", "ffn_norm_g", "final_norm_g", "ev_w_in", "ev_conv_w", "ev_pool_w", "ev_pool_scale", "ev_w_out",
        "od_w_in", "od_b_f", "od_w_out", "rel_bias", "ffn_w_in", "ffn_conv_w", "ffn_conv_b", "ffn_w_out", "c_2", "ctx_2",
        "c_ctx_2", "ada_w_2", "ada_b_2", "norm_mix_g_2", "norm_ffn_g_2", "mla_wq_a_2", "mla_q_a_norm_2", "mla_wq_b_2",
        "mla_wkv_a_2", "mla_kv_a_norm_2", "mla_wkv_b_2", "mla_q_norm_2", "mla_k_norm_2", "mla_wo_2", "gm_w_in_2",
        "gm_ln_g_2", "gm_ln_b_2", "gm_ws_2", "gm_bs_2", "gm_w_out_2", "ffn_w1_2", "ffn_w2_2"]


def constants():
    import math

    import numpy as np

    c = np.zeros((P, C_ALL + P), np.float32)
    i = np.arange(P)
    c[:, C_ID:C_ID + P] = np.eye(P)
    c[:, C_ALL:] = np.eye(P)[::-1]
    c[:, C_U:C_U + P] = i[:, None] <= i[None, :]
    c[:, C_U + P:C_U + 2 * P] = 1.0
    c[:, C_MASK:C_MASK + P] = np.where(i[None, :] <= i[:, None], 0.0, NEG)
    for g in range(4):
        c[:, C_TAB + 16 * g:C_TAB + 16 * g + 16] = 1.0 / np.minimum(np.arange(16) + 1, 2 << g)
    half = ROPE // 2
    grid_w, theta = 64, 10000.0
    pos = np.arange(S)
    inv = (np.float32(theta) ** (-np.arange(0, half, 2, dtype=np.float32) / np.float32(half))).astype(np.float32)
    ang_r = (pos // grid_w).astype(np.float32)[:, None] * inv[None, :]
    ang_c = (pos % grid_w).astype(np.float32)[:, None] * inv[None, :]
    ang = np.concatenate([ang_r, ang_r, ang_c, ang_c], axis=-1).astype(np.float32)
    sign = np.tile(np.repeat([-1.0, 1.0], half // 2), 2)
    c[:, C_COS:C_COS + P] = np.cos(ang).reshape(TT, P, ROPE).transpose(1, 0, 2).reshape(P, P)
    c[:, C_SIN:C_SIN + P] = (np.sin(ang) * sign).reshape(TT, P, ROPE).transpose(1, 0, 2).reshape(P, P)

    buckets, far, exact = 32, 128, 16
    hot = np.zeros((33, 511), np.float32)
    for m in range(511):
        d = 255 - m
        if d < 0:
            hot[32, m] = NEG
        elif d < exact:
            hot[d, m] = 1.0
        else:
            b = exact + int(np.float32(np.log(np.float32(d) / np.float32(exact))) / np.float32(math.log(far / exact))
                            * np.float32(buckets - exact))
            hot[min(b, buckets - 1), m] = 1.0
    return c, hot


def kernel(**inputs):
    import numpy as _np
    import concourse.bacc as _bacc
    from concourse.bass_utils import run_bass_kernel_spmd as _run

    nc = _bacc.Bacc("TRN2", target_bir_lowering=False, num_devices=1)
    arrays, views = {}, {}

    def give(name, a):
        arrays[f"in_{name}"] = a
        views[name] = nc.dram_tensor(f"in_{name}", a.shape, mybir.dt.from_np(a.dtype), kind="ExternalInput").ap()

    for name in _INS:
        give(name, _np.ascontiguousarray(inputs[name]))
    consts, onehot = constants()
    give("consts", consts)
    give("onehot", onehot)
    out = nc.dram_tensor("out_0", (1, S, D), mybir.dt.from_np(_np.dtype("float32")), kind="ExternalOutput").ap()
    build(nc, views, out)
    r = _run(nc, [arrays], core_ids=[0])
    return r.results[0]["out_0"]
```
